# Optimizing a Trainium2 kernel written in Bass

```python
import math
import jax, jax.numpy as jnp
from jax import lax
import numpy as np

D_MODEL = 1024
BATCH = 1
SEQ = 512
DEPTH = 1

D_A = 512
HEAD_DIM_A = 128
N_HEADS_A = D_A // HEAD_DIM_A
CHUNK_A = 64
N_HEADS_B = 8
HEAD_DIM_B = 64
D_B = N_HEADS_B * HEAD_DIM_B
IDX_HEADS = 8
IDX_DIM = 64
TOPK_MAX = 256
Q_BLOCK = 128
N_BUCKETS = 32
MAX_DISTANCE = 128
ALPHA = (2 * DEPTH) ** 0.25
BETA = (8 * DEPTH) ** -0.25
LN_EPS = 1e-5
RMS_EPS = 1e-6

SPLITS = [D_A, D_A, D_A, D_A, D_B, D_B, D_B, D_B, IDX_HEADS * IDX_DIM, IDX_DIM, IDX_HEADS, D_MODEL, D_MODEL]
N_IN = sum(SPLITS)

kernel_name = "hgrn2_dsa_gated_hybrid_deepnorm"

def layer_norm(x, g, b):
    xf = x.astype(jnp.float32)
    mu = jnp.mean(xf, axis=-1, keepdims=True)
    var = jnp.mean(jnp.square(xf - mu), axis=-1, keepdims=True)
    return ((xf - mu) * lax.rsqrt(var + LN_EPS) * g.astype(jnp.float32) + b.astype(jnp.float32)).astype(x.dtype)

def t5_bucket(dist):
    max_exact = N_BUCKETS // 2
    d = jnp.maximum(dist, 0)
    df = jnp.maximum(d, 1).astype(jnp.float32)
    large = max_exact + (jnp.log(df / max_exact) / math.log(MAX_DISTANCE / max_exact)
                         * (N_BUCKETS - max_exact)).astype(jnp.int32)
    large = jnp.minimum(large, N_BUCKETS - 1)
    return jnp.where(d < max_exact, d, large)

def hgrn2_mix(q, f_logit, i, lb):
    B, L, _ = q.shape
    nc = L // CHUNK_A
    f32 = jnp.float32
    fl = f_logit.astype(f32)
    lbf = lb.astype(f32)
    log_f = jnp.logaddexp(jnp.log(lbf), jnp.log1p(-lbf) + jax.nn.log_sigmoid(fl))
    k = (1.0 - lbf) * jax.nn.sigmoid(-fl)

    def heads(t):
        return t.astype(f32).reshape(B, nc, CHUNK_A, N_HEADS_A, HEAD_DIM_A).transpose(1, 0, 3, 2, 4)

    qh, kh, vh, gh = heads(q), heads(k), heads(i), heads(log_f)
    bcum = jnp.cumsum(gh, axis=-2)
    causal = jnp.tril(jnp.ones((CHUNK_A, CHUNK_A), dtype=bool))[:, :, None]

    def step(S, inp):
        qc, kc, vc, bc = inp
        o_inter = jnp.einsum('bhtk,bhkv->bhtv', qc * jnp.exp(bc), S)
        diff = bc[:, :, :, None, :] - bc[:, :, None, :, :]
        decay = jnp.where(causal, jnp.exp(jnp.where(causal, diff, 0.0)), 0.0)
        scores = jnp.einsum('bhtk,bhtsk,bhsk->bhts', qc, decay, kc)
        o = o_inter + jnp.einsum('bhts,bhsv->bhtv', scores, vc)
        b_last = bc[:, :, -1:, :]
        S = jnp.exp(b_last[:, :, 0, :, None]) * S + jnp.einsum('bhsk,bhsv->bhkv', kc * jnp.exp(b_last - bc), vc)
        return S, o

    S0 = jnp.zeros((B, N_HEADS_A, HEAD_DIM_A, HEAD_DIM_A), f32)
    _, o = lax.scan(step, S0, (qh, kh, vh, bcum))
    return o.transpose(1, 0, 3, 2, 4).reshape(B, L, N_HEADS_A, HEAD_DIM_A)

def dsa_mix(q, k, v, q_idx, k_idx, w_idx, rel_bias):
    B, L, _ = q.shape
    f32 = jnp.float32
    topk = min(TOPK_MAX, L // 4)
    nb = L // Q_BLOCK
    kh = k.reshape(B, L, N_HEADS_B, HEAD_DIM_B)
    vh = v.reshape(B, L, N_HEADS_B, HEAD_DIM_B)
    kif = k_idx.astype(f32)
    key_pos = jnp.arange(L, dtype=jnp.int32)
    bidx = jnp.arange(B)[:, None, None]

    def to_blocks(t):
        return t.reshape(B, nb, Q_BLOCK, t.shape[-1]).transpose(1, 0, 2, 3)

    def block(args):
        qb, qib, wb, start = args
        qpos = start + jnp.arange(Q_BLOCK, dtype=jnp.int32)
        causal = key_pos[None, :] <= qpos[:, None]
        qi = qib.astype(f32).reshape(B, Q_BLOCK, IDX_HEADS, IDX_DIM)
        dots = jnp.einsum('bthd,bsd->bths', qi, kif) * (IDX_DIM ** -0.5)
        score = jnp.einsum('bth,bths->bts', wb.astype(f32) * (IDX_HEADS ** -0.5), jax.nn.relu(dots))
        score = jnp.where(causal[None], score, -jnp.inf)
        _, idx = lax.top_k(score, topk)
        valid = idx <= qpos[None, :, None]
        ks = kh[bidx, idx]
        vs = vh[bidx, idx]
        qh = qb.reshape(B, Q_BLOCK, N_HEADS_B, HEAD_DIM_B)
        logits = jnp.einsum('bthd,btkhd->bhtk', qh, ks).astype(f32) * (HEAD_DIM_B ** -0.5)
        bias = rel_bias[t5_bucket(qpos[None, :, None] - idx)].astype(f32)
        logits = logits + bias.transpose(0, 3, 1, 2)
        logits = jnp.where(valid[:, None], logits, -jnp.inf)
        p = jax.nn.softmax(logits, axis=-1)
        o = jnp.einsum('bhtk,btkhd->bthd', p.astype(vs.dtype), vs)
        return o.reshape(B, Q_BLOCK, D_B)

    starts = jnp.arange(nb, dtype=jnp.int32) * Q_BLOCK
    o = lax.map(block, (to_blocks(q), to_blocks(q_idx), to_blocks(w_idx), starts))
    return o.transpose(1, 0, 2, 3).reshape(B, L, D_B)

def hybrid_layer(x, w_in, b_in, w_up_a, w_up_b, w_out, lb, norm_a_g, rel_bias, ln_g, ln_b):
    B, L, _ = x.shape
    proj = jnp.einsum('bld,dn->bln', x, w_in) + b_in
    cuts = [int(c) for c in np.cumsum(SPLITS)[:-1]]
    qa, fa, ia, za, qb, kb, vb, zb, qi, ki, wi, ga, gb = jnp.split(proj, cuts, axis=-1)
    oa = hgrn2_mix(qa, fa, ia, lb)
    oa = oa * lax.rsqrt(jnp.mean(jnp.square(oa), axis=-1, keepdims=True) + RMS_EPS)
    oa = oa.reshape(B, L, D_A) * norm_a_g.astype(jnp.float32)
    ua = jnp.einsum('blc,cd->bld', (oa.astype(x.dtype) * jax.nn.silu(za)), w_up_a)
    ob = dsa_mix(qb, kb, vb, qi, ki, wi, rel_bias)
    ub = jnp.einsum('blc,cd->bld', ob * jax.nn.silu(zb), w_up_b)
    merged = jax.nn.sigmoid(ga) * ua + jax.nn.sigmoid(gb) * ub
    y = jnp.einsum('bld,de->ble', merged, w_out)
    return layer_norm(ALPHA * x + y, ln_g, ln_b)

def setup_inputs(seed: int = 0) -> dict:
    key = jax.random.key(seed)
    ks = jax.random.split(key, 12)
    f32 = jnp.float32
    x = jax.random.normal(ks[0], (BATCH, SEQ, D_MODEL), f32)
    w_in = jax.random.normal(ks[1], (DEPTH, D_MODEL, N_IN), f32) * D_MODEL ** -0.5
    b_in = jax.random.normal(ks[2], (DEPTH, N_IN), f32) * 0.02
    w_up_a = jax.random.normal(ks[3], (DEPTH, D_A, D_MODEL), f32) * (D_A ** -0.5) * BETA
    w_up_b = jax.random.normal(ks[4], (DEPTH, D_B, D_MODEL), f32) * (D_B ** -0.5) * BETA
    w_out = jax.random.normal(ks[5], (DEPTH, D_MODEL, D_MODEL), f32) * (D_MODEL ** -0.5) * BETA
    lb_logits = jax.random.normal(ks[6], (DEPTH, D_A), f32) * 0.5
    norm_a_g = 1.0 + 0.02 * jax.random.normal(ks[7], (DEPTH, D_A), f32)
    rel_bias = jax.random.normal(ks[8], (N_BUCKETS, N_HEADS_B), f32) * 0.5
    ln_g = 1.0 + 0.02 * jax.random.normal(ks[9], (DEPTH, D_MODEL), f32)
    ln_b = 0.02 * jax.random.normal(ks[10], (DEPTH, D_MODEL), f32)
    return {"x": x, "w_in": w_in, "b_in": b_in, "w_up_a": w_up_a, "w_up_b": w_up_b, "w_out": w_out,
            "lb_logits": lb_logits, "norm_a_g": norm_a_g, "rel_bias": rel_bias, "ln_g": ln_g, "ln_b": ln_b}

def reference(x, w_in, b_in, w_up_a, w_up_b, w_out, lb_logits, norm_a_g, rel_bias, ln_g, ln_b):
    lbs = jnp.cumsum(jax.nn.softmax(lb_logits.astype(jnp.float32), axis=0), axis=0)
    lbs = lbs - lbs[0:1]
    h = x
    for layer in range(DEPTH):
        h = hybrid_layer(h, w_in[layer], b_in[layer], w_up_a[layer], w_up_b[layer], w_out[layer],
                         lbs[layer], norm_a_g[layer], rel_bias, ln_g[layer], ln_b[layer])
    return h


_drawn_inputs = setup_inputs


def setup_inputs(seed=0):
    import zlib

    import numpy as np

    out = dict(_drawn_inputs(seed))
    spreads = {}
    factors = {'b_in': 8.0,
     'w_up_b': 2.876,
     'norm_a_g': 8.0,
     'rel_bias': 8.0,
     'ln_g': 2.845,
     'ln_b': 2.92}
    for name, (base, spread) in spreads.items():
        noise = np.random.default_rng([zlib.crc32(name.encode()), seed]).standard_normal(out[name].shape)
        drawn = base * np.exp(spread * noise) if base else spread * noise
        out[name] = __import__('jax').numpy.asarray(drawn.astype(out[name].dtype))
    for name, factor in factors.items():
        out[name] = (out[name] * factor).astype(out[name].dtype)
    return out
```

```python
from contextlib import ExitStack

import numpy as np
import concourse.bass as bass
from concourse import mybir

F32 = mybir.dt.float32
F32R = mybir.dt.float32r
I32 = mybir.dt.int32
ALU = mybir.AluOpType
ACT = mybir.ActivationFunctionType

P = 128
D_MODEL, SEQ, DEPTH = 1024, 512, 1
D_A = D_B = 512
HEADS_A, HEADS_B, HEADS_I = 4, 8, 8
TOPK = min(256, SEQ // 4)
BUCKETS, MAX_DISTANCE = 32, 128
ALPHA = (2 * DEPTH) ** 0.25
LN_EPS, RMS_EPS = 1e-5, 1e-6
KT = D_MODEL // P
TB = SEQ // P
UW = 256
QSCALE = 64 ** -0.5
WSCALE = HEADS_I ** -0.5
NEG = -1e30
TAKEN = -3e38
F_FLOOR = -40.0
SEG = 64
NSEG = SEQ // SEG
LEVELS = (64, 32, 16, 8, 4, 2, 1)

UNITS = ["qi0", "qi1", "kiwi", "vb0", "vb1", "qb0", "kb0", "qb1", "kb1", "zb0", "zb1", "za0", "za1",
         "ia0", "ia1", "fa0", "qa0", "fa1", "qa1", "ga0", "ga1", "ga2", "ga3",
         "gb0", "up0", "gb1", "up1", "gb2", "up2", "gb3", "up3"]
NMAIN = len(UNITS)
NOUT = 4
NU = NMAIN + NOUT
COLUMNS = {"qa": 0, "fa": 512, "ia": 1024, "za": 1536, "qb": 2048, "kb": 2560, "vb": 3072, "zb": 3584,
           "qi": 4096, "ki": 4608, "wi": 4672, "ga": 4680, "gb": 5704}
WKI = 2 * 64 + HEADS_I
NPROJ = [sum(not n.startswith("up") for n in UNITS[:u]) for u in range(NMAIN + 1)]

DOTS = [(b, h) for b in range(1, TB) for h in range(HEADS_I)]
ITEMS = [(b, h) for b in range(TB) for h in range(HEADS_B)]
QK0 = len(DOTS)
TREE0 = QK0 + len(ITEMS)
N_CONSTS = 9
T5W = SEQ + P
TREE = [("diag", 0), ("diag", 1), ("lv", 0), ("128", 0), ("256", 0), ("256", 1),
        ("lv", 1), ("lv", 2), ("lv", 3), ("lv", 4), ("lv", 5), ("lv", 6)]
NTREE = len(TREE)

Q_DOTS = 4 * 3
Q_ATT = 4 * 8
Q_TREE = (72, 80)
ROUNDS = TOPK // 8


def topk_rounds():
    plan = {}
    for b, first, per in ((1, 17, 2), (2, 25, 2), (3, 33, 1)):
        for r in range(ROUNDS):
            plan.setdefault(first + r // per, []).append((b, r))
    return plan


def lvl_item(pair, lv):
    return TREE0 + NTREE * pair + TREE.index(("lv", lv))


def hybrid_kernel(nc, x_t, x_tok, w_units, w_kiwi, b_cols, b_ia, b_vb, b_wi, lb_cols, g_cols, rel_bias,
                  ln_g, ln_b, one_hot, ident, causal, tree_masks, out):
    with ExitStack() as ctx:
        def sb(name, shape, dt=F32, stack=ctx):
            return stack.enter_context(nc.sbuf_tensor(name, shape, dt))

        def sem(name):
            return ctx.enter_context(nc.semaphore(name))

        x_hi, x_lo = (sb(n, [P, KT, SEQ], F32R) for n in ("x_hi", "x_lo"))
        w_raw = sb("w_raw", [P, 2, KT * UW])
        w_hi, w_lo = (sb(n, [P, 2, KT, UW], F32R) for n in ("w_hi", "w_lo"))
        id_sb = sb("id_sb", [P, P])
        causal_sb = sb("causal_sb", [P, P])
        ones_sb = sb("ones_sb", [P, P])
        masks_sb = sb("masks_sb", [P, len(LEVELS), 64], I32)
        bias = sb("bias", [P, 2 * NMAIN])
        bias_mod = sb("bias_mod", [P, 2 * NMAIN])
        bias_ia, bias_vb = sb("bias_ia", [P, D_A]), sb("bias_vb", [P, D_B])
        bias_wi = sb("bias_wi", [P, HEADS_I])
        w_idx = sb("w_idx", [P, TB, HEADS_I])
        lb = sb("lb", [P, 7, HEADS_A])
        g_a = sb("g_a", [P, HEADS_A])
        eps = sb("eps", [P, 2])
        best8 = sb("best8", [P, 8])
        nmax, prob_sum, prob_rcp = (sb(n, [P, 2]) for n in ("nmax", "prob_sum", "prob_rcp"))
        stats, aggr, rstd = sb("stats", [P, TB, 2, 6]), sb("aggr", [P, TB, 2]), sb("rstd", [P, TB, 2])
        z_a = sb("z_a", [P, HEADS_A, SEQ])
        z_b = sb("z_b", [P, HEADS_B // 2, SEQ])
        U1 = 78 * 1024 + 512

        with ExitStack() as s:
            q_idx, k_idx = sb("q_idx", [P, 4, SEQ], stack=s), sb("k_idx", [P, SEQ], stack=s)
            score = {b: sb(f"score{b}", [P, (b + 1) * P], stack=s) for b in range(1, TB)}
            scratch = sb("scratch", [P, 2, SEQ], stack=s)
            q_b, k_b = sb("q_b", [P, 4, SEQ], stack=s), sb("k_b", [P, 4, SEQ], stack=s)
            v_b = sb("v_b", [P, TB, D_B], stack=s)
            t5 = sb("t5", [P, HEADS_B, SEQ], stack=s)
            pen = {b: sb(f"pen{b}", [P, (b + 1) * P], stack=s) for b in range(1, TB)}
            logit = sb("logit", [P, 2, SEQ], stack=s)
            prob = sb("prob", [P, 2, SEQ], stack=s)
            prob_t = sb("prob_t", [P, 2, SEQ], stack=s)
        with ExitStack() as s:
            cum = sb("cum", [P, HEADS_A, SEQ], stack=s)
            q_a = sb("q_a", [P, HEADS_A, SEQ], stack=s)
            k_a = sb("k_a", [P, 2, SEQ], stack=s)
            q_r, k_l = sb("q_r", [P, 2, SEQ], stack=s), sb("k_l", [P, 2, SEQ], stack=s)
            dec = sb("dec", [P, 2, 2 * SEQ], stack=s)
            q_c = sb("q_c", [P, 2, 2, SEQ // 2], stack=s)
            k_c = sb("k_c", [P, 2, 2 * SEQ], stack=s)
            far = sb("far", [P, 4, 2, SEQ // 2], stack=s)
            far_f = sb("far_f", [P, 4, 2, 4], stack=s)
            att = sb("att", [P, 2, TB, SEQ], stack=s)
            reset = sb("reset", [P, SEQ], stack=s)
            far_g = sb("far_g", [P, 2, NSEG], stack=s)
            square = sb("square", [P, 2, SEQ], stack=s)
        with ExitStack() as s:
            o_hi, o_lo = (sb(n, [P, 8, SEQ], F32R, s) for n in ("o_hi", "o_lo"))
            m_hi, m_lo = (sb(n, [P, KT, SEQ], F32R, s) for n in ("m_hi", "m_lo"))
            g_b = sb("g_b", [P, 2, SEQ], stack=s)
            mix = sb("mix", [P, 2, SEQ], stack=s)
        with ExitStack() as s:
            y_sb = sb("y_sb", [P, TB, D_MODEL], stack=s)
        sb("over", [P, U1 // 4])
        with ExitStack() as s:
            v_a = sb("v_a", [P, TB, D_A], stack=s)
            gate_a = sb("gate_a", [P, KT, SEQ], stack=s)
        with ExitStack() as s:
            hot_sb, table = sb("hot_sb", [BUCKETS, T5W], stack=s), sb("table", [HEADS_B, T5W], stack=s)
            rel_sb = sb("rel_sb", [BUCKETS, HEADS_B], stack=s)
            sb("under", [P, 2048 - 2 * T5W - HEADS_B], stack=s)
            x_raw = sb("x_raw", [P, KT, SEQ], stack=s)
        with ExitStack() as s:
            ln_gb = sb("ln_gb", [P, 2, D_MODEL], stack=s)
            x_res = sb("x_res", [P, TB, D_MODEL], stack=s)

        ps = [ctx.enter_context(nc.psum_tensor(f"bank{i}", [P, 512], F32)) for i in range(8)]
        proj_bank, log_bank, turn_bank, out_bank = ps[0:2], ps[2:4], ps[4:6], ps[6:8]
        up_bank = log_bank + turn_bank
        y_bank = [out_bank + proj_bank, log_bank + turn_bank]
        t5_rep = nc.dram_tensor("t5_rep", [P, HEADS_B, T5W], F32).ap()


        x_in = [sem(f"x_in{j}") for j in range(4)]
        w_in = [sem(f"w_in{j}") for j in range(2)]
        consts_in, table_in, rep_out, t5_in = sem("consts_in"), sem("table_in"), sem("rep_out"), sem("t5_in")
        ln_in = sem("ln_in")
        res_in = [sem(f"res_in{t}") for t in range(TB)]
        y_out = sem("y_out")
        table_full, table_done = sem("table_full"), sem("table_done")
        pool_set, bias_mod_done = sem("pool_set"), sem("bias_mod_done")
        lb_step, lb_exp, dve_step = sem("lb_step"), sem("lb_exp"), sem("dve_step")
        x_hi_done, x_lo_done = sem("x_hi_done"), sem("x_lo_done")
        hi_done, lo_done = sem("hi_done"), sem("lo_done")
        part_done = sem("part_done")
        proj_out = [sem(f"proj_out{j}") for j in range(2)]
        log_full, log_out = sem("log_full"), [sem(f"log_out{j}") for j in range(2)]
        turn_full, turn_out = sem("turn_full"), [sem(f"turn_out{j}") for j in range(2)]
        pv_done, recur_done = sem("pv_done"), sem("recur_done")
        out_out = [sem(f"out_out{j}") for j in range(2)]
        up_out = [sem(f"up_out{j}") for j in range(4)]
        w_idx_done, relu_used, pen_done, topk_step = sem("w_idx_done"), sem("relu_used"), sem("pen_done"), sem("topk_step")
        logit_pre, exp_done, rcp_done, norm_done = (sem(n) for n in ("logit_pre", "exp_done", "rcp_done", "norm_done"))
        ez_done, dz_done, rz_done, z_done = (sem(n) for n in ("ez_done", "dz_done", "rz_done", "z_done"))
        gate_a_plus1, gate_a_done = sem("gate_a_plus1"), sem("gate_a_done")
        gate_b_plus1, gate_b_done = sem("gate_b_plus1"), sem("gate_b_done")
        f_dve, f_act, cum_done, k_raw, k_done = (sem(n) for n in ("forget_dve", "forget_act", "cum_done", "k_raw", "k_done"))
        seg_decay, rl_done, near_done = sem("seg_decay"), sem("rl_done"), sem("near_done")
        reset_set, far_f_step, far_f_done, far_done = (sem(n) for n in ("reset_set", "far_f_step", "far_f_done", "far_done"))
        dist_pool, dist_dve = sem("dist_pool"), sem("dist_dve")
        fac_done, qk_done = sem("fac_done"), sem("qk_done")
        sq_done, ln_ms, rms_done, branch_a = (sem(n) for n in ("sq_done", "ln_ms", "rms_done", "branch_a"))
        o_hi_done, o_lo_done = sem("o_hi_done"), sem("o_lo_done")
        mix_part, mix_done, m_hi_done, m_lo_done = (sem(n) for n in ("mix_part", "mix_done", "m_hi_done", "m_lo_done"))
        y_full, y_aggr = sem("y_full"), sem("y_aggr")
        ln_log, ln_rstd, ln_norm = sem("ln_log"), sem("ln_rstd"), sem("ln_norm")
        ln_scaled, y_pool, y_dve = sem("ln_scaled"), sem("y_pool"), sem("y_dve")

        rounds = topk_rounds()
        BLOCK_OUT = {47: 0, 50: 1, 58: 2, 66: 3}

        def unit_width(u):
            return WKI if u < NMAIN and UNITS[u] == "kiwi" else UW

        def raw(u):
            w = unit_width(u)
            return w_raw[:, u % 2, 0:KT * w].rearrange("p (k n) -> p k n", k=KT)

        def split_target(u, over_x, ring):
            if NMAIN <= u < NMAIN + 2:
                c = (u - NMAIN) * UW
                return over_x[:, :, c:c + UW]
            return ring[:, u % 2, :, 0:unit_width(u)]

        def wait_split_target(eng, u):
            last = {NMAIN: NMAIN - 2, NMAIN + 1: NMAIN - 2, NMAIN + 2: NMAIN - 2, NMAIN + 3: NMAIN - 1}.get(u, u - 2)
            if last >= 0:
                eng.wait_ge(part_done, 2 * last + 2)

        def wait_proj_out(eng, name, i):
            eng.wait_ge(proj_out[i], NPROJ[UNITS.index(name)] + 1)

        def wait_log_out(eng, idx):
            eng.wait_ge(log_out[idx % 2], idx // 2 + 1)

        def wait_turn_out(eng, idx):
            eng.wait_ge(turn_out[idx % 2], idx // 2 + 1)

        def wait_tree_out(eng, p):
            wait_log_out(eng, TREE0 + NTREE * (p + 1) - 2)
            wait_log_out(eng, TREE0 + NTREE * (p + 1) - 1)

        def wait_lvl_multiplied(eng, p, lv):
            eng.wait_ge(log_full, TREE0 + NTREE * p + TREE.index(("lv", lv)) + 1)

        def rows(h):
            return slice(64 * (h % 2), 64 * (h % 2) + 64)

        def queries(b):
            return slice(b * P, b * P + P)

        def tree_at(q):
            return [(p, n) for p in range(2) for n in range(NTREE) if Q_TREE[p] + n // 2 == q]

        def flat(ap):
            return ap.rearrange("p a t -> p (a t)")

        def groups(tile, h):
            return tile.rearrange("p (n w) -> p n w", w=2 * h)

        def strided(base, dims):
            return bass.AP(base.tensor, base.offset, [list(base.ap[0])] + dims)

        def att_blocks(a, h=None):
            step = SEQ + P
            if h is None:
                return strided(att[:, a, 0, 0:P], [[step, TB], [1, P]])
            return strided(att[:, a, 0, h:P], [[step, TB], [2 * h, 64 // h], [1, h]])

        def z_part(n):
            return (z_b if n < 4 else z_a)[:, n % 4, :]

        def wait_dist(eng, p, lv):
            if lv % 2:
                eng.wait_ge(dist_dve, 3 * p + lv // 2 + 1)
            else:
                eng.wait_ge(dist_pool, 4 * p + lv // 2 + 1)

        def part_out_at(q):
            u, i = (q // 4 - 1, 1) if q % 4 == 0 else (q // 4, 0)
            if u < 0 or q % 2 or not UNITS[u][2:].isdigit():
                return None
            return UNITS[u][:2], 2 * int(UNITS[u][2]) + i

        def merged_at(q):
            part = part_out_at(q)
            return part[1] if part and part[0] == "up" else None

        def level_distance(engine, p, lv):
            h = LEVELS[lv]
            c = groups(flat(cum[:, 2 * p:2 * p + 2, :]), h)
            return engine.tensor_tensor(groups(dec[:, lv % 2, :], h), c,
                                        c[:, :, h - 1:h].broadcast_to([P, 2 * SEQ // (2 * h), 2 * h]), ALU.subtract)

        block = ctx.enter_context(nc.Block())

        @block.sync
        def _(sp):
            for u in range(NU):
                if u >= 2:
                    sp.wait_ge(lo_done, 4 * (u - 1))
                if u < NMAIN and UNITS[u] == "kiwi":
                    unit = w_kiwi
                else:
                    unit = w_units[u - (u > UNITS.index("kiwi"))]
                sp.dma_start(w_raw[:, u % 2, 0:KT * unit_width(u)], unit).then_inc(w_in[u % 2], 16)
                if u == 3:
                    sp.wait_ge(table_done, 2)
                    sp.dma_start(t5_rep.rearrange("p h d -> h p d"),
                                 table[:].unsqueeze(1).broadcast_to([HEADS_B, P, T5W])).then_inc(rep_out, 16)
                if u == 5:
                    sp.wait_ge(rep_out, 16)
                    skewed = bass.AP(t5_rep.tensor, t5_rep.offset + P - 1,
                                     [[HEADS_B * T5W - 1, P], [T5W, HEADS_B], [1, SEQ]])
                    sp.dma_start(t5[:], skewed).then_inc(t5_in, 16)
            sp.wait_ge(recur_done, HEADS_A)
            sp.dma_start(ln_gb[:, 0, :], ln_g.partition_broadcast(P)).then_inc(ln_in, 16)
            sp.dma_start(ln_gb[:, 1, :], ln_b.partition_broadcast(P)).then_inc(ln_in, 16)
            sp.wait_ge(mix_done, KT)
            for t in range(TB):
                sp.dma_start(x_res[:, t, :], x_tok[t]).then_inc(res_in[t], 16)
            for t in range(TB):
                if t < TB - 1:
                    sp.wait_ge(y_pool, t + 1)
                else:
                    sp.wait_ge(y_dve, 1)
                sp.dma_start(out[t], y_sb[:, t, :]).then_inc(y_out, 16)
            sp.wait_ge(y_out, 16 * TB)

        @block.tensor
        def _(pe):
            def split_product(dst, a_hi, a_lo, b_hi, b_lo, first, last):
                nc.tensor.matmul(dst, a_hi, b_hi, start=first, stop=False)
                nc.tensor.matmul(dst, a_hi, b_lo, start=False, stop=False)
                return nc.tensor.matmul(dst, a_lo, b_hi, start=False, stop=last)

            def wait_piece(u, k):
                if k % 2 == 0:
                    pe.wait_ge(lo_done, 4 * u + k // 2 + 1)
                    if u == 0:
                        pe.wait_ge(x_lo_done, k // 2 + 1)

            def wait_bank(u, i):
                if NPROJ[u]:
                    pe.wait_ge(proj_out[i], NPROJ[u])

            def quarter_f(u, i, j):
                if j == 0:
                    wait_bank(u, i)
                c = slice(i * P, i * P + P)
                for k in range(4 * j, 4 * j + 4):
                    if i == 0:
                        wait_piece(u, k)
                    mm = split_product(proj_bank[i][:], w_hi[:, u % 2, k, c], w_lo[:, u % 2, k, c],
                                       x_hi[:, k, :], x_lo[:, k, :], k == 0, k == KT - 1)
                if j == 1:
                    mm.then_inc(part_done, 1)

            def quarter_t(u, i, j):
                if j == 0:
                    wait_bank(u, i)
                tk = queries(2 * i + j)
                for k in range(KT):
                    if i == 0 and j == 0:
                        wait_piece(u, k)
                    mm = split_product(proj_bank[i][:, j * UW:(j + 1) * UW], x_hi[:, k, tk], x_lo[:, k, tk],
                                       w_hi[:, u % 2, k, :], w_lo[:, u % 2, k, :], k == 0, k == KT - 1)
                if j == 1:
                    mm.then_inc(part_done, 1)

            def quarter_wi(u, j):
                if j == 0:
                    wait_bank(u, 1)
                c = slice(2 * 64, WKI)
                for t in (2 * j, 2 * j + 1):
                    for k in range(KT):
                        mm = split_product(proj_bank[1][:, t * HEADS_I:(t + 1) * HEADS_I],
                                           x_hi[:, k, queries(t)], x_lo[:, k, queries(t)],
                                           w_hi[:, u % 2, k, c], w_lo[:, u % 2, k, c], k == 0, k == KT - 1)
                if j == 1:
                    mm.then_inc(part_done, 1)

            def quarter_up(u, i, j):
                fill = 2 * (2 * int(UNITS[u][2]) + i) + j
                if fill < 2:
                    wait_log_out(pe, TREE0 + 2 * NTREE - 2 + fill)
                    pe.wait_ge(o_hi_done, 2 * (j + 1))
                    pe.wait_ge(o_lo_done, 2 * (j + 1))
                elif fill < 4:
                    wait_turn_out(pe, len(ITEMS) + HEADS_A - 4 + fill)
                else:
                    pe.wait_ge(up_out[fill % 4], fill // 4)
                c = slice(i * P, i * P + P)
                for k in range(4 * j, 4 * j + 4):
                    if i == 0:
                        wait_piece(u, k)
                    mm = split_product(up_bank[fill % 4][:], w_hi[:, u % 2, k, c], w_lo[:, u % 2, k, c],
                                       o_hi[:, k, :], o_lo[:, k, :], k % 4 == 0, k % 4 == 3)
                if j == 1:
                    mm.then_inc(part_done, 1)

            def log_slot(idx):
                if idx >= 2:
                    wait_log_out(pe, idx - 2)
                return log_bank[idx % 2]

            def dots(i):
                b, h = DOTS[i]
                dst = log_slot(i)
                if i == 0:
                    for name in ("qi0", "qi1"):
                        wait_proj_out(pe, name, 0)
                        wait_proj_out(pe, name, 1)
                    wait_proj_out(pe, "kiwi", 0)
                n = (b + 1) * P
                nc.tensor.matmul(dst[:, 0:n], q_idx[rows(h), h // 2, queries(b)], k_idx[rows(h), 0:n],
                                 start=True, stop=True).then_inc(log_full, 1)

            def scores(i):
                b, h = ITEMS[i]
                dst = log_slot(QK0 + i)
                if b == 0 and h % 2 == 0:
                    wait_proj_out(pe, f"qb{h // 4}", h // 2 % 2)
                    wait_proj_out(pe, f"kb{h // 4}", h // 2 % 2)
                n = (b + 1) * P
                nc.tensor.matmul(dst[:, 0:n], q_b[rows(h), h // 2, queries(b)], k_b[rows(h), h // 2, 0:n],
                                 start=True, stop=True).then_inc(log_full, 1)

            def turn_probs(i):
                b, h = ITEMS[i]
                pe.wait_ge(norm_done, i + 1)
                if i >= 2:
                    wait_turn_out(pe, i - 2)
                for c in range(b + 1):
                    mm = nc.tensor.transpose(turn_bank[i % 2][:, queries(c)], prob[:, i % 2, queries(c)], id_sb[:])
                mm.then_inc(turn_full, 1)

            def attend(i):
                b, h = ITEMS[i]
                wait_turn_out(pe, i)
                if i == 0:
                    wait_proj_out(pe, "vb1", 0)
                    wait_proj_out(pe, "vb1", 1)
                if h == 0 and b >= 2:
                    pe.wait_ge(out_out[b % 2], b // 2)
                for c in range(b + 1):
                    mm = nc.tensor.matmul(out_bank[b % 2][rows(h), queries(h // 2)], v_b[:, c, h * 64:h * 64 + 64],
                                          prob_t[:, i % 2, queries(c)], start=(c == 0), stop=(c == b),
                                          skip_group_check=True)
                mm.then_inc(pv_done, 1)

            def tree(p, n):
                kind, m = TREE[n]
                idx = TREE0 + NTREE * p + n
                dst = log_slot(idx)
                if kind == "diag":
                    pe.wait_ge(k_done, 2 * (p + 1))
                    for t in range(TB):
                        mm = nc.tensor.matmul(dst[:, queries(t)], k_a[:, m, queries(t)],
                                              q_a[:, 2 * p + m, queries(t)], start=True, stop=True)
                elif kind == "lv":
                    if m == 0:
                        pe.wait_ge(near_done, 2 * p + 2)
                    else:
                        pe.wait_ge(qk_done, 2 * (6 * p + m))
                    for a in range(2):
                        for t in range(TB):
                            c = (a * TB + t) * 64
                            if m == 0:
                                key, query = k_l[:, a, queries(t)], q_r[:, a, t * P + 64:t * P + P]
                            else:
                                ring = (m - 1) % 2
                                key = k_c[:, ring, a * SEQ + t * P:a * SEQ + t * P + P]
                                query = q_c[:, ring, a, t * 64:t * 64 + 64]
                            mm = nc.tensor.matmul(dst[:, c:c + 64], key, query, start=True, stop=True)
                elif kind == "128":
                    pe.wait_ge(far_done, 6 * p + 4)
                    for a in range(2):
                        for t in range(2):
                            mm = nc.tensor.matmul(dst[:, queries(2 * a + t)], far[:, 0, a, queries(t)],
                                                  far[:, 1, a, queries(t)], start=True, stop=True)
                else:
                    pe.wait_ge(far_done, 6 * p + 6)
                    for t in range(2):
                        mm = nc.tensor.matmul(dst[:, t * 256:t * 256 + 256], far[:, 2, m, queries(t)],
                                              far[:, 3, m, :], start=True, stop=True)
                mm.then_inc(log_full, 1)

            def recur(h):
                bank = out_bank[h % 2]
                pe.wait_ge(out_out[h % 2], 2 + h // 2)
                wait_tree_out(pe, h // 2)
                if h == 0:
                    wait_proj_out(pe, "ia1", 0)
                    wait_proj_out(pe, "ia1", 1)
                for s in range(TB):
                    mm = nc.tensor.matmul(bank[:, s * P:SEQ], v_a[:, s, queries(h)], att[:, h % 2, s, s * P:SEQ],
                                          start=(s == 0), stop=(s == TB - 1), skip_group_check=True)
                mm.then_inc(recur_done, 1)

            def mean_square(h):
                i = len(ITEMS) + h
                pe.wait_ge(sq_done, h + 1)
                wait_turn_out(pe, i - 2)
                nc.tensor.matmul(turn_bank[i % 2][:], ones_sb[:], square[:, h % 2, :], start=True,
                                 stop=True).then_inc(turn_full, 1)

            def side(q):
                for i in range(2 * (q - Q_DOTS), 2 * (q - Q_DOTS) + 2):
                    if 0 <= i < len(DOTS):
                        dots(i)
                i = q - Q_ATT
                if 0 <= i - 1 < len(ITEMS):
                    turn_probs(i - 1)
                if 0 <= i < len(ITEMS):
                    scores(i)
                if 0 <= i - 2 < len(ITEMS):
                    attend(i - 2)
                for p, n in tree_at(q):
                    tree(p, n)
                for h in range(HEADS_A):
                    if q == Q_TREE[h // 2] + 7:
                        recur(h)
                    if q == Q_TREE[h // 2] + 8:
                        mean_square(h)

            pe.wait_ge(table_in, 32)
            for c in range(2):
                mm = nc.tensor.matmul(turn_bank[c][0:HEADS_B, 0:320], rel_sb[:], hot_sb[:, c * 320:c * 320 + 320],
                                      start=True, stop=True)
            mm.then_inc(table_full, 1)
            for u, name in enumerate(UNITS):
                for q in range(4):
                    i, j = q // 2, q % 2
                    if name.startswith("up"):
                        quarter_up(u, i, j)
                    elif name[:2] in ("vb", "ia"):
                        quarter_t(u, i, j)
                    elif name == "kiwi" and i == 1:
                        quarter_wi(u, j)
                    else:
                        quarter_f(u, i, j)
                    if u == 0 and q == 0:
                        pe.wait_ge(pool_set, 1)
                        pe.wait_ge(consts_in, 16 * N_CONSTS)
                    side(4 * u + q)
            for half in range(2):
                pe.wait_ge(lo_done, 4 * (NMAIN + 2 * half + 2))
                for t in range(TB):
                    bank = y_bank[half][t]
                    if half == 0 and t < 2:
                        pe.wait_ge(out_out[t], 4)
                    elif half == 0:
                        pe.wait_ge(proj_out[t - 2], NPROJ[NMAIN])
                    else:
                        pe.wait_ge(up_out[t], 2 * KT // 4)
                    for k in range(KT):
                        if half == 0 and t == 0:
                            pe.wait_ge(m_lo_done, k + 1)
                        m = m_hi[:, k, queries(t)], m_lo[:, k, queries(t)]
                        if half == 0:
                            mm = split_product(bank[:], *m, x_hi[:, k, :], x_lo[:, k, :], k == 0, k == KT - 1)
                        else:
                            mm = split_product(bank[:].rearrange("p (s n) -> p s n", s=2), *m,
                                               w_hi[:, :, k, :], w_lo[:, :, k, :], k == 0, k == KT - 1)
                    mm.then_inc(y_full, 1)

        @block.scalar
        def _(act):
            nc.scalar.preload_act_table_set("natural_log_exp_and_others")
            act.dma_start(rel_sb[:], rel_bias).then_inc(table_in, 16)
            act.dma_start(hot_sb[:], one_hot).then_inc(table_in, 16)
            for j in range(4):
                act.dma_start(x_raw[:, 2 * j:2 * j + 2, :], x_t[:, 2 * j:2 * j + 2, :]).then_inc(x_in[j], 16)
            for dst, src in ((bias[:], b_cols), (lb[:, 0, :], lb_cols), (g_a[:], g_cols), (id_sb[:], ident),
                             (causal_sb[:], causal), (masks_sb[:], tree_masks),
                             (bias_ia[:], b_ia.partition_broadcast(P)), (bias_vb[:], b_vb.partition_broadcast(P)),
                             (bias_wi[:], b_wi.partition_broadcast(P))):
                act.dma_start(dst, src).then_inc(consts_in, 16)

            def split_hi(u, a):
                if a == 0:
                    act.wait_ge(w_in[u % 2], 16 * (u // 2 + 1))
                    wait_split_target(act, u)
                k = slice(4 * a, 4 * a + 4)
                nc.scalar.activation(split_target(u, x_hi, w_hi)[:, k, :], raw(u)[:, k, :],
                                     ACT.Copy).then_inc(hi_done, 1)

            def leave_bank(u, i):
                name = UNITS[u]
                kind = name[:2]
                if kind in ("vb", "ia", "up") or (name == "kiwi" and i == 1):
                    return
                act.wait_ge(part_done, 2 * u + i + 1)
                tile = 0 if name == "kiwi" else 2 * int(name[2]) + i
                c = 2 * u + i
                func, b_col, scale = ACT.Identity, bias[:, c:c + 1], 1.0
                if kind == "ki":
                    dst = k_idx[:]
                elif kind == "qi":
                    dst = q_idx[:, tile, :]
                elif kind == "qb":
                    dst, b_col, scale = q_b[:, tile, :], bias_mod[:, c:c + 1], QSCALE
                    act.wait_ge(bias_mod_done, 2)
                elif kind == "kb":
                    dst = k_b[:, tile, :]
                elif kind in ("zb", "za"):
                    dst = (z_b if kind == "zb" else z_a)[:, tile, :]
                elif kind in ("fa", "qa"):
                    dst = (cum if kind == "fa" else q_a)[:, tile, :]
                    if name == "fa0" and i == 0:
                        act.wait_ge(pen_done, TB - 1)
                        act.wait_ge(z_done, 8)
                elif kind == "ga":
                    dst, func, b_col, scale = gate_a[:, tile, :], ACT.Exp, bias_mod[:, c:c + 1], -1.0
                    if tile == 0:
                        act.wait_ge(x_lo_done, 4)
                else:
                    dst, func, b_col, scale = g_b[:, tile % 2, :], ACT.Exp, bias_mod[:, c:c + 1], -1.0
                    if tile == 0:
                        act.wait_ge(branch_a, HEADS_A)
                    elif tile >= 2:
                        act.wait_ge(mix_done, tile - 1)
                nc.scalar.activation(dst, proj_bank[i][:], func, bias=b_col, scale=scale).then_inc(proj_out[i], 1)
                if kind in ("zb", "za"):
                    n = 2 * (u - UNITS.index("zb0")) + i
                    wait_proj_out(act, name, i)
                    if n < 2:
                        act.wait_ge(relu_used, len(DOTS))
                    else:
                        act.wait_ge(z_done, n - 1)
                    nc.scalar.activation(scratch[:, n % 2, :], z_part(n), ACT.Exp, scale=-1.0).then_inc(ez_done, 1)

            def relu(i):
                b, h = DOTS[i]
                act.wait_ge(log_full, i + 1)
                if i >= 2:
                    act.wait_ge(relu_used, i - 1)
                n = (b + 1) * P
                nc.scalar.activation(scratch[:, i % 2, 0:n], log_bank[i % 2][:, 0:n], ACT.Relu,
                                     scale=QSCALE).then_inc(log_out[i % 2], 1)

            def softmax_exp(i):
                b, h = ITEMS[i]
                wait_log_out(act, QK0 + i)
                if i >= 2:
                    act.wait_ge(turn_full, i - 1)
                    act.wait_ge(rcp_done, i - 1)
                n = (b + 1) * P
                nc.scalar.activation(prob[:, i % 2, 0:n], logit[:, i % 2, 0:n], ACT.Exp,
                                     bias=nmax[:, i % 2:i % 2 + 1], scale=-1.0,
                                     accum_out=prob_sum[:, i % 2:i % 2 + 1]).then_inc(exp_done, 1)

            def forget(p, n):
                act.wait_ge(f_dve, 4 * p + (1, 1, 2, 2, 4)[n])
                if n in (1, 3):
                    act.wait_ge(f_act, 6 * p + (1, 0, 3)[n - 1])
                if n == 0:
                    nc.scalar.activation(dec[:, 0, :], dec[:, 0, :], ACT.Exp).then_inc(f_act, 1)
                elif n == 1:
                    nc.scalar.activation(dec[:, 0, :], dec[:, 0, :], ACT.Ln, bias=1.0).then_inc(f_act, 1)
                elif n == 2:
                    nc.scalar.activation(dec[:, 1, :], dec[:, 1, :], ACT.Exp, scale=-1.0).then_inc(f_act, 1)
                elif n == 3:
                    act.wait_ge(lb_step, 5)
                    for a in range(2):
                        c = slice(a * SEQ, a * SEQ + SEQ)
                        nc.scalar.activation(dec[:, 1, c], dec[:, 1, c], ACT.Ln, bias=1.0,
                                             scale=lb[:, 5, 2 * p + a:2 * p + a + 1]).then_inc(f_act, 1)
                else:
                    if p:
                        act.wait_ge(log_full, TREE0 + NTREE)
                        act.wait_ge(qk_done, 12)
                    nc.scalar.activation(flat(k_a[:]), k_c[:, 1, :], ACT.Exp).then_inc(f_act, 1)

            def near_factors(p):
                act.wait_ge(cum_done, 2 * (p + 1))
                cp = cum[:, 2 * p:2 * p + 2, :]
                if p:
                    act.wait_ge(far_f_done, p)
                    wait_lvl_multiplied(act, 0, 0)
                    act.wait_ge(far_done, 6)
                nc.scalar.activation(far_g[:], cp[:, :, SEG - 1::SEG], ACT.Exp).then_inc(seg_decay, 1)
                nc.scalar.activation(q_r[:], cp, ACT.Exp).then_inc(rl_done, 1)
                wait_dist(act, p, 0)
                nc.scalar.activation(flat(k_l[:]), dec[:, 0, :], ACT.Exp).then_inc(rl_done, 1)

            def level_factors(p, lv):
                wait_dist(act, p, lv)
                h = LEVELS[lv]
                v = groups(dec[:, lv % 2, :], h)
                nc.scalar.activation(v[:, :, h:2 * h], v[:, :, h:2 * h], ACT.Exp).then_inc(fac_done, 1)
                nc.scalar.activation(v[:, :, 0:h], v[:, :, 0:h], ACT.Exp, scale=-1.0).then_inc(fac_done, 1)

            def tree_copy(p, n):
                kind, m = TREE[n]
                if kind not in ("128", "256"):
                    return
                idx = TREE0 + NTREE * p + n
                act.wait_ge(log_full, idx + 1)
                if p:
                    act.wait_ge(recur_done, 2)
                bank = log_bank[idx % 2]
                if kind == "128":
                    for a in range(2):
                        ins = nc.scalar.activation(
                            strided(att[:, a, 0, P:2 * P], [[2 * (SEQ + P), 2], [1, P]]),
                            bank[:, 2 * a * P:2 * a * P + 2 * P].rearrange("p (t n) -> p t n", t=2), ACT.Copy)
                else:
                    ins = nc.scalar.activation(att[:, m, 0:2, 2 * P:SEQ],
                                               bank[:].rearrange("p (t n) -> p t n", t=2), ACT.Copy)
                ins.then_inc(log_out[idx % 2], 1)

            def squares(h):
                act.wait_ge(recur_done, h + 1)
                if h >= 2:
                    act.wait_ge(branch_a, h - 1)
                nc.scalar.activation(square[:, h % 2, :], out_bank[h % 2][:], ACT.Square).then_inc(sq_done, 1)

            def inverse_rms(h):
                i = len(ITEMS) + h
                act.wait_ge(turn_full, i + 1)
                nc.scalar.activation(square[:, h % 2, :], turn_bank[i % 2][:], ACT.Ln,
                                     bias=eps[:, 0:1]).then_inc(turn_out[i % 2], 1)
                wait_turn_out(act, i)
                nc.scalar.activation(square[:, h % 2, :], square[:, h % 2, :], ACT.Exp,
                                     scale=-0.5).then_inc(rms_done, 1)

            def round_merged(m):
                act.wait_ge(mix_done, m + 1)
                nc.scalar.activation(m_hi[:, m, :], mix[:, m % 2, :], ACT.Copy).then_inc(m_hi_done, 1)

            def side(q):
                for i in range(2 * (q - Q_DOTS), 2 * (q - Q_DOTS) + 2):
                    if 0 <= i < len(DOTS):
                        relu(i)
                if 0 <= q - Q_ATT < len(ITEMS):
                    softmax_exp(q - Q_ATT)
                for p, n in tree_at(q + 1):
                    if TREE[n][0] == "lv" and TREE[n][1]:
                        level_factors(p, TREE[n][1])
                for p in range(2):
                    at = q - Q_TREE[p]
                    if at == -4:
                        forget(p, 0)
                        forget(p, 1)
                    if at == -3:
                        forget(p, 2)
                        forget(p, 3)
                    if at == -2:
                        forget(p, 4)
                        near_factors(p)
                for p, n in tree_at(q):
                    tree_copy(p, n)
                for h in range(HEADS_A):
                    if q == Q_TREE[h // 2] + 7:
                        squares(h)
                    if q == Q_TREE[h // 2] + 8:
                        inverse_rms(h)

            act.wait_ge(lb_step, 1)
            nc.scalar.activation(lb[:, 2, :], lb[:, 1, :], ACT.Exp).then_inc(lb_exp, 1)
            act.wait_ge(pool_set, 1)
            act.wait_ge(consts_in, 16 * N_CONSTS)
            for u in (0, 1):
                split_hi(u, 0)
                split_hi(u, 1)
            for q in range(4 * NMAIN):
                u, j = q // 4, q % 4
                if j == 0 and u >= 1:
                    leave_bank(u - 1, 1)
                    split_hi(u + 1, 0)
                elif j == 1 and u >= 1:
                    split_hi(u + 1, 1)
                elif j == 2:
                    leave_bank(u, 0)
                side(q)
                if UNITS[u] == "gb0":
                    act.wait_ge(branch_a, HEADS_A)
                    z = z_a if j < 2 else z_b
                    nc.scalar.activation(flat(o_hi[:, 2 * j:2 * j + 2, :]), flat(z[:, 2 * j % 4:2 * j % 4 + 2, :]),
                                         ACT.Copy).then_inc(o_hi_done, 1)
                m = merged_at(q)
                if m is not None:
                    round_merged(m)
                if u == NMAIN - 1 and j >= 2:
                    split_hi(u + 2, j - 2)
            round_merged(KT - 1)
            for u in (NMAIN + 2, NMAIN + 3):
                split_hi(u, 0)
                split_hi(u, 1)
            for t in range(TB):
                act.wait_ge(y_aggr, t + 1)
                nc.scalar.activation(rstd[:, t, 0:1], aggr[:, t, 1:2], ACT.Ln, bias=eps[:, 1:2]).then_inc(ln_log, 1)
                act.wait_ge(ln_log, t + 1)
                nc.scalar.activation(rstd[:, t, 1:2], rstd[:, t, 0:1], ACT.Exp, scale=-0.5).then_inc(ln_rstd, 1)

        @block.vector
        def _(dve):
            steps = [0]

            def link(ins):
                steps[0] += 1
                ins.then_inc(dve_step, 1)
                dve.wait_ge(dve_step, steps[0])

            def split_x(j):
                k = slice(2 * j, 2 * j + 2)
                dve.wait_ge(x_in[j], 16)
                nc.vector.tensor_copy(x_hi[:, k, :], x_raw[:, k, :]).then_inc(x_hi_done, 1)
                dve.wait_ge(x_hi_done, j + 1)
                nc.vector.tensor_tensor(x_lo[:, k, :], x_raw[:, k, :], x_hi[:, k, :].bitcast(F32),
                                        ALU.subtract).then_inc(x_lo_done, 1)

            def lower_bound():
                dve.wait_ge(consts_in, 16 * N_CONSTS)
                nc.vector.tensor_tensor(lb[:, 1, :], lb[:, 0, :], lb[:, 0, :], ALU.subtract).then_inc(lb_step, 1)
                dve.wait_ge(lb_exp, 1)
                nc.vector.reciprocal(lb[:, 3, :], lb[:, 2, :]).then_inc(lb_step, 1)
                dve.wait_ge(lb_step, 2)
                nc.vector.tensor_tensor(lb[:, 4, :], lb[:, 2, :], lb[:, 3, :], ALU.mult).then_inc(lb_step, 1)
                dve.wait_ge(lb_step, 3)
                nc.vector.tensor_tensor(lb[:, 5, :], lb[:, 4, :], lb[:, 4, :], ALU.subtract).then_inc(lb_step, 1)
                dve.wait_ge(lb_step, 4)
                nc.vector.tensor_scalar(lb[:, 6, :], lb[:, 5, :], -1.0, 1.0, ALU.mult, ALU.add).then_inc(lb_step, 1)
                nc.vector.tensor_scalar(bias_mod[:], bias[:], -1.0, None, ALU.mult).then_inc(bias_mod_done, 1)
                dve.wait_ge(bias_mod_done, 1)
                first, last = 2 * UNITS.index("qb0"), 2 * UNITS.index("qb1") + 2
                nc.vector.tensor_scalar(bias_mod[:, first:last], bias[:, first:last], QSCALE, None,
                                        ALU.mult).then_inc(bias_mod_done, 1)

            def leave_bank(u, i):
                name = UNITS[u]
                kind = name[:2]
                if kind in ("vb", "ia"):
                    n = int(name[2])
                    c = slice(n * UW, n * UW + UW)
                    if kind == "ia":
                        dve.wait_ge(rep_out, 16)
                    dve.wait_ge(part_done, 2 * u + i + 1)
                    row = (bias_vb if kind == "vb" else bias_ia)[:, c].unsqueeze(1).broadcast_to([P, 2, UW])
                    nc.vector.tensor_tensor((v_b if kind == "vb" else v_a)[:, 2 * i:2 * i + 2, c],
                                            proj_bank[i][:].rearrange("p (t n) -> p t n", t=2), row,
                                            ALU.add).then_inc(proj_out[i], 1)
                elif name == "kiwi" and i == 1:
                    dve.wait_ge(part_done, 2 * u + 2)
                    nc.vector.tensor_tensor(
                        w_idx[:], proj_bank[1][:, 0:TB * HEADS_I].rearrange("p (t h) -> p t h", t=TB),
                        bias_wi[:].unsqueeze(1).broadcast_to([P, TB, HEADS_I]), ALU.add).then_inc(proj_out[1], 1)
                    wait_proj_out(dve, "kiwi", 1)
                    link(nc.vector.tensor_scalar(w_idx[:], w_idx[:], WSCALE, None, ALU.mult))

            def add_score(i):
                b, h = DOTS[i]
                wait_log_out(dve, i)
                n = (b + 1) * P
                w = w_idx[:, b, h:h + 1]
                if h == 0:
                    ins = nc.vector.tensor_scalar(score[b][:], scratch[:, i % 2, 0:n], w, None, ALU.mult)
                else:
                    dve.wait_ge(relu_used, i)
                    ins = nc.vector.scalar_tensor_tensor(out=score[b][:], in0=scratch[:, i % 2, 0:n], scalar=w,
                                                         in1=score[b][:], op0=ALU.mult, op1=ALU.add)
                ins.then_inc(relu_used, 1)
                if h == HEADS_I - 1:
                    dve.wait_ge(relu_used, i + 1)
                    diag = score[b][:, b * P:b * P + P]
                    link(nc.vector.tensor_tensor(diag, diag, causal_sb[:], ALU.add))

            def topk_round(b, r):
                link(nc.vector.max(best8[:], score[b][:]))
                link(nc.vector.match_replace(score[b][:], best8[:], score[b][:], TAKEN))
                if r == ROUNDS - 1:
                    nc.vector.tensor_scalar(pen[b][:], score[b][:], TAKEN, NEG, ALU.not_equal,
                                            ALU.mult).then_inc(pen_done, 1)

            def move_probs(i):
                b, h = ITEMS[i]
                dve.wait_ge(turn_full, i + 1)
                if i >= 2:
                    dve.wait_ge(pv_done, i - 1)
                n = (b + 1) * P
                nc.vector.tensor_copy(prob_t[:, i % 2, 0:n], turn_bank[i % 2][:, 0:n]).then_inc(turn_out[i % 2], 1)

            def logits(i):
                b, h = ITEMS[i]
                dve.wait_ge(log_full, QK0 + i + 1)
                dve.wait_ge(logit_pre, i + 1)
                if i >= 2:
                    dve.wait_ge(exp_done, i - 1)
                n = (b + 1) * P
                lg = logit[:, i % 2, 0:n]
                nc.vector.tensor_tensor_reduce(out=lg, in0=log_bank[i % 2][:, 0:n], in1=lg, scale=-1.0, scalar=3e38,
                                               op0=ALU.add, op1=ALU.min,
                                               accum_out=nmax[:, i % 2:i % 2 + 1]).then_inc(log_out[i % 2], 1)

            def sum_reciprocal(i):
                dve.wait_ge(exp_done, i + 1)
                if i >= 2:
                    dve.wait_ge(norm_done, i - 1)
                nc.vector.reciprocal(prob_rcp[:, i % 2:i % 2 + 1],
                                     prob_sum[:, i % 2:i % 2 + 1]).then_inc(rcp_done, 1)

            def block_out(b):
                dve.wait_ge(pv_done, HEADS_B * (b + 1))
                dve.wait_ge(z_done, 4)
                z = z_b[:, :, queries(b)]
                nc.vector.tensor_tensor(z, out_bank[b % 2][:].rearrange("p (c t) -> p c t", c=4), z,
                                        ALU.mult).then_inc(out_out[b % 2], 1)

            def silu(n):
                dve.wait_ge(dz_done, n + 1)
                e = scratch[:, n % 2, :]
                nc.vector.reciprocal(e, e).then_inc(rz_done, 1)
                dve.wait_ge(rz_done, n + 1)
                nc.vector.tensor_tensor(z_part(n), z_part(n), e, ALU.mult).then_inc(z_done, 1)

            def gate_reciprocal(m, branch):
                if branch == "a":
                    dve.wait_ge(gate_a_plus1, m + 1)
                    nc.vector.reciprocal(gate_a[:, m, :], gate_a[:, m, :]).then_inc(gate_a_done, 1)
                else:
                    dve.wait_ge(gate_b_plus1, m + 1)
                    nc.vector.reciprocal(g_b[:, m % 2, :], g_b[:, m % 2, :]).then_inc(gate_b_done, 1)

            def forget(p, n):
                f = flat(cum[:, 2 * p:2 * p + 2, :])
                if n == 0:
                    if p == 0:
                        dve.wait_ge(pv_done, len(ITEMS))
                    else:
                        dve.wait_ge(qk_done, 12)
                    for name in (f"fa{p}", f"qa{p}"):
                        wait_proj_out(dve, name, 0)
                        wait_proj_out(dve, name, 1)
                    nc.vector.scalar_tensor_tensor(out=dec[:, 0, :], in0=f, scalar=-1.0, in1=f, op0=ALU.mult,
                                                   op1=ALU.min).then_inc(f_dve, 1)
                    nc.vector.tensor_scalar(dec[:, 1, :], f, F_FLOOR, None, ALU.max).then_inc(f_dve, 1)
                else:
                    if p:
                        dve.wait_ge(log_full, TREE0 + NTREE)
                    log_sig = k_c[:, 0, :]
                    dve.wait_ge(f_act, 6 * p + 2)
                    nc.vector.scalar_tensor_tensor(out=log_sig, in0=f, scalar=0.0, in1=dec[:, 0, :], op0=ALU.min,
                                                   op1=ALU.subtract).then_inc(f_dve, 1)
                    dve.wait_ge(f_dve, 4 * p + 3)
                    nc.vector.tensor_tensor(k_c[:, 1, :], log_sig, f, ALU.subtract).then_inc(f_dve, 1)
                    dve.wait_ge(f_dve, 4 * p + 4)
                    dve.wait_ge(f_act, 6 * p + 5)
                    link(nc.vector.tensor_tensor(log_sig, log_sig, dec[:, 1, :], ALU.add))
                    dve.wait_ge(reset_set, 2)
                    for a in range(2):
                        nc.vector.tensor_tensor_scan(cum[:, 2 * p + a, :], reset[:], log_sig[:, a * SEQ:a * SEQ + SEQ],
                                                     0.0, ALU.mult, ALU.add).then_inc(cum_done, 1)

            def near_products(p):
                dve.wait_ge(rl_done, 2 * p + 2)
                dve.wait_ge(k_done, 2 * (p + 1))
                nc.vector.tensor_tensor(q_r[:], q_r[:], q_a[:, 2 * p:2 * p + 2, :], ALU.mult).then_inc(near_done, 1)
                nc.vector.tensor_tensor(k_l[:], k_l[:], k_a[:], ALU.mult).then_inc(near_done, 1)

            def far_products(p):
                dve.wait_ge(near_done, 2 * p + 2)
                dve.wait_ge(far_f_done, p + 1)
                if p:
                    dve.wait_ge(log_full, TREE0 + NTREE)
                for kind, (src, quad0) in enumerate(((k_l, 0), (q_r, 2))):
                    for a in range(2):
                        s4 = src[:, a, :].rearrange("p (b s t) -> p b s t", b=2, t=SEG)[:, :, quad0:quad0 + 2, :]
                        f4 = far_f[:, kind, a, :].rearrange("p (b s) -> p b s", b=2)
                        nc.vector.tensor_tensor(far[:, kind, a, :].rearrange("p (b s t) -> p b s t", b=2, t=SEG), s4,
                                                f4.unsqueeze(3).broadcast_to([P, 2, 2, SEG]),
                                                ALU.mult).then_inc(far_done, 1)
                for kind, (src, half) in enumerate(((k_l, 0), (q_r, 256)), 2):
                    s4 = src[:, :, half:half + 256].rearrange("p a (s t) -> p a s t", t=SEG)
                    nc.vector.tensor_tensor(far[:, kind, :, :].rearrange("p a (s t) -> p a s t", t=SEG), s4,
                                            far_f[:, kind, :, :].unsqueeze(3).broadcast_to([P, 2, 4, SEG]),
                                            ALU.mult).then_inc(far_done, 1)

            def distance(p, lv):
                if lv > 1:
                    dve.wait_ge(qk_done, 2 * (6 * p + lv - 2))
                level_distance(nc.vector, p, lv).then_inc(dist_dve, 1)

            def level_products(p, lv):
                h = LEVELS[lv]
                ring = (lv - 1) % 2
                dve.wait_ge(fac_done, 2 * (6 * p + lv))
                if lv > 2:
                    wait_lvl_multiplied(dve, p, lv - 2)
                v = groups(dec[:, lv % 2, :], h)
                q = groups(flat(q_a[:, 2 * p:2 * p + 2, :]), h)
                k = groups(flat(k_a[:]), h)
                nc.vector.tensor_tensor(flat(q_c[:, ring]).rearrange("p (n t) -> p n t", t=h), v[:, :, h:2 * h],
                                        q[:, :, h:2 * h], ALU.mult).then_inc(qk_done, 1)
                nc.vector.tensor_tensor(groups(k_c[:, ring, :], h)[:, :, 0:h], v[:, :, 0:h], k[:, :, 0:h],
                                        ALU.mult).then_inc(qk_done, 1)

            def tree_place(p, n):
                kind, m = TREE[n]
                if kind not in ("diag", "lv"):
                    return
                idx = TREE0 + NTREE * p + n
                bank = log_bank[idx % 2]
                dve.wait_ge(log_full, idx + 1)
                if kind == "diag":
                    if p:
                        dve.wait_ge(recur_done, m + 1)
                    nc.vector.tensor_tensor(att_blocks(m), bank[:].rearrange("p (t n) -> p t n", t=TB),
                                            id_sb[:].unsqueeze(1).broadcast_to([P, TB, P]),
                                            ALU.mult).then_inc(log_out[idx % 2], 1)
                    return
                h = LEVELS[m]
                if m == 0:
                    for d in range(2):
                        wait_log_out(dve, TREE0 + NTREE * p + d)
                else:
                    link_level(p, m)
                for a in range(2):
                    src = strided(bank[:, a * 256:a * 256 + 256], [[64, TB], [h, 64 // h], [1, h]])
                    mask = strided(masks_sb[:, m, :], [[0, TB], [h, 64 // h], [1, h]])
                    ins = nc.vector.copy_predicated(att_blocks(a, h), mask, src)
                ins.then_inc(log_out[idx % 2], 1)

            def link_level(p, lv):
                wait_log_out(dve, TREE0 + NTREE * p + TREE.index(("lv", lv - 1)))

            def gate_branch_a(h):
                dve.wait_ge(rms_done, h + 1)
                dve.wait_ge(z_done, 8)
                root = square[:, h % 2, :]
                nc.vector.tensor_tensor(root, out_bank[h % 2][:], root, ALU.mult).then_inc(out_out[h % 2], 1)
                dve.wait_ge(out_out[h % 2], 2 + h // 2 + 1)
                nc.vector.scalar_tensor_tensor(out=z_a[:, h, :], in0=root, scalar=g_a[:, h:h + 1], in1=z_a[:, h, :],
                                               op0=ALU.mult, op1=ALU.mult).then_inc(branch_a, 1)

            def split_branches(j):
                z = z_a if j < 2 else z_b
                dve.wait_ge(branch_a, HEADS_A)
                dve.wait_ge(o_hi_done, j + 1)
                nc.vector.tensor_tensor(flat(o_lo[:, 2 * j:2 * j + 2, :]), flat(z[:, 2 * j % 4:2 * j % 4 + 2, :]),
                                        flat(o_hi[:, 2 * j:2 * j + 2, :]).bitcast(F32),
                                        ALU.subtract).then_inc(o_lo_done, 1)

            def merge(m):
                u = UNITS.index(f"up{m // 2}")
                dve.wait_ge(part_done, 2 * u + m % 2 + 1)
                dve.wait_ge(gate_a_done, m + 1)
                dve.wait_ge(gate_b_done, m + 1)
                if m >= 2:
                    dve.wait_ge(m_hi_done, m - 1)
                    dve.wait_ge(m_lo_done, m - 1)
                fa, fb = 2 * m % 4, (2 * m + 1) % 4
                mx, gb = mix[:, m % 2, :], g_b[:, m % 2, :]
                nc.vector.tensor_tensor(mx, up_bank[fa][:], gate_a[:, m, :], ALU.mult).then_inc(up_out[fa], 1)
                nc.vector.tensor_tensor(gb, up_bank[fb][:], gb, ALU.mult).then_inc(up_out[fb], 1)
                dve.wait_ge(up_out[fa], m // 2 + 1)
                dve.wait_ge(up_out[fb], m // 2 + 1)
                nc.vector.tensor_tensor(mx, mx, gb, ALU.add).then_inc(mix_done, 1)
                dve.wait_ge(m_hi_done, m + 1)
                nc.vector.tensor_tensor(m_lo[:, m, :], mx, m_hi[:, m, :].bitcast(F32),
                                        ALU.subtract).then_inc(m_lo_done, 1)

            def residual(t, half):
                c = slice(half * 512, half * 512 + 512)
                dve.wait_ge(y_full, TB * half + t + 1)
                dve.wait_ge(res_in[t], 16)
                link(nc.vector.scalar_tensor_tensor(out=y_sb[:, t, c], in0=x_res[:, t, c], scalar=ALPHA,
                                                    in1=y_bank[half][t][:], op0=ALU.mult, op1=ALU.add))
                link(nc.vector.bn_stats(stats[:, t, half, :], y_sb[:, t, c]))

            def side(q):
                u, j = q // 4, q % 4
                if j == 0 and u >= 1:
                    leave_bank(u - 1, 1)
                if j == 2:
                    leave_bank(u, 0)
                for i in range(2 * (q - Q_DOTS), 2 * (q - Q_DOTS) + 2):
                    if 0 <= i < len(DOTS):
                        add_score(i)
                i = q - Q_ATT
                if 0 <= i - 1 < len(ITEMS):
                    move_probs(i - 1)
                if 0 <= i < len(ITEMS):
                    logits(i)
                    sum_reciprocal(i)
                if q in BLOCK_OUT:
                    block_out(BLOCK_OUT[q])
                part = part_out_at(q)
                if part:
                    name, tile = part
                    if name in ("zb", "za"):
                        silu(tile + 4 * (name == "za"))
                    if name in ("ga", "gb"):
                        gate_reciprocal(tile, name[1])
                for b, r in rounds.get(q, ()):
                    topk_round(b, r)
                for p in range(2):
                    at = q - Q_TREE[p]
                    if at == -4:
                        forget(p, 0)
                    if at == -3:
                        forget(p, 1)
                    if at == -1:
                        near_products(p)
                    if at == 0:
                        far_products(p)
                    if at == 0:
                        distance(p, 1)
                    if at == 2:
                        level_products(p, 1)
                        distance(p, 3)
                        level_products(p, 2)
                    if at == 3:
                        level_products(p, 3)
                        distance(p, 5)
                        level_products(p, 4)
                    if at == 4:
                        level_products(p, 5)
                        level_products(p, 6)
                for p, n in tree_at(q):
                    tree_place(p, n)
                for h in range(HEADS_A):
                    if q == Q_TREE[h // 2] + 8:
                        gate_branch_a(h)
                if UNITS[u] == "gb0":
                    split_branches(j)
                m = merged_at(q)
                if m is not None:
                    merge(m)

            for c in range(2):
                if c == 0:
                    dve.wait_ge(table_full, 1)
                nc.vector.tensor_copy(table[:, c * 320:c * 320 + 320],
                                      turn_bank[c][0:HEADS_B, 0:320]).then_inc(table_done, 1)
            for j in range(4):
                split_x(j)
            lower_bound()
            for q in range(4 * NMAIN):
                side(q)
            merge(KT - 1)
            for t in range(TB):
                residual(t, 0)
            for t in range(TB):
                residual(t, 1)
                nc.vector.bn_aggr(aggr[:, t, :], stats[:, t, :, :].rearrange("p a b -> p (a b)")).then_inc(y_aggr, 1)
                dve.wait_ge(ln_rstd, t + 1)
                y = y_sb[:, t, :]
                nc.vector.tensor_scalar(y, y, aggr[:, t, 0:1], rstd[:, t, 1:2], ALU.subtract,
                                        ALU.mult).then_inc(ln_norm, 1)
                if t == TB - 1:
                    dve.wait_ge(ln_norm, TB)
                    dve.wait_ge(ln_in, 32)
                    link(nc.vector.tensor_tensor(y, y, ln_gb[:, 0, :], ALU.mult))
                    nc.vector.tensor_tensor(y, y, ln_gb[:, 1, :], ALU.add).then_inc(y_dve, 1)

        @block.gpsimd
        def _(pool):
            nc.gpsimd.memset(ones_sb[:], 1.0 / P)
            nc.gpsimd.memset(eps[:, 0:1], RMS_EPS)
            nc.gpsimd.memset(eps[:, 1:2], LN_EPS).then_inc(pool_set, 1)

            def split_lo(u, j):
                pool.wait_ge(hi_done, 2 * u + j // 2 + 1)
                k = slice(2 * j, 2 * j + 2)
                nc.gpsimd.tensor_tensor(split_target(u, x_lo, w_lo)[:, k, :], raw(u)[:, k, :],
                                        split_target(u, x_hi, w_hi)[:, k, :].bitcast(F32),
                                        ALU.subtract).then_inc(lo_done, 1)

            def bias_and_penalty(i):
                b, h = ITEMS[i]
                if i == 0:
                    pool.wait_ge(t5_in, 16)
                    pool.wait_ge(consts_in, 16 * N_CONSTS)
                if h == 0 and b:
                    pool.wait_ge(pen_done, b)
                if i >= 2:
                    pool.wait_ge(exp_done, i - 1)
                n = (b + 1) * P
                nc.gpsimd.tensor_tensor(logit[:, i % 2, 0:n], t5[:, h, SEQ - n:SEQ], pen[b][:] if b else causal_sb[:],
                                        ALU.add).then_inc(logit_pre, 1)

            def normalise(i):
                b, h = ITEMS[i]
                pool.wait_ge(rcp_done, i + 1)
                p = prob[:, i % 2, 0:(b + 1) * P]
                nc.gpsimd.tensor_scalar(p, p, prob_rcp[:, i % 2:i % 2 + 1], None, ALU.mult).then_inc(norm_done, 1)

            def plus_one(q):
                part = part_out_at(q)
                if part is None:
                    return
                name, tile = part
                if name in ("zb", "za"):
                    n = tile + 4 * (name == "za")
                    pool.wait_ge(ez_done, n + 1)
                    t, done = scratch[:, n % 2, :], dz_done
                elif name == "ga":
                    wait_proj_out(pool, f"ga{tile // 2}", tile % 2)
                    t, done = gate_a[:, tile, :], gate_a_plus1
                elif name == "gb":
                    wait_proj_out(pool, f"gb{tile // 2}", tile % 2)
                    t, done = g_b[:, tile % 2, :], gate_b_plus1
                else:
                    return
                nc.gpsimd.tensor_scalar(t, t, 1.0, None, ALU.add).then_inc(done, 1)

            def make_reset():
                pool.wait_ge(pv_done, len(ITEMS))
                nc.gpsimd.memset(far_f[:], 1.0)
                nc.gpsimd.memset(reset[:], 1.0).then_inc(reset_set, 1)
                pool.wait_ge(reset_set, 1)
                nc.gpsimd.memset(reset[:, 0:SEQ:SEG], 0.0).then_inc(reset_set, 1)

            def finish_k(p):
                pool.wait_ge(f_act, 6 * p + 6)
                pool.wait_ge(lb_step, 5)
                for a in range(2):
                    nc.gpsimd.tensor_scalar(k_a[:, a, :], k_a[:, a, :], lb[:, 6, 2 * p + a:2 * p + a + 1], None,
                                            ALU.mult).then_inc(k_done, 1)

            def end_distance(p):
                pool.wait_ge(cum_done, 2 * (p + 1))
                c = flat(cum[:, 2 * p:2 * p + 2, :]).rearrange("p (s t) -> p s t", t=SEG)
                nc.gpsimd.tensor_tensor(dec[:, 0, :].rearrange("p (s t) -> p s t", t=SEG),
                                        c[:, :, SEG - 1:SEG].broadcast_to([P, 2 * NSEG, SEG]), c,
                                        ALU.subtract).then_inc(dist_pool, 1)

            def far_factors(p):
                pool.wait_ge(seg_decay, p + 1)
                if p:
                    pool.wait_ge(far_done, 6)
                n = 7 * p
                g = far_g
                for dst, src in ((far_f[:, 0, :, 0:4:2], g[:, :, 1:8:4]), (far_f[:, 1, :, 1:4:2], g[:, :, 2:8:4]),
                                 (far_f[:, 2, :, 2:3], g[:, :, 3:4]), (far_f[:, 3, :, 1:2], g[:, :, 4:5])):
                    n += 1
                    nc.gpsimd.tensor_copy(dst, src).then_inc(far_f_step, 1)
                for dst, x, y in ((far_f[:, 2, :, 1:2], far_f[:, 2, :, 2:3], g[:, :, 2:3]),
                                  (far_f[:, 3, :, 2:3], far_f[:, 3, :, 1:2], g[:, :, 5:6]),
                                  (far_f[:, 2, :, 0:1], far_f[:, 2, :, 1:2], g[:, :, 1:2])):
                    pool.wait_ge(far_f_step, n)
                    n += 1
                    nc.gpsimd.tensor_tensor(dst, x, y, ALU.mult).then_inc(far_f_step, 1)
                pool.wait_ge(far_f_step, n)
                nc.gpsimd.tensor_tensor(far_f[:, 3, :, 3:4], far_f[:, 3, :, 2:3], g[:, :, 6:7],
                                        ALU.mult).then_inc(far_f_done, 1)

            def distance(p, lv):
                if lv == 2:
                    pool.wait_ge(rl_done, 2 * p + 2)
                else:
                    pool.wait_ge(qk_done, 2 * (6 * p + lv - 2))
                level_distance(nc.gpsimd, p, lv).then_inc(dist_pool, 1)

            def side(q):
                j = q % 4
                u = q // 4 + 1
                if u >= 2:
                    for piece in ((0,), (1, 2), (3,), ())[j]:
                        split_lo(u, piece)
                if q == Q_ATT - 1:
                    bias_and_penalty(0)
                    bias_and_penalty(1)
                i = q - Q_ATT
                if 0 <= i < len(ITEMS):
                    normalise(i)
                    if i + 2 < len(ITEMS):
                        bias_and_penalty(i + 2)
                plus_one(q)
                if q == Q_TREE[0] - 5:
                    make_reset()
                for p in range(2):
                    at = q - Q_TREE[p]
                    if at == -2:
                        end_distance(p)
                        finish_k(p)
                        far_factors(p)
                    if at == 1:
                        distance(p, 2)
                    if at == 2:
                        distance(p, 4)
                    if at == 3:
                        distance(p, 6)

            for u in (0, 1):
                for j in range(4):
                    split_lo(u, j)
            for q in range(4 * NMAIN):
                side(q)
            for u in range(NMAIN + 1, NU):
                for j in range(4):
                    split_lo(u, j)
            pool.wait_ge(ln_in, 32)
            for t in range(TB - 1):
                y = y_sb[:, t, :]
                pool.wait_ge(ln_norm, t + 1)
                nc.gpsimd.tensor_tensor(y, y, ln_gb[:, 0, :], ALU.mult).then_inc(ln_scaled, 1)
                pool.wait_ge(ln_scaled, t + 1)
                nc.gpsimd.tensor_tensor(y, y, ln_gb[:, 1, :], ALU.add).then_inc(y_pool, 1)


def t5_one_hot():
    d = np.arange(SEQ - 1, -1, -1)
    exact = BUCKETS // 2
    large = exact + (np.log(np.maximum(d, 1).astype(np.float32) / np.float32(exact))
                     / np.float32(np.log(MAX_DISTANCE / exact)) * (BUCKETS - exact)).astype(np.int32)
    bucket = np.where(d < exact, d, np.minimum(large, BUCKETS - 1))
    hot = np.zeros((BUCKETS, T5W), np.float32)
    hot[bucket, np.arange(SEQ)] = 1.0
    return hot


def tree_level_masks():
    key, n = np.arange(P)[:, None], np.arange(64)[None, :]
    return np.stack([(key // (2 * h) == n // h) & (key % (2 * h) < h) for h in LEVELS], 1).astype(np.int32)


def kernel(**inputs):
    import concourse.bacc as bacc
    from concourse.bass_utils import run_bass_kernel_spmd

    a = {k: np.asarray(v) for k, v in inputs.items()}
    x, w_in, b_in = a["x"][0], a["w_in"][0], a["b_in"][0]

    def unit(rows_by_tile):
        return rows_by_tile.reshape(KT, P, -1).transpose(1, 0, 2).reshape(P, -1)

    units, b_cols = [], np.zeros((P, 2 * NMAIN), np.float32)
    for u, name in enumerate(UNITS):
        kind = name[:2]
        if name == "kiwi":
            ki = COLUMNS["ki"]
            w_kiwi = unit(np.concatenate([w_in[:, ki:ki + 64], w_in[:, ki:ki + 64 + HEADS_I]], 1))
            b_cols[:, 2 * u] = np.concatenate([b_in[ki:ki + 64]] * 2)
        elif kind == "up":
            c = slice(int(name[2]) * UW, int(name[2]) * UW + UW)
            units.append(unit(np.concatenate([a["w_up_a"][0][:, c], a["w_up_b"][0][:, c]], 0)))
        else:
            c = COLUMNS[kind] + int(name[2]) * UW
            units.append(unit(w_in[:, c:c + UW]))
            b_cols[:, 2 * u], b_cols[:, 2 * u + 1] = b_in[c:c + P], b_in[c + P:c + UW]
    for n in (0, 1, 3, 2):
        units.append(unit(a["w_out"][0][:, n * UW:n * UW + UW]))
    arrays = {
        "x_t": x.reshape(SEQ, KT, P).transpose(2, 1, 0), "x_tok": x.reshape(TB, P, D_MODEL),
        "w_units": np.stack(units), "w_kiwi": w_kiwi, "b_cols": b_cols,
        "b_ia": b_in[COLUMNS["ia"]:COLUMNS["ia"] + D_A], "b_vb": b_in[COLUMNS["vb"]:COLUMNS["vb"] + D_B],
        "b_wi": b_in[COLUMNS["wi"]:COLUMNS["wi"] + HEADS_I],
        "lb_cols": a["lb_logits"][0].reshape(HEADS_A, P).T, "g_cols": a["norm_a_g"][0].reshape(HEADS_A, P).T,
        "rel_bias": a["rel_bias"], "ln_g": a["ln_g"][0], "ln_b": a["ln_b"][0],
        "one_hot": t5_one_hot(), "ident": np.eye(P, dtype=np.float32),
        "causal": np.where(np.arange(P)[None, :] > np.arange(P)[:, None], np.float32(NEG), np.float32(0)),
        "tree_masks": tree_level_masks(),
    }
    arrays = {k: np.ascontiguousarray(v) for k, v in arrays.items()}
    nc = bacc.Bacc("TRN2", target_bir_lowering=False, num_devices=1)
    args = [nc.dram_tensor(f"in_{k}", v.shape, mybir.dt.from_np(v.dtype), kind="ExternalInput").ap()
            for k, v in arrays.items()]
    out = nc.dram_tensor("out_0", (TB, P, D_MODEL), F32, kind="ExternalOutput").ap()
    hybrid_kernel(nc, *args, out)
    r = run_bass_kernel_spmd(nc, [{f"in_{k}": v for k, v in arrays.items()}], core_ids=[0])
    return r.results[0]["out_0"].reshape(1, SEQ, D_MODEL)
```

```python
from contextlib import ExitStack

import numpy as np
import concourse.bass as bass
from concourse import mybir

F32 = mybir.dt.float32
F32R = mybir.dt.float32r
I32 = mybir.dt.int32
ALU = mybir.AluOpType
ACT = mybir.ActivationFunctionType

P = 128
D_MODEL, SEQ, DEPTH = 1024, 512, 1
D_A = D_B = 512
HEADS_A, HEADS_B, HEADS_I = 4, 8, 8
TOPK = min(256, SEQ // 4)
BUCKETS, MAX_DISTANCE = 32, 128
ALPHA = (2 * DEPTH) ** 0.25
LN_EPS, RMS_EPS = 1e-5, 1e-6
KT = D_MODEL // P
TB = SEQ // P
UW = 256
QSCALE = 64 ** -0.5
WSCALE = HEADS_I ** -0.5
NEG = -1e30
TAKEN = -3e38
F_FLOOR = -40.0
SEG = 64
NSEG = SEQ // SEG
LEVELS = (64, 32, 16, 8, 4, 2, 1)

UNITS = ["qi0", "qi1", "kiwi", "zb0", "zb1", "za0", "za1", "qb0", "kb0", "vb0", "qb1", "kb1", "vb1",
         "ia0", "ia1", "fa0", "qa0", "fa1", "qa1", "ga0", "ga1", "ga2", "ga3",
         "gb0", "gb1", "up0", "gb2", "up1", "gb3", "up2", "up3"]
NMAIN = len(UNITS)
NOUT = 4
NU = NMAIN + NOUT
COLUMNS = {"qa": 0, "fa": 512, "ia": 1024, "za": 1536, "qb": 2048, "kb": 2560, "vb": 3072, "zb": 3584,
           "qi": 4096, "ki": 4608, "wi": 4672, "ga": 4680, "gb": 5704}
WKI = 2 * 64 + HEADS_I
NPROJ = [sum(not n.startswith("up") for n in UNITS[:u]) for u in range(NMAIN + 1)]

DOTS = [(b, h) for b in range(1, TB) for h in range(HEADS_I)]
ITEMS = [(b, 4 * g + h) for g in range(2) for b in range(TB) for h in range(4)]
GROUPS = [(g, b) for g in range(2) for b in range(TB)]
QK0 = len(DOTS)
TREE0 = QK0 + len(ITEMS)
N_CONSTS = 9
T5W = SEQ + P
TREE = [("diag", 0), ("diag", 1), ("lv", 0), ("128", 0), ("256", 0), ("256", 1),
        ("lv", 1), ("lv", 2), ("lv", 3), ("lv", 4), ("lv", 5), ("lv", 6)]
NTREE = len(TREE)

Q_DOTS = 4 * 3
Q_ITEM = [39 + i if i < 16 else 55 + 2 * (i - 16) // 3 for i in range(len(ITEMS))]
Q_GROUP = [Q_ITEM[4 * n + 3] + 3 for n in range(len(GROUPS))]
Q_TREE = (73, 81)
Q_MERGE = 4 * UNITS.index("gb0")
TURNS = sorted([(q + 1, 0, i) for i, q in enumerate(Q_ITEM)] + [(q, 1, n) for n, q in enumerate(Q_GROUP)])
TURNS = [t[1:] for t in TURNS]
ROUNDS = TOPK // 8


def topk_rounds():
    plan = {}
    for b, first, per in ((1, 17, 2), (2, 25, 2), (3, 33, 1.5)):
        for r in range(ROUNDS):
            plan.setdefault(first + int(r / per), []).append((b, r))
    return plan


def lvl_item(pair, lv):
    return TREE0 + NTREE * pair + TREE.index(("lv", lv))


def hybrid_kernel(nc, x_t, x_tok, w_units, w_kiwi, b_cols, b_ia, b_vb, b_wi, lb_cols, g_cols, rel_bias,
                  ln_g, ln_b, one_hot, ident, causal, tree_masks, out):
    with ExitStack() as ctx:
        def sb(name, shape, dt=F32, stack=ctx):
            return stack.enter_context(nc.sbuf_tensor(name, shape, dt))

        def sem(name):
            return ctx.enter_context(nc.semaphore(name))

        x_hi, x_lo = (sb(n, [P, KT, SEQ], F32R) for n in ("x_hi", "x_lo"))
        w_raw = sb("w_raw", [P, 2, KT * UW])
        w_hi, w_lo = (sb(n, [P, 2, KT, UW], F32R) for n in ("w_hi", "w_lo"))
        id_sb = sb("id_sb", [P, P])
        causal_sb = sb("causal_sb", [P, P])
        ones_sb = sb("ones_sb", [P, P])
        masks_sb = sb("masks_sb", [P, len(LEVELS), 64], I32)
        bias = sb("bias", [P, 2 * NMAIN])
        bias_q = sb("bias_q", [P, 2 * NMAIN])
        bias_ia, bias_vb = sb("bias_ia", [P, D_A]), sb("bias_vb", [P, D_B])
        bias_wi = sb("bias_wi", [P, HEADS_I])
        w_idx = sb("w_idx", [P, TB, HEADS_I])
        lb = sb("lb", [P, 7, HEADS_A])
        g_a = sb("g_a", [P, HEADS_A])
        eps = sb("eps", [P, 2])
        best8 = sb("best8", [P, 8])
        nmax = sb("nmax", [P, 2])
        prob_sum, prob_rcp = sb("prob_sum", [P, 2, 4]), sb("prob_rcp", [P, 2, 4])
        stats, aggr, rstd = sb("stats", [P, TB, 2, 6]), sb("aggr", [P, TB, 2]), sb("rstd", [P, TB, 2])
        z_a = sb("z_a", [P, HEADS_A, SEQ])
        z_b = sb("z_b", [P, HEADS_B // 2, SEQ])
        U1 = 78 * 1024 + 512

        with ExitStack() as s:
            q_idx, k_idx = sb("q_idx", [P, 4, SEQ], stack=s), sb("k_idx", [P, SEQ], stack=s)
            score = {b: sb(f"score{b}", [P, (b + 1) * P], stack=s) for b in range(1, TB)}
            relus = sb("relus", [P, 2, SEQ], stack=s)
            q_b, k_b = sb("q_b", [P, 4, SEQ], stack=s), sb("k_b", [P, 4, SEQ], stack=s)
            v_b = sb("v_b", [P, TB, D_B], stack=s)
            t5 = sb("t5", [P, HEADS_B, SEQ], stack=s)
            pen = {b: sb(f"pen{b}", [P, (b + 1) * P], stack=s) for b in range(1, TB)}
            logit = sb("logit", [P, 2, SEQ], stack=s)
            prob = sb("prob", [P, 2, SEQ], stack=s)
            prob_t = sb("prob_t", [P, 2, SEQ], stack=s)
            o_tok = sb("o_tok", [P, 2, 4 * 64], stack=s)
        with ExitStack() as s:
            cum = sb("cum", [P, HEADS_A, SEQ], stack=s)
            q_a = sb("q_a", [P, HEADS_A, SEQ], stack=s)
            k_a = sb("k_a", [P, 2, SEQ], stack=s)
            q_r, k_l = sb("q_r", [P, 2, SEQ], stack=s), sb("k_l", [P, 2, SEQ], stack=s)
            dec = sb("dec", [P, 2, 2 * SEQ], stack=s)
            q_c = sb("q_c", [P, 2, 2, SEQ // 2], stack=s)
            k_c = sb("k_c", [P, 2, 2 * SEQ], stack=s)
            far = sb("far", [P, 4, 2, SEQ // 2], stack=s)
            far_f = sb("far_f", [P, 4, 2, 4], stack=s)
            att = sb("att", [P, 2, TB, SEQ], stack=s)
            reset = sb("reset", [P, SEQ], stack=s)
            far_g = sb("far_g", [P, 2, NSEG], stack=s)
            square = sb("square", [P, 2, SEQ], stack=s)
        with ExitStack() as s:
            o_hi, o_lo = (sb(n, [P, 8, SEQ], F32R, s) for n in ("o_hi", "o_lo"))
            m_hi, m_lo = (sb(n, [P, KT, SEQ], F32R, s) for n in ("m_hi", "m_lo"))
            g_b = sb("g_b", [P, 4, SEQ], stack=s)
            mix = sb("mix", [P, 2, SEQ], stack=s)
        with ExitStack() as s:
            y_sb = sb("y_sb", [P, TB, D_MODEL], stack=s)
        sb("over", [P, U1 // 4])
        with ExitStack() as s:
            v_a = sb("v_a", [P, TB, D_A], stack=s)
            gate_a = sb("gate_a", [P, KT, SEQ], stack=s)
        with ExitStack() as s:
            hot_sb, table = sb("hot_sb", [BUCKETS, T5W], stack=s), sb("table", [HEADS_B, T5W], stack=s)
            rel_sb = sb("rel_sb", [BUCKETS, HEADS_B], stack=s)
            sb("under", [P, 2048 - 2 * T5W - HEADS_B], stack=s)
            x_raw = sb("x_raw", [P, KT, SEQ], stack=s)
        with ExitStack() as s:
            ln_gb = sb("ln_gb", [P, 2, D_MODEL], stack=s)
            x_res = sb("x_res", [P, TB, D_MODEL], stack=s)

        ps = [ctx.enter_context(nc.psum_tensor(f"bank{i}", [P, 512], F32)) for i in range(8)]
        proj_bank, log_bank, turn_bank, out_bank = ps[0:2], ps[2:4], ps[4:6], ps[6:8]
        up_bank = log_bank + turn_bank
        y_bank = [out_bank + proj_bank, log_bank + turn_bank]
        t5_rep = nc.dram_tensor("t5_rep", [P, HEADS_B, T5W], F32).ap()


        x_in = [sem(f"x_in{j}") for j in range(4)]
        w0_in = [sem(f"w0_in{j}") for j in range(4)]
        w_in = [sem(f"w_in{j}") for j in range(2)]
        consts_in, table_in, rep_out, t5_in = sem("consts_in"), sem("table_in"), sem("rep_out"), sem("t5_in")
        ln_in = sem("ln_in")
        res_in = [sem(f"res_in{t}") for t in range(TB)]
        y_out = sem("y_out")
        table_full, table_done = sem("table_full"), sem("table_done")
        pool_set, bias_q_done = sem("pool_set"), sem("bias_q_done")
        lb_step, lb_exp, dve_step = sem("lb_step"), sem("lb_exp"), sem("dve_step")
        x_hi_done, x_lo_done = sem("x_hi_done"), sem("x_lo_done")
        hi_done, lo_done = sem("hi_done"), sem("lo_done")
        part_done = sem("part_done")
        proj_out = [sem(f"proj_out{j}") for j in range(2)]
        log_full, log_out = sem("log_full"), [sem(f"log_out{j}") for j in range(2)]
        turn_full, turn_out = sem("turn_full"), [sem(f"turn_out{j}") for j in range(2)]
        pv_done, recur_done = sem("pv_done"), sem("recur_done")
        out_out = [sem(f"out_out{j}") for j in range(2)]
        up_out = [sem(f"up_out{j}") for j in range(4)]
        w_idx_done, relu_used, pen_done, topk_step = sem("w_idx_done"), sem("relu_used"), sem("pen_done"), sem("topk_step")
        logit_pre, exp_done, rcp_done = sem("logit_pre"), sem("exp_done"), sem("rcp_done")
        z_sig, gate_a_done = sem("z_sig"), sem("gate_a_done")
        f_dve, f_act, cum_done, k_raw, k_done = (sem(n) for n in ("forget_dve", "forget_act", "cum_done", "k_raw", "k_done"))
        seg_decay, rl_done, near_done = sem("seg_decay"), sem("rl_done"), sem("near_done")
        reset_set, far_f_step, far_f_done, far_done = (sem(n) for n in ("reset_set", "far_f_step", "far_f_done", "far_done"))
        dist_pool, dist_dve = sem("dist_pool"), sem("dist_dve")
        fac_done, qk_done = sem("fac_done"), sem("qk_done")
        sq_done, ln_ms, rms_done, branch_a = (sem(n) for n in ("sq_done", "ln_ms", "rms_done", "branch_a"))
        o_hi_done, o_lo_done = sem("o_hi_done"), sem("o_lo_done")
        mix_part, mix_done, m_hi_done, m_lo_done = (sem(n) for n in ("mix_part", "mix_done", "m_hi_done", "m_lo_done"))
        y_full, y_aggr = sem("y_full"), sem("y_aggr")
        ln_log, ln_rstd, y_done = sem("ln_log"), sem("ln_rstd"), sem("y_done")

        rounds = topk_rounds()

        def unit_width(u):
            return WKI if u < NMAIN and UNITS[u] == "kiwi" else UW

        def raw(u):
            w = unit_width(u)
            return w_raw[:, u % 2, 0:KT * w].rearrange("p (k n) -> p k n", k=KT)

        def split_target(u, over_x, ring):
            if NMAIN <= u < NMAIN + 2:
                c = (u - NMAIN) * UW
                return over_x[:, :, c:c + UW]
            return ring[:, u % 2, :, 0:unit_width(u)]

        def wait_split_target(eng, u):
            gb3, up2, up3 = (UNITS.index(n) for n in ("gb3", "up2", "up3"))
            last = {NMAIN: gb3, NMAIN + 1: gb3, NMAIN + 2: up2, NMAIN + 3: up3}.get(u, u - 2)
            if last >= 0:
                eng.wait_ge(part_done, 2 * last + 2)

        def wait_proj_out(eng, name, i):
            eng.wait_ge(proj_out[i], NPROJ[UNITS.index(name)] + 1)

        def wait_log_out(eng, idx):
            eng.wait_ge(log_out[idx % 2], idx // 2 + 1)

        def wait_turn_out(eng, idx):
            eng.wait_ge(turn_out[idx % 2], idx // 2 + 1)

        def item_turn(i):
            return TURNS.index((0, i))

        def group_turn(n):
            return TURNS.index((1, n))

        def wait_tree_out(eng, p):
            wait_log_out(eng, TREE0 + NTREE * (p + 1) - 2)
            wait_log_out(eng, TREE0 + NTREE * (p + 1) - 1)

        def wait_lvl_multiplied(eng, p, lv):
            eng.wait_ge(log_full, TREE0 + NTREE * p + TREE.index(("lv", lv)) + 1)

        def items_at(q):
            return [i for i in range(len(ITEMS)) if Q_ITEM[i] == q]

        def groups_at(q):
            return [n for n in range(len(GROUPS)) if Q_GROUP[n] == q]

        def rows(h):
            return slice(64 * (h % 2), 64 * (h % 2) + 64)

        def queries(b):
            return slice(b * P, b * P + P)

        def tree_at(q):
            return [(p, n) for p in range(2) for n in range(NTREE) if Q_TREE[p] + n // 2 == q]

        def flat(ap):
            return ap.rearrange("p a t -> p (a t)")

        def groups(tile, h):
            return tile.rearrange("p (n w) -> p n w", w=2 * h)

        def strided(base, dims):
            return bass.AP(base.tensor, base.offset, [list(base.ap[0])] + dims)

        def att_blocks(a, h=None):
            step = SEQ + P
            if h is None:
                return strided(att[:, a, 0, 0:P], [[step, TB], [1, P]])
            return strided(att[:, a, 0, h:P], [[step, TB], [2 * h, 64 // h], [1, h]])

        def z_part(n):
            return (z_b if n < 4 else z_a)[:, n % 4, :]

        def wait_dist(eng, p, lv):
            if lv % 2:
                eng.wait_ge(dist_dve, 3 * p + lv // 2 + 1)
            else:
                eng.wait_ge(dist_pool, 4 * p + lv // 2 + 1)

        def part_out_at(q):
            u, i = (q // 4 - 1, 1) if q % 4 == 0 else (q // 4, 0)
            if u < 0 or q % 2 or not UNITS[u][2:].isdigit():
                return None
            return UNITS[u][:2], 2 * int(UNITS[u][2]) + i

        def merged_at(q):
            part = part_out_at(q)
            return part[1] if part and part[0] == "up" else None

        def level_distance(engine, p, lv):
            h = LEVELS[lv]
            c = groups(flat(cum[:, 2 * p:2 * p + 2, :]), h)
            return engine.tensor_tensor(groups(dec[:, lv % 2, :], h), c,
                                        c[:, :, h - 1:h].broadcast_to([P, 2 * SEQ // (2 * h), 2 * h]), ALU.subtract)

        block = ctx.enter_context(nc.Block())

        @block.sync
        def _(sp):
            for j in range(4):
                k = slice(2 * j, 2 * j + 2)
                sp.dma_start(raw(0)[:, k, :], w_units[0].rearrange("p (k n) -> p k n", k=KT)[:, k, :]).then_inc(w0_in[j], 16)
                sp.dma_start(x_raw[:, k, :], x_t[:, k, :]).then_inc(x_in[j], 16)
            for u in range(1, NU):
                if u >= 2:
                    sp.wait_ge(lo_done, 4 * (u - 1))
                if u < NMAIN and UNITS[u] == "kiwi":
                    unit = w_kiwi
                else:
                    unit = w_units[u - (u > UNITS.index("kiwi"))]
                sp.dma_start(w_raw[:, u % 2, 0:KT * unit_width(u)], unit).then_inc(w_in[u % 2], 16)
                if u == 3:
                    sp.wait_ge(table_done, 2)
                    sp.dma_start(t5_rep.rearrange("p h d -> h p d"),
                                 table[:].unsqueeze(1).broadcast_to([HEADS_B, P, T5W])).then_inc(rep_out, 16)
                if u == 5:
                    sp.wait_ge(rep_out, 16)
                    skewed = bass.AP(t5_rep.tensor, t5_rep.offset + P - 1,
                                     [[HEADS_B * T5W - 1, P], [T5W, HEADS_B], [1, SEQ]])
                    sp.dma_start(t5[:], skewed).then_inc(t5_in, 16)
            sp.wait_ge(recur_done, HEADS_A)
            sp.dma_start(ln_gb[:, 0, :], ln_g.partition_broadcast(P)).then_inc(ln_in, 16)
            sp.dma_start(ln_gb[:, 1, :], ln_b.partition_broadcast(P)).then_inc(ln_in, 16)
            sp.wait_ge(mix_done, KT)
            for t in range(TB):
                sp.dma_start(x_res[:, t, :], x_tok[t]).then_inc(res_in[t], 16)
            for t in range(TB):
                for half in range(2):
                    c = slice(half * 512, half * 512 + 512)
                    sp.wait_ge(y_done, 2 * t + half + 1)
                    sp.dma_start(out[t][:, c], y_sb[:, t, c]).then_inc(y_out, 16)
            sp.wait_ge(y_out, 16 * 2 * TB)

        @block.tensor
        def _(pe):
            def split_product(dst, a_hi, a_lo, b_hi, b_lo, first, last):
                nc.tensor.matmul(dst, a_hi, b_hi, start=first, stop=False)
                nc.tensor.matmul(dst, a_hi, b_lo, start=False, stop=False)
                return nc.tensor.matmul(dst, a_lo, b_hi, start=False, stop=last)

            def wait_piece(u, k):
                if k % 2 == 0:
                    pe.wait_ge(lo_done, 4 * u + k // 2 + 1)
                    if u == 0:
                        pe.wait_ge(x_lo_done, k // 2 + 1)

            def wait_bank(u, i):
                if NPROJ[u]:
                    pe.wait_ge(proj_out[i], NPROJ[u])

            def quarter_f(u, i, j):
                if j == 0:
                    wait_bank(u, i)
                c = slice(i * P, i * P + P)
                for k in range(4 * j, 4 * j + 4):
                    if i == 0:
                        wait_piece(u, k)
                    mm = split_product(proj_bank[i][:], w_hi[:, u % 2, k, c], w_lo[:, u % 2, k, c],
                                       x_hi[:, k, :], x_lo[:, k, :], k == 0, k == KT - 1)
                if j == 1:
                    mm.then_inc(part_done, 1)

            def quarter_t(u, i, j):
                if j == 0:
                    wait_bank(u, i)
                tk = queries(2 * i + j)
                for k in range(KT):
                    if i == 0 and j == 0:
                        wait_piece(u, k)
                    mm = split_product(proj_bank[i][:, j * UW:(j + 1) * UW], x_hi[:, k, tk], x_lo[:, k, tk],
                                       w_hi[:, u % 2, k, :], w_lo[:, u % 2, k, :], k == 0, k == KT - 1)
                if j == 1:
                    mm.then_inc(part_done, 1)

            def quarter_wi(u, j):
                if j == 0:
                    wait_bank(u, 1)
                c = slice(2 * 64, WKI)
                for t in (2 * j, 2 * j + 1):
                    for k in range(KT):
                        mm = split_product(proj_bank[1][:, t * HEADS_I:(t + 1) * HEADS_I],
                                           x_hi[:, k, queries(t)], x_lo[:, k, queries(t)],
                                           w_hi[:, u % 2, k, c], w_lo[:, u % 2, k, c], k == 0, k == KT - 1)
                if j == 1:
                    mm.then_inc(part_done, 1)

            def quarter_up(u, i, j):
                fill = 2 * (2 * int(UNITS[u][2]) + i) + j
                if fill < 2:
                    wait_log_out(pe, TREE0 + 2 * NTREE - 2 + fill)
                    pe.wait_ge(o_hi_done, 2 * (j + 1))
                    pe.wait_ge(o_lo_done, 2 * (j + 1))
                elif fill < 4:
                    wait_turn_out(pe, len(TURNS) + HEADS_A - 4 + fill)
                else:
                    pe.wait_ge(up_out[fill % 4], fill // 4)
                c = slice(i * P, i * P + P)
                for k in range(4 * j, 4 * j + 4):
                    if i == 0:
                        wait_piece(u, k)
                    mm = split_product(up_bank[fill % 4][:], w_hi[:, u % 2, k, c], w_lo[:, u % 2, k, c],
                                       o_hi[:, k, :], o_lo[:, k, :], k % 4 == 0, k % 4 == 3)
                if j == 1:
                    mm.then_inc(part_done, 1)

            def log_slot(idx):
                if idx >= 2:
                    wait_log_out(pe, idx - 2)
                return log_bank[idx % 2]

            def dots(i):
                b, h = DOTS[i]
                dst = log_slot(i)
                if i == 0:
                    for name in ("qi0", "qi1"):
                        wait_proj_out(pe, name, 0)
                        wait_proj_out(pe, name, 1)
                    wait_proj_out(pe, "kiwi", 0)
                n = (b + 1) * P
                nc.tensor.matmul(dst[:, 0:n], q_idx[rows(h), h // 2, queries(b)], k_idx[rows(h), 0:n],
                                 start=True, stop=True).then_inc(log_full, 1)

            def scores(i):
                b, h = ITEMS[i]
                dst = log_slot(QK0 + i)
                if b == 0 and h % 2 == 0:
                    wait_proj_out(pe, f"qb{h // 4}", h // 2 % 2)
                    wait_proj_out(pe, f"kb{h // 4}", h // 2 % 2)
                n = (b + 1) * P
                nc.tensor.matmul(dst[:, 0:n], q_b[rows(h), h // 2, queries(b)], k_b[rows(h), h // 2, 0:n],
                                 start=True, stop=True).then_inc(log_full, 1)

            def turn_probs(i):
                b, h = ITEMS[i]
                n = item_turn(i)
                pe.wait_ge(exp_done, i + 1)
                if n >= 2:
                    wait_turn_out(pe, n - 2)
                for c in range(b + 1):
                    mm = nc.tensor.transpose(turn_bank[n % 2][:, queries(c)], prob[:, i % 2, queries(c)], id_sb[:])
                mm.then_inc(turn_full, 1)

            def attend(i):
                b, h = ITEMS[i]
                n = i // 4
                wait_turn_out(pe, item_turn(i))
                if b == 0 and h % 4 == 0:
                    wait_proj_out(pe, f"vb{h // 4}", 0)
                    wait_proj_out(pe, f"vb{h // 4}", 1)
                if h % 4 == 0 and n >= 2:
                    pe.wait_ge(out_out[n % 2], n // 2)
                for c in range(b + 1):
                    mm = nc.tensor.matmul(out_bank[n % 2][:, h % 4 * 64:h % 4 * 64 + 64], prob_t[:, i % 2, queries(c)],
                                          v_b[:, c, h * 64:h * 64 + 64], start=(c == 0), stop=(c == b),
                                          skip_group_check=True)
                mm.then_inc(pv_done, 1)

            def turn_group(n):
                m = group_turn(n)
                pe.wait_ge(out_out[n % 2], n // 2 + 1)
                wait_turn_out(pe, m - 2)
                for c in range(2):
                    mm = nc.tensor.transpose(turn_bank[m % 2][:, queries(c)], o_tok[:, n % 2, queries(c)], id_sb[:])
                mm.then_inc(turn_full, 1)

            def tree(p, n):
                kind, m = TREE[n]
                idx = TREE0 + NTREE * p + n
                dst = log_slot(idx)
                if kind == "diag":
                    pe.wait_ge(k_done, 2 * (p + 1))
                    for t in range(TB):
                        mm = nc.tensor.matmul(dst[:, queries(t)], k_a[:, m, queries(t)],
                                              q_a[:, 2 * p + m, queries(t)], start=True, stop=True)
                elif kind == "lv":
                    if m == 0:
                        pe.wait_ge(near_done, 2 * p + 2)
                    else:
                        pe.wait_ge(qk_done, 2 * (6 * p + m))
                    for a in range(2):
                        for t in range(TB):
                            c = (a * TB + t) * 64
                            if m == 0:
                                key, query = k_l[:, a, queries(t)], q_r[:, a, t * P + 64:t * P + P]
                            else:
                                ring = (m - 1) % 2
                                key = k_c[:, ring, a * SEQ + t * P:a * SEQ + t * P + P]
                                query = q_c[:, ring, a, t * 64:t * 64 + 64]
                            mm = nc.tensor.matmul(dst[:, c:c + 64], key, query, start=True, stop=True)
                elif kind == "128":
                    pe.wait_ge(far_done, 6 * p + 4)
                    for a in range(2):
                        for t in range(2):
                            mm = nc.tensor.matmul(dst[:, queries(2 * a + t)], far[:, 0, a, queries(t)],
                                                  far[:, 1, a, queries(t)], start=True, stop=True)
                else:
                    pe.wait_ge(far_done, 6 * p + 6)
                    for t in range(2):
                        mm = nc.tensor.matmul(dst[:, t * 256:t * 256 + 256], far[:, 2, m, queries(t)],
                                              far[:, 3, m, :], start=True, stop=True)
                mm.then_inc(log_full, 1)

            def recur(h):
                bank = out_bank[h % 2]
                pe.wait_ge(out_out[h % 2], len(GROUPS) // 2 + h // 2)
                wait_tree_out(pe, h // 2)
                if h == 0:
                    wait_proj_out(pe, "ia1", 0)
                    wait_proj_out(pe, "ia1", 1)
                for s in range(TB):
                    mm = nc.tensor.matmul(bank[:, s * P:SEQ], v_a[:, s, queries(h)], att[:, h % 2, s, s * P:SEQ],
                                          start=(s == 0), stop=(s == TB - 1), skip_group_check=True)
                mm.then_inc(recur_done, 1)

            def mean_square(h):
                i = len(TURNS) + h
                pe.wait_ge(sq_done, h + 1)
                wait_turn_out(pe, i - 2)
                nc.tensor.matmul(turn_bank[i % 2][:], ones_sb[:], square[:, h % 2, :], start=True,
                                 stop=True).then_inc(turn_full, 1)

            def side(q):
                for i in range(2 * (q - Q_DOTS), 2 * (q - Q_DOTS) + 2):
                    if 0 <= i < len(DOTS):
                        dots(i)
                for i in items_at(q - 1):
                    turn_probs(i)
                for n in groups_at(q):
                    turn_group(n)
                for i in items_at(q):
                    scores(i)
                for i in items_at(q - 2):
                    attend(i)
                for p, n in tree_at(q):
                    tree(p, n)
                for h in range(HEADS_A):
                    if q == Q_TREE[h // 2] + 7:
                        recur(h)
                    if q == Q_TREE[h // 2] + 8:
                        mean_square(h)

            def t5_table():
                pe.wait_ge(table_in, 32)
                for c in range(2):
                    mm = nc.tensor.matmul(turn_bank[c][0:HEADS_B, 0:T5W // 2], rel_sb[:],
                                          hot_sb[:, c * T5W // 2:(c + 1) * T5W // 2], start=True, stop=True)
                mm.then_inc(table_full, 1)

            for u, name in enumerate(UNITS):
                for q in range(4):
                    i, j = q // 2, q % 2
                    if name.startswith("up"):
                        quarter_up(u, i, j)
                    elif name[:2] in ("vb", "ia"):
                        quarter_t(u, i, j)
                    elif name == "kiwi" and i == 1:
                        quarter_wi(u, j)
                    else:
                        quarter_f(u, i, j)
                    if (u, q) == (1, 3):
                        t5_table()
                        pe.wait_ge(pool_set, 1)
                        pe.wait_ge(consts_in, 16 * N_CONSTS)
                    side(4 * u + q)
            for half in range(2):
                pe.wait_ge(lo_done, 4 * (NMAIN + 2 * half + 2))
                for t in range(TB):
                    bank = y_bank[half][t]
                    if half == 0 and t < 2:
                        pe.wait_ge(out_out[t], len(GROUPS) // 2 + 2)
                    elif half == 0:
                        pe.wait_ge(proj_out[t - 2], NPROJ[NMAIN])
                    else:
                        pe.wait_ge(up_out[t], 2 * KT // 4)
                    for k in range(KT):
                        if half == 0 and t == 0:
                            pe.wait_ge(m_lo_done, k + 1)
                        m = m_hi[:, k, queries(t)], m_lo[:, k, queries(t)]
                        if half == 0:
                            mm = split_product(bank[:], *m, x_hi[:, k, :], x_lo[:, k, :], k == 0, k == KT - 1)
                        else:
                            mm = split_product(bank[:].rearrange("p (s n) -> p s n", s=2), *m,
                                               w_hi[:, :, k, :], w_lo[:, :, k, :], k == 0, k == KT - 1)
                    mm.then_inc(y_full, 1)

        @block.scalar
        def _(act):
            def round_tiles(u, k):
                nc.scalar.activation(split_target(u, x_hi, w_hi)[:, k, :], raw(u)[:, k, :],
                                     ACT.Copy).then_inc(hi_done, 1)

            def split_hi(u, a):
                if a == 0:
                    act.wait_ge(w_in[u % 2], 16 * ((u + 1) // 2))
                    wait_split_target(act, u)
                round_tiles(u, slice(4 * a, 4 * a + 4))

            def leave_bank(u, i):
                name = UNITS[u]
                kind = name[:2]
                if kind in ("vb", "ia", "up") or (name == "kiwi" and i == 1):
                    return
                act.wait_ge(part_done, 2 * u + i + 1)
                tile = 0 if name == "kiwi" else 2 * int(name[2]) + i
                c = 2 * u + i
                func, b_col, scale = ACT.Identity, bias[:, c:c + 1], 1.0
                if kind == "ki":
                    dst = k_idx[:]
                elif kind == "qi":
                    dst = q_idx[:, tile, :]
                elif kind == "qb":
                    dst, b_col, scale = q_b[:, tile, :], bias_q[:, c:c + 1], QSCALE
                    act.wait_ge(bias_q_done, 1)
                elif kind == "kb":
                    dst = k_b[:, tile, :]
                elif kind in ("zb", "za"):
                    n = 2 * (u - UNITS.index("zb0")) + i
                    if n == 0:
                        act.wait_ge(x_lo_done, 4)
                    nc.scalar.activation(gate_a[:, n, :], proj_bank[i][:], ACT.Sigmoid, bias=b_col).then_inc(z_sig, 1)
                    return
                elif kind in ("fa", "qa"):
                    dst = (cum if kind == "fa" else q_a)[:, tile, :]
                    if name == "fa0" and i == 0:
                        act.wait_ge(pen_done, TB - 1)
                elif kind == "ga":
                    dst = gate_a[:, tile, :]
                    if tile == 0:
                        wait_proj_out(act, "za1", 0)
                        wait_proj_out(act, "za1", 1)
                else:
                    dst, func = g_b[:, tile % 4, :], ACT.Sigmoid
                    if tile == 0:
                        act.wait_ge(branch_a, HEADS_A)
                    elif tile >= 4:
                        act.wait_ge(mix_done, tile - 3)
                nc.scalar.activation(dst, proj_bank[i][:], func, bias=b_col, scale=scale).then_inc(proj_out[i], 1)

            def relu(i):
                b, h = DOTS[i]
                act.wait_ge(log_full, i + 1)
                if i >= 2:
                    act.wait_ge(relu_used, i - 1)
                n = (b + 1) * P
                nc.scalar.activation(relus[:, i % 2, 0:n], log_bank[i % 2][:, 0:n], ACT.Relu,
                                     scale=QSCALE).then_inc(log_out[i % 2], 1)

            def softmax_exp(i):
                b, h = ITEMS[i]
                wait_log_out(act, QK0 + i)
                if i >= 2:
                    act.wait_ge(turn_full, item_turn(i - 2) + 1)
                if i >= 8:
                    act.wait_ge(rcp_done, i // 4 - 1)
                n = (b + 1) * P
                nc.scalar.activation(prob[:, i % 2, 0:n], logit[:, i % 2, 0:n], ACT.Exp,
                                     bias=nmax[:, i % 2:i % 2 + 1], scale=-1.0,
                                     accum_out=prob_sum[:, i // 4 % 2, h % 4:h % 4 + 1]).then_inc(exp_done, 1)

            def forget(p, n):
                act.wait_ge(f_dve, 4 * p + (1, 1, 2, 2, 4)[n])
                if n in (1, 3):
                    act.wait_ge(f_act, 6 * p + (1, 0, 3)[n - 1])
                if n == 0:
                    nc.scalar.activation(dec[:, 0, :], dec[:, 0, :], ACT.Exp).then_inc(f_act, 1)
                elif n == 1:
                    nc.scalar.activation(dec[:, 0, :], dec[:, 0, :], ACT.Ln, bias=1.0).then_inc(f_act, 1)
                elif n == 2:
                    nc.scalar.activation(dec[:, 1, :], dec[:, 1, :], ACT.Exp, scale=-1.0).then_inc(f_act, 1)
                elif n == 3:
                    act.wait_ge(lb_step, 5)
                    for a in range(2):
                        c = slice(a * SEQ, a * SEQ + SEQ)
                        nc.scalar.activation(dec[:, 1, c], dec[:, 1, c], ACT.Ln, bias=1.0,
                                             scale=lb[:, 5, 2 * p + a:2 * p + a + 1]).then_inc(f_act, 1)
                else:
                    if p:
                        act.wait_ge(log_full, TREE0 + NTREE)
                        act.wait_ge(qk_done, 12)
                    nc.scalar.activation(flat(k_a[:]), k_c[:, 1, :], ACT.Exp).then_inc(f_act, 1)

            def near_factors(p):
                act.wait_ge(cum_done, 2 * (p + 1))
                cp = cum[:, 2 * p:2 * p + 2, :]
                if p:
                    act.wait_ge(far_f_done, p)
                    wait_lvl_multiplied(act, 0, 0)
                    act.wait_ge(far_done, 6)
                nc.scalar.activation(far_g[:], cp[:, :, SEG - 1::SEG], ACT.Exp).then_inc(seg_decay, 1)
                nc.scalar.activation(q_r[:], cp, ACT.Exp).then_inc(rl_done, 1)
                wait_dist(act, p, 0)
                nc.scalar.activation(flat(k_l[:]), dec[:, 0, :], ACT.Exp).then_inc(rl_done, 1)

            def level_factors(p, lv):
                wait_dist(act, p, lv)
                h = LEVELS[lv]
                v = groups(dec[:, lv % 2, :], h)
                nc.scalar.activation(v[:, :, h:2 * h], v[:, :, h:2 * h], ACT.Exp).then_inc(fac_done, 1)
                nc.scalar.activation(v[:, :, 0:h], v[:, :, 0:h], ACT.Exp, scale=-1.0).then_inc(fac_done, 1)

            def tree_copy(p, n):
                kind, m = TREE[n]
                if kind not in ("128", "256"):
                    return
                idx = TREE0 + NTREE * p + n
                act.wait_ge(log_full, idx + 1)
                if p:
                    act.wait_ge(recur_done, 2)
                bank = log_bank[idx % 2]
                if kind == "128":
                    for a in range(2):
                        ins = nc.scalar.activation(
                            strided(att[:, a, 0, P:2 * P], [[2 * (SEQ + P), 2], [1, P]]),
                            bank[:, 2 * a * P:2 * a * P + 2 * P].rearrange("p (t n) -> p t n", t=2), ACT.Copy)
                else:
                    ins = nc.scalar.activation(att[:, m, 0:2, 2 * P:SEQ],
                                               bank[:].rearrange("p (t n) -> p t n", t=2), ACT.Copy)
                ins.then_inc(log_out[idx % 2], 1)

            def squares(h):
                act.wait_ge(recur_done, h + 1)
                if h >= 2:
                    act.wait_ge(branch_a, h - 1)
                nc.scalar.activation(square[:, h % 2, :], out_bank[h % 2][:], ACT.Square).then_inc(sq_done, 1)

            def inverse_rms(h):
                i = len(TURNS) + h
                act.wait_ge(turn_full, i + 1)
                nc.scalar.activation(square[:, h % 2, :], turn_bank[i % 2][:], ACT.Ln,
                                     bias=eps[:, 0:1]).then_inc(turn_out[i % 2], 1)
                wait_turn_out(act, i)
                nc.scalar.activation(square[:, h % 2, :], square[:, h % 2, :], ACT.Exp,
                                     scale=-0.5).then_inc(rms_done, 1)

            def round_merged(m):
                act.wait_ge(mix_done, m + 1)
                nc.scalar.activation(m_hi[:, m, :], mix[:, m % 2, :], ACT.Copy).then_inc(m_hi_done, 1)

            def side(q):
                for i in range(2 * (q - Q_DOTS), 2 * (q - Q_DOTS) + 2):
                    if 0 <= i < len(DOTS):
                        relu(i)
                for i in items_at(q):
                    softmax_exp(i)
                for p, n in tree_at(q + 1):
                    if TREE[n][0] == "lv" and TREE[n][1]:
                        level_factors(p, TREE[n][1])
                for p in range(2):
                    at = q - Q_TREE[p]
                    if at == -4:
                        forget(p, 0)
                        forget(p, 1)
                    if at == -3:
                        forget(p, 2)
                        forget(p, 3)
                    if at == -2:
                        forget(p, 4)
                        near_factors(p)
                for p, n in tree_at(q):
                    tree_copy(p, n)
                for h in range(HEADS_A):
                    if q == Q_TREE[h // 2] + 7:
                        squares(h)
                    if q == Q_TREE[h // 2] + 8:
                        inverse_rms(h)

            for j in range(4):
                act.wait_ge(w0_in[j], 16)
                round_tiles(0, slice(2 * j, 2 * j + 2))
            act.dma_start(rel_sb[:], rel_bias).then_inc(table_in, 16)
            act.dma_start(hot_sb[:], one_hot).then_inc(table_in, 16)
            for dst, src in ((bias[:], b_cols), (lb[:, 0, :], lb_cols), (g_a[:], g_cols), (id_sb[:], ident),
                             (causal_sb[:], causal), (masks_sb[:], tree_masks),
                             (bias_ia[:], b_ia.partition_broadcast(P)), (bias_vb[:], b_vb.partition_broadcast(P)),
                             (bias_wi[:], b_wi.partition_broadcast(P))):
                act.dma_start(dst, src).then_inc(consts_in, 16)
            split_hi(1, 0)
            split_hi(1, 1)
            act.wait_ge(lb_step, 1)
            nc.scalar.activation(lb[:, 2, :], lb[:, 1, :], ACT.Exp).then_inc(lb_exp, 1)
            nc.scalar.preload_act_table_set("sigmoid_and_others")
            act.wait_ge(pool_set, 1)
            act.wait_ge(consts_in, 16 * N_CONSTS)
            for q in range(4 * NMAIN):
                u, j = q // 4, q % 4
                if j == 0 and u >= 1:
                    leave_bank(u - 1, 1)
                    split_hi(u + 1, 0)
                elif j == 1 and u >= 1:
                    split_hi(u + 1, 1)
                elif j == 2:
                    leave_bank(u, 0)
                if q == Q_ITEM[0] - 2:
                    nc.scalar.preload_act_table_set("natural_log_exp_and_others")
                if q == Q_MERGE:
                    nc.scalar.preload_act_table_set("sigmoid_and_others")
                side(q)
                if Q_MERGE <= q < Q_MERGE + 4:
                    act.wait_ge(branch_a, HEADS_A)
                    z = z_a if j < 2 else z_b
                    nc.scalar.activation(flat(o_hi[:, 2 * j:2 * j + 2, :]), flat(z[:, 2 * j % 4:2 * j % 4 + 2, :]),
                                         ACT.Copy).then_inc(o_hi_done, 1)
                if Q_MERGE + 4 <= q < Q_MERGE + 8:
                    if q == Q_MERGE + 4:
                        wait_proj_out(act, "ga3", 0)
                        wait_proj_out(act, "ga3", 1)
                    g = flat(gate_a[:, 2 * j:2 * j + 2, :])
                    nc.scalar.activation(g, g, ACT.Sigmoid).then_inc(gate_a_done, 1)
                m = merged_at(q)
                if m is not None:
                    round_merged(m)
                if u == NMAIN - 1:
                    if j >= 2:
                        split_hi(u + 2, j - 2)
            split_hi(NMAIN + 2, 0)
            split_hi(NMAIN + 2, 1)
            round_merged(KT - 1)
            nc.scalar.preload_act_table_set("natural_log_exp_and_others")
            split_hi(NMAIN + 3, 0)
            split_hi(NMAIN + 3, 1)
            for t in range(TB):
                act.wait_ge(y_aggr, t + 1)
                nc.scalar.activation(rstd[:, t, 0:1], aggr[:, t, 1:2], ACT.Ln, bias=eps[:, 1:2]).then_inc(ln_log, 1)
                act.wait_ge(ln_log, t + 1)
                nc.scalar.activation(rstd[:, t, 1:2], rstd[:, t, 0:1], ACT.Exp, scale=-0.5).then_inc(ln_rstd, 1)

        @block.vector
        def _(dve):
            steps = [0]

            def link(ins):
                steps[0] += 1
                ins.then_inc(dve_step, 1)
                dve.wait_ge(dve_step, steps[0])

            def split_x(j):
                k = slice(2 * j, 2 * j + 2)
                dve.wait_ge(x_in[j], 16)
                nc.vector.tensor_copy(x_hi[:, k, :], x_raw[:, k, :]).then_inc(x_hi_done, 1)
                dve.wait_ge(x_hi_done, j + 1)
                nc.vector.tensor_tensor(x_lo[:, k, :], x_raw[:, k, :], x_hi[:, k, :].bitcast(F32),
                                        ALU.subtract).then_inc(x_lo_done, 1)

            def lower_bound():
                dve.wait_ge(consts_in, 16 * N_CONSTS)
                nc.vector.tensor_tensor(lb[:, 1, :], lb[:, 0, :], lb[:, 0, :], ALU.subtract).then_inc(lb_step, 1)
                dve.wait_ge(lb_exp, 1)
                nc.vector.reciprocal(lb[:, 3, :], lb[:, 2, :]).then_inc(lb_step, 1)
                dve.wait_ge(lb_step, 2)
                nc.vector.tensor_tensor(lb[:, 4, :], lb[:, 2, :], lb[:, 3, :], ALU.mult).then_inc(lb_step, 1)
                dve.wait_ge(lb_step, 3)
                nc.vector.tensor_tensor(lb[:, 5, :], lb[:, 4, :], lb[:, 4, :], ALU.subtract).then_inc(lb_step, 1)
                dve.wait_ge(lb_step, 4)
                nc.vector.tensor_scalar(lb[:, 6, :], lb[:, 5, :], -1.0, 1.0, ALU.mult, ALU.add).then_inc(lb_step, 1)
                nc.vector.tensor_scalar(bias_q[:], bias[:], QSCALE, None, ALU.mult).then_inc(bias_q_done, 1)

            def leave_bank(u, i):
                name = UNITS[u]
                kind = name[:2]
                if kind in ("vb", "ia"):
                    n = int(name[2])
                    c = slice(n * UW, n * UW + UW)
                    if kind == "ia":
                        dve.wait_ge(rep_out, 16)
                    dve.wait_ge(part_done, 2 * u + i + 1)
                    row = (bias_vb if kind == "vb" else bias_ia)[:, c].unsqueeze(1).broadcast_to([P, 2, UW])
                    nc.vector.tensor_tensor((v_b if kind == "vb" else v_a)[:, 2 * i:2 * i + 2, c],
                                            proj_bank[i][:].rearrange("p (t n) -> p t n", t=2), row,
                                            ALU.add).then_inc(proj_out[i], 1)
                elif kind in ("zb", "za"):
                    n = 2 * (u - UNITS.index("zb0")) + i
                    dve.wait_ge(z_sig, n + 1)
                    nc.vector.scalar_tensor_tensor(out=z_part(n), in0=proj_bank[i][:],
                                                   scalar=bias[:, 2 * u + i:2 * u + i + 1], in1=gate_a[:, n, :],
                                                   op0=ALU.add, op1=ALU.mult).then_inc(proj_out[i], 1)
                elif name == "kiwi" and i == 1:
                    dve.wait_ge(part_done, 2 * u + 2)
                    nc.vector.tensor_tensor(
                        w_idx[:], proj_bank[1][:, 0:TB * HEADS_I].rearrange("p (t h) -> p t h", t=TB),
                        bias_wi[:].unsqueeze(1).broadcast_to([P, TB, HEADS_I]), ALU.add).then_inc(proj_out[1], 1)
                    wait_proj_out(dve, "kiwi", 1)
                    link(nc.vector.tensor_scalar(w_idx[:], w_idx[:], WSCALE, None, ALU.mult))

            def add_score(i):
                b, h = DOTS[i]
                wait_log_out(dve, i)
                n = (b + 1) * P
                w = w_idx[:, b, h:h + 1]
                if h == 0:
                    ins = nc.vector.tensor_scalar(score[b][:], relus[:, i % 2, 0:n], w, None, ALU.mult)
                else:
                    dve.wait_ge(relu_used, i)
                    ins = nc.vector.scalar_tensor_tensor(out=score[b][:], in0=relus[:, i % 2, 0:n], scalar=w,
                                                         in1=score[b][:], op0=ALU.mult, op1=ALU.add)
                ins.then_inc(relu_used, 1)
                if h == HEADS_I - 1:
                    dve.wait_ge(relu_used, i + 1)
                    diag = score[b][:, b * P:b * P + P]
                    link(nc.vector.tensor_tensor(diag, diag, causal_sb[:], ALU.add))

            def topk_round(b, r):
                link(nc.vector.max(best8[:], score[b][:]))
                link(nc.vector.match_replace(score[b][:], best8[:], score[b][:], TAKEN))
                if r == ROUNDS - 1:
                    nc.vector.tensor_scalar(pen[b][:], score[b][:], TAKEN, NEG, ALU.not_equal,
                                            ALU.mult).then_inc(pen_done, 1)

            def move_probs(i):
                b, h = ITEMS[i]
                m = item_turn(i)
                dve.wait_ge(turn_full, m + 1)
                if i >= 2:
                    dve.wait_ge(pv_done, i - 1)
                n = (b + 1) * P
                nc.vector.tensor_copy(prob_t[:, i % 2, 0:n], turn_bank[m % 2][:, 0:n]).then_inc(turn_out[m % 2], 1)

            def logits(i):
                b, h = ITEMS[i]
                dve.wait_ge(log_full, QK0 + i + 1)
                dve.wait_ge(logit_pre, i + 1)
                if i >= 2:
                    dve.wait_ge(exp_done, i - 1)
                n = (b + 1) * P
                lg = logit[:, i % 2, 0:n]
                nc.vector.tensor_tensor_reduce(out=lg, in0=log_bank[i % 2][:, 0:n], in1=lg, scale=-1.0, scalar=3e38,
                                               op0=ALU.add, op1=ALU.min,
                                               accum_out=nmax[:, i % 2:i % 2 + 1]).then_inc(log_out[i % 2], 1)

            def divide_group(n):
                dve.wait_ge(exp_done, 4 * n + 4)
                if n >= 2:
                    dve.wait_ge(out_out[n % 2], n // 2)
                    dve.wait_ge(turn_full, group_turn(n - 2) + 1)
                nc.vector.reciprocal(prob_rcp[:, n % 2, :], prob_sum[:, n % 2, :]).then_inc(rcp_done, 1)
                dve.wait_ge(rcp_done, n + 1)
                dve.wait_ge(pv_done, 4 * n + 4)
                nc.vector.tensor_tensor(o_tok[:, n % 2, :].rearrange("p (h d) -> p h d", h=4),
                                        out_bank[n % 2][:, 0:256].rearrange("p (h d) -> p h d", h=4),
                                        prob_rcp[:, n % 2, :].unsqueeze(2).broadcast_to([P, 4, 64]),
                                        ALU.mult).then_inc(out_out[n % 2], 1)

            def gate_group(n):
                g, b = GROUPS[n]
                m = group_turn(n)
                dve.wait_ge(turn_full, m + 1)
                if n == 0:
                    for name in ("zb0", "zb1"):
                        wait_proj_out(dve, name, 0)
                        wait_proj_out(dve, name, 1)
                z = z_b[:, 2 * g:2 * g + 2, queries(b)]
                nc.vector.tensor_tensor(z, turn_bank[m % 2][:, 0:256].rearrange("p (c t) -> p c t", c=2), z,
                                        ALU.mult).then_inc(turn_out[m % 2], 1)

            def forget(p, n):
                f = flat(cum[:, 2 * p:2 * p + 2, :])
                if n == 0:
                    if p == 0:
                        dve.wait_ge(pv_done, len(ITEMS))
                    else:
                        dve.wait_ge(qk_done, 12)
                    for name in (f"fa{p}", f"qa{p}"):
                        wait_proj_out(dve, name, 0)
                        wait_proj_out(dve, name, 1)
                    nc.vector.scalar_tensor_tensor(out=dec[:, 0, :], in0=f, scalar=-1.0, in1=f, op0=ALU.mult,
                                                   op1=ALU.min).then_inc(f_dve, 1)
                    nc.vector.tensor_scalar(dec[:, 1, :], f, F_FLOOR, None, ALU.max).then_inc(f_dve, 1)
                else:
                    if p:
                        dve.wait_ge(log_full, TREE0 + NTREE)
                    log_sig = k_c[:, 0, :]
                    dve.wait_ge(f_act, 6 * p + 2)
                    nc.vector.scalar_tensor_tensor(out=log_sig, in0=f, scalar=0.0, in1=dec[:, 0, :], op0=ALU.min,
                                                   op1=ALU.subtract).then_inc(f_dve, 1)
                    dve.wait_ge(f_dve, 4 * p + 3)
                    nc.vector.tensor_tensor(k_c[:, 1, :], log_sig, f, ALU.subtract).then_inc(f_dve, 1)
                    dve.wait_ge(f_dve, 4 * p + 4)
                    dve.wait_ge(f_act, 6 * p + 5)
                    link(nc.vector.tensor_tensor(log_sig, log_sig, dec[:, 1, :], ALU.add))
                    dve.wait_ge(reset_set, 2)
                    for a in range(2):
                        nc.vector.tensor_tensor_scan(cum[:, 2 * p + a, :], reset[:], log_sig[:, a * SEQ:a * SEQ + SEQ],
                                                     0.0, ALU.mult, ALU.add).then_inc(cum_done, 1)

            def near_products(p):
                dve.wait_ge(rl_done, 2 * p + 2)
                dve.wait_ge(k_done, 2 * (p + 1))
                nc.vector.tensor_tensor(q_r[:], q_r[:], q_a[:, 2 * p:2 * p + 2, :], ALU.mult).then_inc(near_done, 1)
                nc.vector.tensor_tensor(k_l[:], k_l[:], k_a[:], ALU.mult).then_inc(near_done, 1)

            def far_products(p):
                dve.wait_ge(near_done, 2 * p + 2)
                dve.wait_ge(far_f_done, p + 1)
                if p:
                    dve.wait_ge(log_full, TREE0 + NTREE)
                for kind, (src, quad0) in enumerate(((k_l, 0), (q_r, 2))):
                    for a in range(2):
                        s4 = src[:, a, :].rearrange("p (b s t) -> p b s t", b=2, t=SEG)[:, :, quad0:quad0 + 2, :]
                        f4 = far_f[:, kind, a, :].rearrange("p (b s) -> p b s", b=2)
                        nc.vector.tensor_tensor(far[:, kind, a, :].rearrange("p (b s t) -> p b s t", b=2, t=SEG), s4,
                                                f4.unsqueeze(3).broadcast_to([P, 2, 2, SEG]),
                                                ALU.mult).then_inc(far_done, 1)
                for kind, (src, half) in enumerate(((k_l, 0), (q_r, 256)), 2):
                    s4 = src[:, :, half:half + 256].rearrange("p a (s t) -> p a s t", t=SEG)
                    nc.vector.tensor_tensor(far[:, kind, :, :].rearrange("p a (s t) -> p a s t", t=SEG), s4,
                                            far_f[:, kind, :, :].unsqueeze(3).broadcast_to([P, 2, 4, SEG]),
                                            ALU.mult).then_inc(far_done, 1)

            def distance(p, lv):
                if lv > 1:
                    dve.wait_ge(qk_done, 2 * (6 * p + lv - 2))
                level_distance(nc.vector, p, lv).then_inc(dist_dve, 1)

            def level_products(p, lv):
                h = LEVELS[lv]
                ring = (lv - 1) % 2
                dve.wait_ge(fac_done, 2 * (6 * p + lv))
                if lv > 2:
                    wait_lvl_multiplied(dve, p, lv - 2)
                v = groups(dec[:, lv % 2, :], h)
                q = groups(flat(q_a[:, 2 * p:2 * p + 2, :]), h)
                k = groups(flat(k_a[:]), h)
                nc.vector.tensor_tensor(flat(q_c[:, ring]).rearrange("p (n t) -> p n t", t=h), v[:, :, h:2 * h],
                                        q[:, :, h:2 * h], ALU.mult).then_inc(qk_done, 1)
                nc.vector.tensor_tensor(groups(k_c[:, ring, :], h)[:, :, 0:h], v[:, :, 0:h], k[:, :, 0:h],
                                        ALU.mult).then_inc(qk_done, 1)

            def tree_place(p, n):
                kind, m = TREE[n]
                if kind not in ("diag", "lv"):
                    return
                idx = TREE0 + NTREE * p + n
                bank = log_bank[idx % 2]
                dve.wait_ge(log_full, idx + 1)
                if kind == "diag":
                    if p:
                        dve.wait_ge(recur_done, m + 1)
                    nc.vector.tensor_tensor(att_blocks(m), bank[:].rearrange("p (t n) -> p t n", t=TB),
                                            id_sb[:].unsqueeze(1).broadcast_to([P, TB, P]),
                                            ALU.mult).then_inc(log_out[idx % 2], 1)
                    return
                h = LEVELS[m]
                if m == 0:
                    for d in range(2):
                        wait_log_out(dve, TREE0 + NTREE * p + d)
                else:
                    link_level(p, m)
                for a in range(2):
                    src = strided(bank[:, a * 256:a * 256 + 256], [[64, TB], [h, 64 // h], [1, h]])
                    mask = strided(masks_sb[:, m, :], [[0, TB], [h, 64 // h], [1, h]])
                    ins = nc.vector.copy_predicated(att_blocks(a, h), mask, src)
                ins.then_inc(log_out[idx % 2], 1)

            def link_level(p, lv):
                wait_log_out(dve, TREE0 + NTREE * p + TREE.index(("lv", lv - 1)))

            def gate_branch_a(h):
                dve.wait_ge(rms_done, h + 1)
                for name in ("za0", "za1"):
                    wait_proj_out(dve, name, 0)
                    wait_proj_out(dve, name, 1)
                root = square[:, h % 2, :]
                nc.vector.tensor_tensor(root, out_bank[h % 2][:], root, ALU.mult).then_inc(out_out[h % 2], 1)
                dve.wait_ge(out_out[h % 2], len(GROUPS) // 2 + h // 2 + 1)
                nc.vector.scalar_tensor_tensor(out=z_a[:, h, :], in0=root, scalar=g_a[:, h:h + 1], in1=z_a[:, h, :],
                                               op0=ALU.mult, op1=ALU.mult).then_inc(branch_a, 1)

            def split_branches(j):
                z = z_a if j < 2 else z_b
                dve.wait_ge(branch_a, HEADS_A)
                dve.wait_ge(o_hi_done, j + 1)
                nc.vector.tensor_tensor(flat(o_lo[:, 2 * j:2 * j + 2, :]), flat(z[:, 2 * j % 4:2 * j % 4 + 2, :]),
                                        flat(o_hi[:, 2 * j:2 * j + 2, :]).bitcast(F32),
                                        ALU.subtract).then_inc(o_lo_done, 1)

            def merge(m):
                u = UNITS.index(f"up{m // 2}")
                dve.wait_ge(part_done, 2 * u + m % 2 + 1)
                dve.wait_ge(gate_a_done, m // 2 + 1)
                wait_proj_out(dve, f"gb{m // 2}", m % 2)
                if m >= 2:
                    dve.wait_ge(m_hi_done, m - 1)
                    dve.wait_ge(m_lo_done, m - 1)
                fa, fb = 2 * m % 4, (2 * m + 1) % 4
                mx, gb = mix[:, m % 2, :], g_b[:, m % 4, :]
                nc.vector.tensor_tensor(mx, up_bank[fa][:], gate_a[:, m, :], ALU.mult).then_inc(up_out[fa], 1)
                nc.vector.tensor_tensor(gb, up_bank[fb][:], gb, ALU.mult).then_inc(up_out[fb], 1)
                dve.wait_ge(up_out[fa], m // 2 + 1)
                dve.wait_ge(up_out[fb], m // 2 + 1)
                nc.vector.tensor_tensor(mx, mx, gb, ALU.add).then_inc(mix_done, 1)
                dve.wait_ge(m_hi_done, m + 1)
                nc.vector.tensor_tensor(m_lo[:, m, :], mx, m_hi[:, m, :].bitcast(F32),
                                        ALU.subtract).then_inc(m_lo_done, 1)

            def residual(t, half):
                c = slice(half * 512, half * 512 + 512)
                dve.wait_ge(y_full, TB * half + t + 1)
                dve.wait_ge(res_in[t], 16)
                link(nc.vector.scalar_tensor_tensor(out=y_sb[:, t, c], in0=x_res[:, t, c], scalar=ALPHA,
                                                    in1=y_bank[half][t][:], op0=ALU.mult, op1=ALU.add))
                link(nc.vector.bn_stats(stats[:, t, half, :], y_sb[:, t, c]))

            def side(q):
                u, j = q // 4, q % 4
                if j == 0 and u >= 1:
                    leave_bank(u - 1, 1)
                if j == 2:
                    leave_bank(u, 0)
                for i in range(2 * (q - Q_DOTS), 2 * (q - Q_DOTS) + 2):
                    if 0 <= i < len(DOTS):
                        add_score(i)
                for n in groups_at(q):
                    divide_group(n)
                for i in items_at(q - 1):
                    move_probs(i)
                for n in groups_at(q):
                    gate_group(n)
                for i in items_at(q):
                    logits(i)
                for b, r in rounds.get(q, ()):
                    topk_round(b, r)
                for p in range(2):
                    at = q - Q_TREE[p]
                    if at == -4:
                        forget(p, 0)
                    if at == -3:
                        forget(p, 1)
                    if at == -1:
                        near_products(p)
                    if at == 0:
                        far_products(p)
                    if at == 0:
                        distance(p, 1)
                    if at == 2:
                        level_products(p, 1)
                        distance(p, 3)
                        level_products(p, 2)
                    if at == 3:
                        level_products(p, 3)
                        distance(p, 5)
                        level_products(p, 4)
                    if at == 4:
                        level_products(p, 5)
                        level_products(p, 6)
                for p, n in tree_at(q):
                    tree_place(p, n)
                for h in range(HEADS_A):
                    if q == Q_TREE[h // 2] + 8:
                        gate_branch_a(h)
                if Q_MERGE <= q < Q_MERGE + 4:
                    split_branches(j)
                m = merged_at(q)
                if m is not None:
                    merge(m)

            for j in range(4):
                split_x(j)
            lower_bound()
            for q in range(4 * NMAIN):
                side(q)
                if q == 7:
                    dve.wait_ge(table_full, 1)
                    for c in range(2):
                        nc.vector.tensor_copy(table[:, c * T5W // 2:(c + 1) * T5W // 2],
                                              turn_bank[c][0:HEADS_B, 0:T5W // 2]).then_inc(table_done, 1)
            merge(KT - 1)
            for t in range(TB):
                residual(t, 0)
            for t in range(TB):
                residual(t, 1)
                if t == 0:
                    dve.wait_ge(ln_in, 32)
                nc.vector.bn_aggr(aggr[:, t, :], stats[:, t, :, :].rearrange("p a b -> p (a b)")).then_inc(y_aggr, 1)
                dve.wait_ge(ln_rstd, t + 1)
                for c in (slice(0, 512), slice(512, 1024)):
                    y = y_sb[:, t, c]
                    link(nc.vector.scalar_tensor_tensor(out=y, in0=y, scalar=aggr[:, t, 0:1], in1=ln_gb[:, 0, c],
                                                        op0=ALU.subtract, op1=ALU.mult))
                    nc.vector.scalar_tensor_tensor(out=y, in0=y, scalar=rstd[:, t, 1:2], in1=ln_gb[:, 1, c],
                                                   op0=ALU.mult, op1=ALU.add).then_inc(y_done, 1)

        @block.gpsimd
        def _(pool):
            nc.gpsimd.memset(ones_sb[:], 1.0 / P)
            nc.gpsimd.memset(eps[:, 0:1], RMS_EPS)
            nc.gpsimd.memset(eps[:, 1:2], LN_EPS).then_inc(pool_set, 1)

            def split_lo(u, j):
                pool.wait_ge(hi_done, 2 * u + 2 + j // 2 + 1 if u else j + 1)
                k = slice(2 * j, 2 * j + 2)
                nc.gpsimd.tensor_tensor(split_target(u, x_lo, w_lo)[:, k, :], raw(u)[:, k, :],
                                        split_target(u, x_hi, w_hi)[:, k, :].bitcast(F32),
                                        ALU.subtract).then_inc(lo_done, 1)

            def bias_and_penalty(i):
                b, h = ITEMS[i]
                if i == 0:
                    pool.wait_ge(t5_in, 16)
                    pool.wait_ge(consts_in, 16 * N_CONSTS)
                if h == 0 and b:
                    pool.wait_ge(pen_done, b)
                if i >= 2:
                    pool.wait_ge(exp_done, i - 1)
                n = (b + 1) * P
                nc.gpsimd.tensor_tensor(logit[:, i % 2, 0:n], t5[:, h, SEQ - n:SEQ], pen[b][:] if b else causal_sb[:],
                                        ALU.add).then_inc(logit_pre, 1)

            def make_reset():
                pool.wait_ge(pv_done, len(ITEMS))
                nc.gpsimd.memset(far_f[:], 1.0)
                nc.gpsimd.memset(reset[:], 1.0).then_inc(reset_set, 1)
                pool.wait_ge(reset_set, 1)
                nc.gpsimd.memset(reset[:, 0:SEQ:SEG], 0.0).then_inc(reset_set, 1)

            def finish_k(p):
                pool.wait_ge(f_act, 6 * p + 6)
                pool.wait_ge(lb_step, 5)
                for a in range(2):
                    nc.gpsimd.tensor_scalar(k_a[:, a, :], k_a[:, a, :], lb[:, 6, 2 * p + a:2 * p + a + 1], None,
                                            ALU.mult).then_inc(k_done, 1)

            def end_distance(p):
                pool.wait_ge(cum_done, 2 * (p + 1))
                c = flat(cum[:, 2 * p:2 * p + 2, :]).rearrange("p (s t) -> p s t", t=SEG)
                nc.gpsimd.tensor_tensor(dec[:, 0, :].rearrange("p (s t) -> p s t", t=SEG),
                                        c[:, :, SEG - 1:SEG].broadcast_to([P, 2 * NSEG, SEG]), c,
                                        ALU.subtract).then_inc(dist_pool, 1)

            def far_factors(p):
                pool.wait_ge(seg_decay, p + 1)
                if p:
                    pool.wait_ge(far_done, 6)
                n = 7 * p
                g = far_g
                for dst, src in ((far_f[:, 0, :, 0:4:2], g[:, :, 1:8:4]), (far_f[:, 1, :, 1:4:2], g[:, :, 2:8:4]),
                                 (far_f[:, 2, :, 2:3], g[:, :, 3:4]), (far_f[:, 3, :, 1:2], g[:, :, 4:5])):
                    n += 1
                    nc.gpsimd.tensor_copy(dst, src).then_inc(far_f_step, 1)
                for dst, x, y in ((far_f[:, 2, :, 1:2], far_f[:, 2, :, 2:3], g[:, :, 2:3]),
                                  (far_f[:, 3, :, 2:3], far_f[:, 3, :, 1:2], g[:, :, 5:6]),
                                  (far_f[:, 2, :, 0:1], far_f[:, 2, :, 1:2], g[:, :, 1:2])):
                    pool.wait_ge(far_f_step, n)
                    n += 1
                    nc.gpsimd.tensor_tensor(dst, x, y, ALU.mult).then_inc(far_f_step, 1)
                pool.wait_ge(far_f_step, n)
                nc.gpsimd.tensor_tensor(far_f[:, 3, :, 3:4], far_f[:, 3, :, 2:3], g[:, :, 6:7],
                                        ALU.mult).then_inc(far_f_done, 1)

            def distance(p, lv):
                if lv == 2:
                    pool.wait_ge(rl_done, 2 * p + 2)
                else:
                    pool.wait_ge(qk_done, 2 * (6 * p + lv - 2))
                level_distance(nc.gpsimd, p, lv).then_inc(dist_pool, 1)

            def side(q):
                j = q % 4
                u = q // 4 + 1
                if u >= 2:
                    for piece in ((0,), (1, 2), (3,), ())[j]:
                        split_lo(u, piece)
                if q == Q_ITEM[0] - 1:
                    bias_and_penalty(0)
                    bias_and_penalty(1)
                for i in items_at(q):
                    if i + 2 < len(ITEMS):
                        bias_and_penalty(i + 2)
                if q == Q_TREE[0] - 5:
                    make_reset()
                for p in range(2):
                    at = q - Q_TREE[p]
                    if at == -2:
                        end_distance(p)
                        finish_k(p)
                        far_factors(p)
                    if at == 1:
                        distance(p, 2)
                    if at == 2:
                        distance(p, 4)
                    if at == 3:
                        distance(p, 6)

            for u in (0, 1):
                for j in range(4):
                    split_lo(u, j)
            for q in range(4 * NMAIN):
                side(q)
            for u in range(NMAIN + 1, NU):
                for j in range(4):
                    split_lo(u, j)


def t5_one_hot():
    d = np.arange(SEQ - 1, -1, -1)
    exact = BUCKETS // 2
    large = exact + (np.log(np.maximum(d, 1).astype(np.float32) / np.float32(exact))
                     / np.float32(np.log(MAX_DISTANCE / exact)) * (BUCKETS - exact)).astype(np.int32)
    bucket = np.where(d < exact, d, np.minimum(large, BUCKETS - 1))
    hot = np.zeros((BUCKETS, T5W), np.float32)
    hot[bucket, np.arange(SEQ)] = 1.0
    return hot


def tree_level_masks():
    key, n = np.arange(P)[:, None], np.arange(64)[None, :]
    return np.stack([(key // (2 * h) == n // h) & (key % (2 * h) < h) for h in LEVELS], 1).astype(np.int32)


def kernel(**inputs):
    import concourse.bacc as bacc
    from concourse.bass_utils import run_bass_kernel_spmd

    a = {k: np.asarray(v) for k, v in inputs.items()}
    x, w_in, b_in = a["x"][0], a["w_in"][0], a["b_in"][0]

    def unit(rows_by_tile):
        return rows_by_tile.reshape(KT, P, -1).transpose(1, 0, 2).reshape(P, -1)

    units, b_cols = [], np.zeros((P, 2 * NMAIN), np.float32)
    for u, name in enumerate(UNITS):
        kind = name[:2]
        if name == "kiwi":
            ki = COLUMNS["ki"]
            w_kiwi = unit(np.concatenate([w_in[:, ki:ki + 64], w_in[:, ki:ki + 64 + HEADS_I]], 1))
            b_cols[:, 2 * u] = np.concatenate([b_in[ki:ki + 64]] * 2)
        elif kind == "up":
            c = slice(int(name[2]) * UW, int(name[2]) * UW + UW)
            units.append(unit(np.concatenate([a["w_up_a"][0][:, c], a["w_up_b"][0][:, c]], 0)))
        else:
            c = COLUMNS[kind] + int(name[2]) * UW
            units.append(unit(w_in[:, c:c + UW]))
            b_cols[:, 2 * u], b_cols[:, 2 * u + 1] = b_in[c:c + P], b_in[c + P:c + UW]
    for n in (0, 1, 3, 2):
        units.append(unit(a["w_out"][0][:, n * UW:n * UW + UW]))
    arrays = {
        "x_t": x.reshape(SEQ, KT, P).transpose(2, 1, 0), "x_tok": x.reshape(TB, P, D_MODEL),
        "w_units": np.stack(units), "w_kiwi": w_kiwi, "b_cols": b_cols,
        "b_ia": b_in[COLUMNS["ia"]:COLUMNS["ia"] + D_A], "b_vb": b_in[COLUMNS["vb"]:COLUMNS["vb"] + D_B],
        "b_wi": b_in[COLUMNS["wi"]:COLUMNS["wi"] + HEADS_I],
        "lb_cols": a["lb_logits"][0].reshape(HEADS_A, P).T, "g_cols": a["norm_a_g"][0].reshape(HEADS_A, P).T,
        "rel_bias": a["rel_bias"], "ln_g": a["ln_g"][0], "ln_b": a["ln_b"][0],
        "one_hot": t5_one_hot(), "ident": np.eye(P, dtype=np.float32),
        "causal": np.where(np.arange(P)[None, :] > np.arange(P)[:, None], np.float32(NEG), np.float32(0)),
        "tree_masks": tree_level_masks(),
    }
    arrays = {k: np.ascontiguousarray(v) for k, v in arrays.items()}
    nc = bacc.Bacc("TRN2", target_bir_lowering=False, num_devices=1)
    args = [nc.dram_tensor(f"in_{k}", v.shape, mybir.dt.from_np(v.dtype), kind="ExternalInput").ap()
            for k, v in arrays.items()]
    out = nc.dram_tensor("out_0", (TB, P, D_MODEL), F32, kind="ExternalOutput").ap()
    hybrid_kernel(nc, *args, out)
    r = run_bass_kernel_spmd(nc, [{f"in_{k}": v for k, v in arrays.items()}], core_ids=[0])
    return r.results[0]["out_0"].reshape(1, SEQ, D_MODEL)
```

```python
from contextlib import ExitStack

import numpy as np
import concourse.bass as bass
from concourse import mybir

F32 = mybir.dt.float32
F32R = mybir.dt.float32r
I32 = mybir.dt.int32
ALU = mybir.AluOpType
ACT = mybir.ActivationFunctionType

P = 128
D_MODEL, SEQ, DEPTH = 1024, 512, 1
D_A = D_B = 512
HEADS_A, HEADS_B, HEADS_I = 4, 8, 8
TOPK = min(256, SEQ // 4)
BUCKETS, MAX_DISTANCE = 32, 128
ALPHA = (2 * DEPTH) ** 0.25
LN_EPS, RMS_EPS = 1e-5, 1e-6
KT = D_MODEL // P
TB = SEQ // P
UW = 256
QSCALE = 64 ** -0.5
WSCALE = HEADS_I ** -0.5
NEG = -1e30
TAKEN = -3e38
F_FLOOR = -40.0
SEG = 64
NSEG = SEQ // SEG
LEVELS = (64, 32, 16, 8, 4, 2, 1)

UNITS = ["kiwi", "qi0", "qi1", "zb0", "zb1", "za0", "za1", "qb0", "kb0", "vb0", "qb1", "kb1", "vb1",
         "ia0", "ia1", "fa0", "qa0", "fa1", "qa1", "ga0", "ga1", "ga2", "ga3",
         "gb0", "gb1", "up0", "gb2", "up1", "gb3", "up2", "up3"]
NMAIN = len(UNITS)
NOUT = 4
NU = NMAIN + NOUT
COLUMNS = {"qa": 0, "fa": 512, "ia": 1024, "za": 1536, "qb": 2048, "kb": 2560, "vb": 3072, "zb": 3584,
           "qi": 4096, "ki": 4608, "wi": 4672, "ga": 4680, "gb": 5704}
WKI = 64 + HEADS_I
NPROJ = [sum(n != "kiwi" and not n.startswith("up") for n in UNITS[:u]) for u in range(NMAIN + 1)]

DOTS = [(b, h) for b in range(1, TB) for h in range(HEADS_I)]
ITEMS = [(b, 4 * g + h) for g in range(2) for b in range(TB) for h in range(4)]
GROUPS = [(g, b) for g in range(2) for b in range(TB)]
QK0 = len(DOTS)
TREE0 = QK0 + len(ITEMS)
N_CONSTS = 6
T5W = SEQ + P
TREE = [("diag", 0), ("diag", 1), ("lv", 0), ("128", 0), ("256", 0), ("256", 1),
        ("lv", 1), ("lv", 2), ("lv", 3), ("lv", 4), ("lv", 5), ("lv", 6)]
NTREE = len(TREE)

Q_DOTS = 4 * 3
Q_ITEM = [39 + i if i < 16 else 55 + 2 * (i - 16) // 3 for i in range(len(ITEMS))]
Q_GROUP = [Q_ITEM[4 * n + 3] + 4 for n in range(len(GROUPS))]
Q_PREP = (68, 78)
Q_TREE = (74, 83)
Q_MERGE = 4 * UNITS.index("gb0")
TURNS = sorted([(q + 1, 0, i) for i, q in enumerate(Q_ITEM)] + [(q, 1, n) for n, q in enumerate(Q_GROUP)])
TURNS = [t[1:] for t in TURNS]
ROUNDS = TOPK // 8


def topk_rounds():
    plan = {}
    for b, first, per in ((1, 18, 1.8), (2, 27, 1.8), (3, 36, 1.8)):
        for r in range(ROUNDS):
            plan.setdefault(first + int(r / per), []).append((b, r))
    return plan


def hybrid_kernel(nc, x_t, x_tok, w_units, w_kiwi, b_cols, b_ia, b_vb, lb_cols, g_cols, rel_bias,
                  ln_g, ln_b, one_hot, ident, causal, tree_masks, out):
    with ExitStack() as ctx:
        def sb(name, shape, dt=F32, stack=ctx):
            return stack.enter_context(nc.sbuf_tensor(name, shape, dt))

        def sem(name):
            return ctx.enter_context(nc.semaphore(name))

        x_hi, x_lo = (sb(n, [P, KT, SEQ], F32R) for n in ("x_hi", "x_lo"))
        w_raw = sb("w_raw", [P, 2, KT * UW])
        w_hi, w_lo = (sb(n, [P, 2, KT, UW], F32R) for n in ("w_hi", "w_lo"))
        id_sb = sb("id_sb", [P, P])
        causal_sb = sb("causal_sb", [P, P])
        ones_sb = sb("ones_sb", [P, P])
        masks_sb = sb("masks_sb", [P, len(LEVELS) - 2, 64], I32)
        bias = sb("bias", [P, 2 * NMAIN])
        bias_q = sb("bias_q", [P, 2 * NMAIN])
        bias_ia, bias_vb = sb("bias_ia", [P, D_A]), sb("bias_vb", [P, D_B])
        w_idx = sb("w_idx", [P, TB, HEADS_I])
        lb = sb("lb", [P, 7, HEADS_A])
        g_a = sb("g_a", [P, HEADS_A])
        eps = sb("eps", [P, 2])
        best8 = sb("best8", [P, 8])
        nmax = sb("nmax", [P, 2])
        prob_sum, prob_rcp = sb("prob_sum", [P, 2, 4]), sb("prob_rcp", [P, 2, 4])
        stats, aggr, rstd = sb("stats", [P, TB, 2, 6]), sb("aggr", [P, TB, 2]), sb("rstd", [P, TB, 2])
        z_a = sb("z_a", [P, HEADS_A, SEQ])
        z_b = sb("z_b", [P, HEADS_B // 2, SEQ])
        U1 = 78 * 1024 + 512

        with ExitStack() as s:
            k_hi2, k_lo2 = sb("k_hi2", [P, SEQ], F32R, s), sb("k_lo2", [P, SEQ], F32R, s)
            with ExitStack() as s2:
                q_hl = sb("q_hl", [P, HEADS_I, SEQ], F32R, s2)
            q_b, k_b = sb("q_b", [P, 4, SEQ], stack=s), sb("k_b", [P, 4, SEQ], stack=s)
            score = {b: sb(f"score{b}", [P, (b + 1) * P], stack=s) for b in range(1, TB)}
            wi_t = score[TB - 1][64:WKI, :]
            relus = sb("relus", [P, 2, SEQ], stack=s)
            v_b = sb("v_b", [P, TB, D_B], stack=s)
            t5 = sb("t5", [P, HEADS_B, SEQ], stack=s)
            pen = {b: sb(f"pen{b}", [P, (b + 1) * P], stack=s) for b in range(1, TB)}
            logit = sb("logit", [P, 2, SEQ], stack=s)
            prob = sb("prob", [P, 2, SEQ], stack=s)
            prob_t = sb("prob_t", [P, 2, SEQ], stack=s)
            o_tok = sb("o_tok", [P, 2, 4 * 64], stack=s)
        with ExitStack() as s:
            cum = sb("cum", [P, HEADS_A, SEQ], stack=s)
            q_a = sb("q_a", [P, HEADS_A, SEQ], stack=s)
            k_a = sb("k_a", [P, 2, SEQ], stack=s)
            q_r, k_l = sb("q_r", [P, 2, SEQ], stack=s), sb("k_l", [P, 2, SEQ], stack=s)
            dec = sb("dec", [P, 2, 2 * SEQ], stack=s)
            q_c = sb("q_c", [P, 2, 2, SEQ // 2], stack=s)
            k_c = sb("k_c", [P, 2, 2 * SEQ], stack=s)
            far = sb("far", [P, 4, 2, SEQ // 2], stack=s)
            far_f = sb("far_f", [P, 4, 2, 4], stack=s)
            att = sb("att", [P, 2, TB, SEQ], stack=s)
            reset = sb("reset", [P, SEQ], stack=s)
            far_g = sb("far_g", [P, 2, NSEG], stack=s)
            square = sb("square", [P, 2, SEQ], stack=s)
        with ExitStack() as s:
            o_hi, o_lo = (sb(n, [P, 8, SEQ], F32R, s) for n in ("o_hi", "o_lo"))
            m_hi, m_lo = (sb(n, [P, KT, SEQ], F32R, s) for n in ("m_hi", "m_lo"))
            g_b = sb("g_b", [P, 4, SEQ], stack=s)
            mix = sb("mix", [P, 2, SEQ], stack=s)
        with ExitStack() as s:
            y_sb = sb("y_sb", [P, TB, D_MODEL], stack=s)
        sb("over", [P, U1 // 4])
        with ExitStack() as s:
            v_a = sb("v_a", [P, TB, D_A], stack=s)
            gate_a = sb("gate_a", [P, KT, SEQ], stack=s)
        with ExitStack() as s:
            hot_sb, table = sb("hot_sb", [BUCKETS, T5W], stack=s), sb("table", [HEADS_B, T5W], stack=s)
            rel_sb = sb("rel_sb", [BUCKETS, HEADS_B], stack=s)
            sb("under", [P, 2048 - 2 * T5W - HEADS_B], stack=s)
            x_raw = sb("x_raw", [P, KT, SEQ], stack=s)
        with ExitStack() as s:
            ln_gb = sb("ln_gb", [P, 2, D_MODEL], stack=s)
            x_res = sb("x_res", [P, TB, D_MODEL], stack=s)

        ps = [ctx.enter_context(nc.psum_tensor(f"bank{i}", [P, 512], F32)) for i in range(8)]
        proj_bank, log_bank, turn_bank, out_bank = ps[0:2], ps[2:4], ps[4:6], ps[6:8]
        up_bank = log_bank + turn_bank
        y_bank = [out_bank + proj_bank, log_bank + turn_bank]
        t5_rep = nc.dram_tensor("t5_rep", [P, HEADS_B, T5W], F32).ap()

        x_in = [sem(f"x_in{k}") for k in range(KT)]
        w_in = [[sem(f"w_in{j}_{a}") for a in range(2)] for j in range(2)]
        early_in = sem("early_in")
        k_hi_done, q_hi_done, wi_done, kiwi_out, k_twice = (
            sem(n) for n in ("k_hi_done", "q_hi_done", "wi_done", "kiwi_out", "k_twice"))
        consts_in, table_in, rep_out, t5_in = sem("consts_in"), sem("table_in"), sem("rep_out"), sem("t5_in")
        ln_in = sem("ln_in")
        res_in = [sem(f"res_in{t}") for t in range(TB)]
        y_out = sem("y_out")
        table_full, table_done = sem("table_full"), sem("table_done")
        pool_set, bias_q_done = sem("pool_set"), sem("bias_q_done")
        lb_step, lb_exp, lb_log, dve_step = (sem(n) for n in ("lb_step", "lb_exp", "lb_log", "dve_step"))
        x_hi_done, x_lo_done = sem("x_hi_done"), sem("x_lo_done")
        hi_done, lo_done = sem("hi_done"), sem("lo_done")
        part_done = sem("part_done")
        proj_out = [sem(f"proj_out{j}") for j in range(2)]
        log_full, log_out = sem("log_full"), [sem(f"log_out{j}") for j in range(2)]
        turn_full, turn_out = sem("turn_full"), [sem(f"turn_out{j}") for j in range(2)]
        pv_done, recur_done = sem("pv_done"), sem("recur_done")
        out_out = [sem(f"out_out{j}") for j in range(2)]
        up_out = [sem(f"up_out{j}") for j in range(4)]
        w_idx_done, relu_used, pen_done = sem("w_idx_done"), sem("relu_used"), sem("pen_done")
        logit_pre, exp_done, rcp_done = sem("logit_pre"), sem("exp_done"), sem("rcp_done")
        z_sig, gate_a_done = sem("z_sig"), sem("gate_a_done")
        f_dve, f_act, cum_done, k_done = (sem(n) for n in ("forget_dve", "forget_act", "cum_done", "k_done"))
        seg_decay, rl_done, near_done = sem("seg_decay"), sem("rl_done"), sem("near_done")
        reset_set, far_f_step, far_f_done, far_done = (sem(n) for n in ("reset_set", "far_f_step", "far_f_done", "far_done"))
        dist_pool, dist_dve = sem("dist_pool"), sem("dist_dve")
        fac_done, qk_done = sem("fac_done"), sem("qk_done")
        sq_done, rms_done, branch_a = (sem(n) for n in ("sq_done", "rms_done", "branch_a"))
        o_hi_done, o_lo_done = sem("o_hi_done"), sem("o_lo_done")
        mix_done, m_hi_done, m_lo_done = (sem(n) for n in ("mix_done", "m_hi_done", "m_lo_done"))
        y_full, y_aggr = sem("y_full"), sem("y_aggr")
        ln_log, ln_rstd, y_done = sem("ln_log"), sem("ln_rstd"), sem("y_done")

        rounds = topk_rounds()

        def unit_width(u):
            return WKI if u < NMAIN and UNITS[u] == "kiwi" else UW

        def raw(u):
            w = unit_width(u)
            return w_raw[:, u % 2, 0:KT * w].rearrange("p (k n) -> p k n", k=KT)

        def split_target(u, over_x, ring):
            if NMAIN <= u < NMAIN + 2:
                c = (u - NMAIN) * UW
                return over_x[:, :, c:c + UW]
            return ring[:, u % 2, :, 0:unit_width(u)]

        def wait_split_target(eng, u):
            gb3, up2, up3 = (UNITS.index(n) for n in ("gb3", "up2", "up3"))
            last = {NMAIN: gb3, NMAIN + 1: gb3, NMAIN + 2: up2, NMAIN + 3: up3}.get(u, u - 2)
            if last >= 0:
                eng.wait_ge(part_done, 2 * last + (2 if last else 1))

        def wait_proj_out(eng, name, i):
            eng.wait_ge(proj_out[i], NPROJ[UNITS.index(name)] + 1)

        def wait_log_out(eng, idx):
            eng.wait_ge(log_out[idx % 2], idx // 2 + 1)

        def wait_turn_out(eng, idx):
            eng.wait_ge(turn_out[idx % 2], idx // 2 + 1)

        def item_turn(i):
            return TURNS.index((0, i))

        def group_turn(n):
            return TURNS.index((1, n))

        def wait_tree_out(eng, p):
            wait_log_out(eng, TREE0 + NTREE * (p + 1) - 2)
            wait_log_out(eng, TREE0 + NTREE * (p + 1) - 1)

        def wait_lvl_multiplied(eng, p, lv):
            eng.wait_ge(log_full, TREE0 + NTREE * p + TREE.index(("lv", lv)) + 1)

        def items_at(q):
            return [i for i in range(len(ITEMS)) if Q_ITEM[i] == q]

        def groups_at(q):
            return [n for n in range(len(GROUPS)) if Q_GROUP[n] == q]

        def rows(h):
            return slice(64 * (h % 2), 64 * (h % 2) + 64)

        def queries(b):
            return slice(b * P, b * P + P)

        def tree_at(q):
            return [(p, n) for p in range(2) for n in range(NTREE) if Q_TREE[p] + n // 2 == q]

        def flat(ap):
            return ap.rearrange("p a t -> p (a t)")

        def groups(tile, h):
            return tile.rearrange("p (n w) -> p n w", w=2 * h)

        def strided(base, dims):
            return bass.AP(base.tensor, base.offset, [list(base.ap[0])] + dims)

        def att_blocks(a, h=None):
            step = SEQ + P
            if h is None:
                return strided(att[:, a, 0, 0:P], [[step, TB], [1, P]])
            return strided(att[:, a, 0, h:P], [[step, TB], [2 * h, 64 // h], [1, h]])

        def z_part(n):
            return (z_b if n < 4 else z_a)[:, n % 4, :]

        def wait_dist(eng, p, lv):
            if lv % 2:
                eng.wait_ge(dist_dve, 3 * p + lv // 2 + 1)
            else:
                eng.wait_ge(dist_pool, 4 * p + lv // 2 + 1)

        def part_out_at(q):
            u, i = (q // 4 - 1, 1) if q % 4 == 0 else (q // 4, 0)
            if u < 0 or q % 2 or not UNITS[u][2:].isdigit():
                return None
            return UNITS[u][:2], 2 * int(UNITS[u][2]) + i

        def merged_at(q):
            part = part_out_at(q)
            return part[1] if part and part[0] == "up" else None

        def level_distance(engine, p, lv):
            h = LEVELS[lv]
            c = groups(flat(cum[:, 2 * p:2 * p + 2, :]), h)
            return engine.tensor_tensor(groups(dec[:, lv % 2, :], h), c,
                                        c[:, :, h - 1:h].broadcast_to([P, 2 * SEQ // (2 * h), 2 * h]), ALU.subtract)

        block = ctx.enter_context(nc.Block())

        @block.sync
        def _(sp):
            for k in range(KT):
                sp.dma_start(x_raw[:, k, :], x_t[:, k, :]).then_inc(x_in[k], 16)
            for u in range(1, NU):
                if u >= 2:
                    sp.wait_ge(lo_done, 4 * (u - 1))
                unit = w_units[u - 1]
                for a in range(2):
                    c = slice(a * KT // 2 * UW, (a + 1) * KT // 2 * UW)
                    sp.dma_start(w_raw[:, u % 2, c], unit[:, c]).then_inc(w_in[u % 2][a], 16)
                if u == 3:
                    sp.wait_ge(table_done, 2)
                    sp.dma_start(t5_rep.rearrange("p h d -> h p d"),
                                 table[:].unsqueeze(1).broadcast_to([HEADS_B, P, T5W])).then_inc(rep_out, 16)
                if u == 5:
                    sp.wait_ge(rep_out, 16)
                    skewed = bass.AP(t5_rep.tensor, t5_rep.offset + P - 1,
                                     [[HEADS_B * T5W - 1, P], [T5W, HEADS_B], [1, SEQ]])
                    sp.dma_start(t5[:], skewed).then_inc(t5_in, 16)
            sp.wait_ge(recur_done, HEADS_A)
            sp.dma_start(ln_gb[:, 0, :], ln_g.partition_broadcast(P)).then_inc(ln_in, 16)
            sp.dma_start(ln_gb[:, 1, :], ln_b.partition_broadcast(P)).then_inc(ln_in, 16)
            sp.wait_ge(mix_done, KT)
            for t in range(TB):
                sp.dma_start(x_res[:, t, :], x_tok[t]).then_inc(res_in[t], 16)
            for t in range(TB):
                for half in range(2):
                    c = slice(half * 512, half * 512 + 512)
                    sp.wait_ge(y_done, 2 * t + half + 1)
                    sp.dma_start(out[t][:, c], y_sb[:, t, c]).then_inc(y_out, 16)
            sp.wait_ge(y_out, 16 * 2 * TB)

        @block.tensor
        def _(pe):
            def split_product(dst, a_hi, a_lo, b_hi, b_lo, first, last):
                nc.tensor.matmul(dst, a_hi, b_hi, start=first, stop=False)
                nc.tensor.matmul(dst, a_hi, b_lo, start=False, stop=False)
                return nc.tensor.matmul(dst, a_lo, b_hi, start=False, stop=last)

            def wait_piece(u, k):
                if k % 2 == 0:
                    pe.wait_ge(lo_done, 4 * u + k // 2 + 1)
                if u == 0:
                    pe.wait_ge(x_lo_done, k + 1)

            def wait_bank(u, i):
                if u == 1 and i == 1:
                    pe.wait_ge(kiwi_out, 1)
                if NPROJ[u]:
                    pe.wait_ge(proj_out[i], NPROJ[u])

            def quarter_f(u, i, j):
                bank = proj_bank[1 if UNITS[u] == "kiwi" else i]
                if j == 0:
                    wait_bank(u, i)
                c = slice(i * P, min(i * P + P, unit_width(u)))
                for k in range(4 * j, 4 * j + 4):
                    if i == 0:
                        wait_piece(u, k)
                    mm = split_product(bank[0:c.stop - c.start, :], w_hi[:, u % 2, k, c], w_lo[:, u % 2, k, c],
                                       x_hi[:, k, :], x_lo[:, k, :], k == 0, k == KT - 1)
                if j == 1:
                    mm.then_inc(part_done, 1)

            def quarter_t(u, i, j):
                if j == 0:
                    wait_bank(u, i)
                tk = queries(2 * i + j)
                for k in range(KT):
                    if i == 0 and j == 0:
                        wait_piece(u, k)
                    mm = split_product(proj_bank[i][:, j * UW:(j + 1) * UW], x_hi[:, k, tk], x_lo[:, k, tk],
                                       w_hi[:, u % 2, k, :], w_lo[:, u % 2, k, :], k == 0, k == KT - 1)
                if j == 1:
                    mm.then_inc(part_done, 1)

            def turn_wi():
                pe.wait_ge(wi_done, 1)
                pe.wait_ge(early_in, 32)
                for t in range(TB):
                    mm = nc.tensor.transpose(turn_bank[0][:, t * HEADS_I:(t + 1) * HEADS_I], wi_t[:, queries(t)],
                                             id_sb[64:WKI, 64:WKI])
                mm.then_inc(part_done, 1)

            def quarter_up(u, i, j):
                fill = 2 * (2 * int(UNITS[u][2]) + i) + j
                if fill < 2:
                    wait_log_out(pe, TREE0 + 2 * NTREE - 2 + fill)
                    pe.wait_ge(o_hi_done, 2 * (j + 1))
                    pe.wait_ge(o_lo_done, 2 * (j + 1))
                elif fill < 4:
                    wait_turn_out(pe, len(TURNS) + HEADS_A - 4 + fill)
                else:
                    pe.wait_ge(up_out[fill % 4], fill // 4)
                c = slice(i * P, i * P + P)
                for k in range(4 * j, 4 * j + 4):
                    if i == 0:
                        wait_piece(u, k)
                    mm = split_product(up_bank[fill % 4][:], w_hi[:, u % 2, k, c], w_lo[:, u % 2, k, c],
                                       o_hi[:, k, :], o_lo[:, k, :], k % 4 == 0, k % 4 == 3)
                if j == 1:
                    mm.then_inc(part_done, 1)

            def log_slot(idx):
                if idx >= 2:
                    wait_log_out(pe, idx - 2)
                return log_bank[idx % 2]

            def dots(i):
                b, h = DOTS[i]
                dst = log_slot(i)
                if i == 0:
                    for name in ("qi0", "qi1"):
                        wait_proj_out(pe, name, 0)
                        wait_proj_out(pe, name, 1)
                    pe.wait_ge(k_twice, 2)
                n = (b + 1) * P
                nc.tensor.matmul(dst[:, 0:n], q_hl[:, h, queries(b)], k_hi2[:, 0:n], start=True, stop=False)
                nc.tensor.matmul(dst[:, 0:n], q_hl[rows(h), h, queries(b)], k_lo2[rows(h), 0:n],
                                 start=False, stop=True).then_inc(log_full, 1)

            def scores(i):
                b, h = ITEMS[i]
                dst = log_slot(QK0 + i)
                if b == 0 and h % 2 == 0:
                    wait_proj_out(pe, f"qb{h // 4}", h // 2 % 2)
                    wait_proj_out(pe, f"kb{h // 4}", h // 2 % 2)
                n = (b + 1) * P
                nc.tensor.matmul(dst[:, 0:n], q_b[rows(h), h // 2, queries(b)], k_b[rows(h), h // 2, 0:n],
                                 start=True, stop=True).then_inc(log_full, 1)

            def turn_probs(i):
                b, h = ITEMS[i]
                n = item_turn(i)
                pe.wait_ge(exp_done, i + 1)
                if n >= 2:
                    wait_turn_out(pe, n - 2)
                for c in range(b + 1):
                    mm = nc.tensor.transpose(turn_bank[n % 2][:, queries(c)], prob[:, i % 2, queries(c)], id_sb[:])
                mm.then_inc(turn_full, 1)

            def attend(i):
                b, h = ITEMS[i]
                n = i // 4
                wait_turn_out(pe, item_turn(i))
                if b == 0 and h % 4 == 0:
                    wait_proj_out(pe, f"vb{h // 4}", 0)
                    wait_proj_out(pe, f"vb{h // 4}", 1)
                if h % 4 == 0 and n >= 2:
                    pe.wait_ge(out_out[n % 2], n // 2)
                for c in range(b + 1):
                    mm = nc.tensor.matmul(out_bank[n % 2][:, h % 4 * 64:h % 4 * 64 + 64], prob_t[:, i % 2, queries(c)],
                                          v_b[:, c, h * 64:h * 64 + 64], start=(c == 0), stop=(c == b),
                                          skip_group_check=True)
                mm.then_inc(pv_done, 1)

            def turn_group(n):
                m = group_turn(n)
                pe.wait_ge(out_out[n % 2], n // 2 + 1)
                wait_turn_out(pe, m - 2)
                for c in range(2):
                    mm = nc.tensor.transpose(turn_bank[m % 2][:, queries(c)], o_tok[:, n % 2, queries(c)], id_sb[:])
                mm.then_inc(turn_full, 1)

            def tree(p, n):
                kind, m = TREE[n]
                idx = TREE0 + NTREE * p + n
                dst = log_slot(idx)
                if kind == "diag":
                    pe.wait_ge(k_done, 2 * (p + 1))
                    for t in range(TB):
                        mm = nc.tensor.matmul(dst[:, queries(t)], k_a[:, m, queries(t)],
                                              q_a[:, 2 * p + m, queries(t)], start=True, stop=True)
                elif kind == "lv":
                    if m == 0:
                        pe.wait_ge(near_done, 2 * p + 2)
                    else:
                        pe.wait_ge(qk_done, 2 * (6 * p + m))
                    for a in range(2):
                        for t in range(TB):
                            c = (a * TB + t) * 64
                            if m == 0:
                                parts = ((k_l[:, a, t * P:t * P + 64], q_r[:, a, t * P + 64:t * P + P], 0, 0),)
                            else:
                                key = k_c[:, (m - 1) % 2, a * SEQ + t * P:a * SEQ + t * P + P]
                                query = q_c[:, (m - 1) % 2, a, t * 64:t * 64 + 64]
                                parts = ((key, query, 0, 0),)
                                if m == 1:
                                    parts = ((key[:, 0:32], query[:, 0:32], 0, 0),
                                             (key[:, 64:96], query[:, 32:64], 64, 32))
                            for keys, later, row, col in parts:
                                mm = nc.tensor.matmul(dst[row:row + keys.shape[-1], c + col:c + col + later.shape[-1]],
                                                      keys, later, start=True, stop=True)
                elif kind == "128":
                    pe.wait_ge(far_done, 6 * p + 4)
                    for a in range(2):
                        for t in range(2):
                            mm = nc.tensor.matmul(dst[:, queries(2 * a + t)], far[:, 0, a, queries(t)],
                                                  far[:, 1, a, queries(t)], start=True, stop=True)
                else:
                    pe.wait_ge(far_done, 6 * p + 6)
                    for t in range(2):
                        mm = nc.tensor.matmul(dst[:, t * 256:t * 256 + 256], far[:, 2, m, queries(t)],
                                              far[:, 3, m, :], start=True, stop=True)
                mm.then_inc(log_full, 1)

            def recur(h):
                bank = out_bank[h % 2]
                pe.wait_ge(out_out[h % 2], len(GROUPS) // 2 + h // 2)
                wait_tree_out(pe, h // 2)
                if h == 0:
                    wait_proj_out(pe, "ia1", 0)
                    wait_proj_out(pe, "ia1", 1)
                for s in range(TB):
                    mm = nc.tensor.matmul(bank[:, s * P:SEQ], v_a[:, s, queries(h)], att[:, h % 2, s, s * P:SEQ],
                                          start=(s == 0), stop=(s == TB - 1), skip_group_check=True)
                mm.then_inc(recur_done, 1)

            def mean_square(h):
                i = len(TURNS) + h
                pe.wait_ge(sq_done, h + 1)
                wait_turn_out(pe, i - 2)
                nc.tensor.matmul(turn_bank[i % 2][:], ones_sb[:], square[:, h % 2, :], start=True,
                                 stop=True).then_inc(turn_full, 1)

            def side(q):
                if q == 4:
                    turn_wi()
                for i in range(2 * (q - Q_DOTS), 2 * (q - Q_DOTS) + 2):
                    if 0 <= i < len(DOTS):
                        dots(i)
                for i in items_at(q - 1):
                    turn_probs(i)
                for n in groups_at(q):
                    turn_group(n)
                for i in items_at(q):
                    scores(i)
                for i in items_at(q - 2):
                    attend(i)
                for p, n in tree_at(q):
                    tree(p, n)
                for h in range(HEADS_A):
                    if q == Q_TREE[h // 2] + 7:
                        recur(h)
                    if q == Q_TREE[h // 2] + 8:
                        mean_square(h)

            def t5_table():
                pe.wait_ge(table_in, 32)
                pe.wait_ge(w_idx_done, 1)
                for c in range(2):
                    mm = nc.tensor.matmul(turn_bank[c][0:HEADS_B, 0:T5W // 2], rel_sb[:],
                                          hot_sb[:, c * T5W // 2:(c + 1) * T5W // 2], start=True, stop=True)
                mm.then_inc(table_full, 1)

            for u, name in enumerate(UNITS):
                for q in range(4):
                    i, j = q // 2, q % 2
                    if name.startswith("up"):
                        quarter_up(u, i, j)
                    elif name[:2] in ("vb", "ia"):
                        quarter_t(u, i, j)
                    elif name != "kiwi" or i == 0:
                        quarter_f(u, i, j)
                    if (u, q) == (1, 3):
                        t5_table()
                        pe.wait_ge(pool_set, 1)
                    side(4 * u + q)
            for half in range(2):
                pe.wait_ge(lo_done, 4 * (NMAIN + 2 * half + 2))
                for t in range(TB):
                    bank = y_bank[half][t]
                    if half == 0 and t < 2:
                        pe.wait_ge(out_out[t], len(GROUPS) // 2 + 2)
                    elif half == 0:
                        pe.wait_ge(proj_out[t - 2], NPROJ[NMAIN])
                    else:
                        pe.wait_ge(up_out[t], 2 * KT // 4)
                    for k in range(KT):
                        if half == 0 and t == 0:
                            pe.wait_ge(m_lo_done, k + 1)
                        m = m_hi[:, k, queries(t)], m_lo[:, k, queries(t)]
                        if half == 0:
                            mm = split_product(bank[:], *m, x_hi[:, k, :], x_lo[:, k, :], k == 0, k == KT - 1)
                        else:
                            mm = split_product(bank[:].rearrange("p (s n) -> p s n", s=2), *m,
                                               w_hi[:, :, k, :], w_lo[:, :, k, :], k == 0, k == KT - 1)
                    mm.then_inc(y_full, 1)

        @block.scalar
        def _(act):
            def round_tiles(u, k):
                nc.scalar.activation(split_target(u, x_hi, w_hi)[:, k, :], raw(u)[:, k, :],
                                     ACT.Copy).then_inc(hi_done, 1)

            def split_hi(u, a):
                if u == 0:
                    act.wait_ge(w_in[0][0], 16)
                else:
                    act.wait_ge(w_in[u % 2][a], 16 * (u // 2 + (a == 0 or u % 2)))
                if a == 0:
                    wait_split_target(act, u)
                round_tiles(u, slice(4 * a, 4 * a + 4))

            def leave_bank(u, i):
                name = UNITS[u]
                kind = name[:2]
                if kind in ("vb", "ia", "up") or (name == "kiwi" and i == 1):
                    return
                act.wait_ge(part_done, 2 * u + i + 1)
                tile = 0 if name == "kiwi" else 2 * int(name[2]) + i
                c = 2 * u + i
                func, b_col, scale = ACT.Identity, bias[:, c:c + 1], 1.0
                if kind == "ki":
                    nc.scalar.activation(k_hi2[0:64, :], proj_bank[1][0:64, :], ACT.Identity,
                                         bias=bias[0:64, c:c + 1]).then_inc(k_hi_done, 1)
                    nc.scalar.activation(wi_t, proj_bank[1][64:WKI, :], ACT.Identity,
                                         bias=bias[64:WKI, c:c + 1]).then_inc(wi_done, 1)
                    nc.scalar.preload_act_table_set("sigmoid_and_others")
                    return
                elif kind == "qi":
                    for h in (2 * tile, 2 * tile + 1):
                        nc.scalar.activation(q_hl[rows(h), h, :], proj_bank[i][rows(h), :], ACT.Identity,
                                             bias=bias[rows(h), c:c + 1]).then_inc(q_hi_done, 1)
                    return
                elif kind == "qb":
                    dst, b_col, scale = q_b[:, tile, :], bias_q[:, c:c + 1], QSCALE
                    act.wait_ge(bias_q_done, 1)
                elif kind == "kb":
                    dst = k_b[:, tile, :]
                elif kind in ("zb", "za"):
                    n = 2 * (u - UNITS.index("zb0")) + i
                    if n == 0:
                        act.wait_ge(x_lo_done, KT)
                    nc.scalar.activation(gate_a[:, n, :], proj_bank[i][:], ACT.Sigmoid, bias=b_col).then_inc(z_sig, 1)
                    return
                elif kind in ("fa", "qa"):
                    dst = (cum if kind == "fa" else q_a)[:, tile, :]
                    if name == "fa0" and i == 0:
                        act.wait_ge(pen_done, TB - 1)
                elif kind == "ga":
                    dst = gate_a[:, tile, :]
                    if tile == 0:
                        wait_proj_out(act, "za1", 0)
                        wait_proj_out(act, "za1", 1)
                else:
                    dst, func = g_b[:, tile % 4, :], ACT.Sigmoid
                    if tile == 0:
                        act.wait_ge(branch_a, HEADS_A)
                    elif tile >= 4:
                        act.wait_ge(mix_done, tile - 3)
                nc.scalar.activation(dst, proj_bank[i][:], func, bias=b_col, scale=scale).then_inc(proj_out[i], 1)

            def relu(i):
                b, h = DOTS[i]
                act.wait_ge(log_full, i + 1)
                if i >= 2:
                    act.wait_ge(relu_used, i - 1)
                n = (b + 1) * P
                nc.scalar.activation(relus[:, i % 2, 0:n], log_bank[i % 2][:, 0:n], ACT.Relu,
                                     scale=QSCALE).then_inc(log_out[i % 2], 1)

            def softmax_exp(i):
                b, h = ITEMS[i]
                wait_log_out(act, QK0 + i)
                if i >= 2:
                    act.wait_ge(turn_full, item_turn(i - 2) + 1)
                if i >= 8:
                    act.wait_ge(rcp_done, i // 4 - 1)
                n = (b + 1) * P
                nc.scalar.activation(prob[:, i % 2, 0:n], logit[:, i % 2, 0:n], ACT.Exp,
                                     bias=nmax[:, i % 2:i % 2 + 1], scale=-1.0,
                                     accum_out=prob_sum[:, i // 4 % 2, h % 4:h % 4 + 1]).then_inc(exp_done, 1)

            def forget(p, n):
                act.wait_ge(f_dve, 4 * p + (1, 1, 2, 2, 4)[n])
                if n in (1, 3):
                    act.wait_ge(f_act, 5 * p + (1, 0, 3)[n - 1])
                if n == 0:
                    if p == 0:
                        act.wait_ge(lb_step, 4)
                        nc.scalar.activation(lb[:, 6, :], lb[:, 5, :], ACT.Ln, bias=1.0, scale=-1.0).then_inc(lb_log, 1)
                    nc.scalar.activation(dec[:, 0, :], dec[:, 0, :], ACT.Exp).then_inc(f_act, 1)
                elif n == 1:
                    nc.scalar.activation(dec[:, 0, :], dec[:, 0, :], ACT.Ln, bias=1.0).then_inc(f_act, 1)
                elif n == 2:
                    nc.scalar.activation(dec[:, 1, :], dec[:, 1, :], ACT.Exp, scale=-1.0).then_inc(f_act, 1)
                elif n == 3:
                    act.wait_ge(lb_log, 1)
                    for a in range(2):
                        c = slice(a * SEQ, a * SEQ + SEQ)
                        nc.scalar.activation(dec[:, 1, c], dec[:, 1, c], ACT.Ln, bias=1.0,
                                             scale=lb[:, 5, 2 * p + a:2 * p + a + 1]).then_inc(f_act, 1)
                else:
                    if p:
                        act.wait_ge(log_full, TREE0 + NTREE)
                        act.wait_ge(qk_done, 12)
                    for a in range(2):
                        nc.scalar.activation(k_a[:, a, :], k_c[:, 1, a * SEQ:a * SEQ + SEQ], ACT.Exp,
                                             bias=lb[:, 6, 2 * p + a:2 * p + a + 1]).then_inc(k_done, 1)

            def near_factors(p):
                act.wait_ge(cum_done, 2 * (p + 1))
                cp = cum[:, 2 * p:2 * p + 2, :]
                if p:
                    act.wait_ge(far_f_done, p)
                    wait_lvl_multiplied(act, 0, 0)
                    act.wait_ge(far_done, 6)
                nc.scalar.activation(far_g[:], cp[:, :, SEG - 1::SEG], ACT.Exp).then_inc(seg_decay, 1)
                nc.scalar.activation(q_r[:], cp, ACT.Exp).then_inc(rl_done, 1)
                wait_dist(act, p, 0)
                nc.scalar.activation(flat(k_l[:]), dec[:, 0, :], ACT.Exp).then_inc(rl_done, 1)

            def level_factors(p, lv):
                wait_dist(act, p, lv)
                h = LEVELS[lv]
                v = groups(dec[:, lv % 2, :], h)
                nc.scalar.activation(v[:, :, h:2 * h], v[:, :, h:2 * h], ACT.Exp).then_inc(fac_done, 1)
                nc.scalar.activation(v[:, :, 0:h], v[:, :, 0:h], ACT.Exp, scale=-1.0).then_inc(fac_done, 1)

            def tree_copy(p, n):
                kind, m = TREE[n]
                if kind not in ("128", "256"):
                    return
                idx = TREE0 + NTREE * p + n
                act.wait_ge(log_full, idx + 1)
                if p:
                    act.wait_ge(recur_done, 2)
                bank = log_bank[idx % 2]
                if kind == "128":
                    for a in range(2):
                        ins = nc.scalar.activation(
                            strided(att[:, a, 0, P:2 * P], [[2 * (SEQ + P), 2], [1, P]]),
                            bank[:, 2 * a * P:2 * a * P + 2 * P].rearrange("p (t n) -> p t n", t=2), ACT.Copy)
                else:
                    ins = nc.scalar.activation(att[:, m, 0:2, 2 * P:SEQ],
                                               bank[:].rearrange("p (t n) -> p t n", t=2), ACT.Copy)
                ins.then_inc(log_out[idx % 2], 1)

            def squares(h):
                act.wait_ge(recur_done, h + 1)
                if h >= 2:
                    act.wait_ge(branch_a, h - 1)
                nc.scalar.activation(square[:, h % 2, :], out_bank[h % 2][:], ACT.Square).then_inc(sq_done, 1)

            def inverse_rms(h):
                i = len(TURNS) + h
                act.wait_ge(turn_full, i + 1)
                nc.scalar.activation(square[:, h % 2, :], turn_bank[i % 2][:], ACT.Ln,
                                     bias=eps[:, 0:1]).then_inc(turn_out[i % 2], 1)
                wait_turn_out(act, i)
                nc.scalar.activation(square[:, h % 2, :], square[:, h % 2, :], ACT.Exp,
                                     scale=-0.5).then_inc(rms_done, 1)

            def round_merged(m):
                act.wait_ge(mix_done, m + 1)
                nc.scalar.activation(m_hi[:, m, :], mix[:, m % 2, :], ACT.Copy).then_inc(m_hi_done, 1)

            def side(q):
                for i in range(2 * (q - Q_DOTS), 2 * (q - Q_DOTS) + 2):
                    if 0 <= i < len(DOTS):
                        relu(i)
                for i in items_at(q):
                    softmax_exp(i)
                for p, n in tree_at(q + 1):
                    if TREE[n][0] == "lv" and TREE[n][1]:
                        level_factors(p, TREE[n][1])
                for p in range(2):
                    at = q - Q_PREP[p]
                    if at == 0:
                        forget(p, 0)
                        forget(p, 1)
                    if at == 1:
                        forget(p, 2)
                        forget(p, 3)
                    if at == 2:
                        forget(p, 4)
                        near_factors(p)
                for p, n in tree_at(q):
                    tree_copy(p, n)
                for h in range(HEADS_A):
                    if q == Q_TREE[h // 2] + 7:
                        squares(h)
                    if q == Q_TREE[h // 2] + 8:
                        inverse_rms(h)

            act.dma_start(w_raw[:, 0, 0:KT * WKI], w_kiwi).then_inc(w_in[0][0], 16)
            act.dma_start(bias[:], b_cols).then_inc(early_in, 16)
            act.dma_start(id_sb[:], ident).then_inc(early_in, 16)
            split_hi(0, 0)
            split_hi(0, 1)
            act.dma_start(rel_sb[:], rel_bias).then_inc(table_in, 16)
            act.dma_start(hot_sb[:], one_hot).then_inc(table_in, 16)
            for dst, src in ((lb[:, 0, :], lb_cols), (g_a[:], g_cols), (causal_sb[:], causal), (masks_sb[:], tree_masks),
                             (bias_ia[:], b_ia.partition_broadcast(P)), (bias_vb[:], b_vb.partition_broadcast(P))):
                act.dma_start(dst, src).then_inc(consts_in, 16)
            split_hi(1, 0)
            split_hi(1, 1)
            act.wait_ge(pool_set, 1)
            act.wait_ge(early_in, 32)
            for q in range(4 * NMAIN):
                u, j = q // 4, q % 4
                if j == 0 and u >= 1:
                    leave_bank(u - 1, 1)
                elif j == 2:
                    leave_bank(u, 0)
                if u >= 1 and j < 2:
                    split_hi(u + 1 + (u == NMAIN - 1), j)
                elif u >= NMAIN - 2:
                    split_hi(u + 2 + (u == NMAIN - 1), j - 2)
                if q == Q_ITEM[0] - 2:
                    nc.scalar.preload_act_table_set("natural_log_exp_and_others")
                    act.wait_ge(lb_step, 1)
                    nc.scalar.activation(lb[:, 2, :], lb[:, 1, :], ACT.Exp).then_inc(lb_exp, 1)
                if q == Q_MERGE:
                    nc.scalar.preload_act_table_set("sigmoid_and_others")
                side(q)
                if Q_MERGE <= q < Q_MERGE + 4:
                    act.wait_ge(branch_a, HEADS_A)
                    z = z_a if j < 2 else z_b
                    nc.scalar.activation(flat(o_hi[:, 2 * j:2 * j + 2, :]), flat(z[:, 2 * j % 4:2 * j % 4 + 2, :]),
                                         ACT.Copy).then_inc(o_hi_done, 1)
                if Q_MERGE + 4 <= q < Q_MERGE + 8:
                    if q == Q_MERGE + 4:
                        wait_proj_out(act, "ga3", 0)
                        wait_proj_out(act, "ga3", 1)
                    g = flat(gate_a[:, 2 * j:2 * j + 2, :])
                    nc.scalar.activation(g, g, ACT.Sigmoid).then_inc(gate_a_done, 1)
                m = merged_at(q)
                if m is not None:
                    round_merged(m)
            round_merged(KT - 1)
            nc.scalar.preload_act_table_set("natural_log_exp_and_others")
            split_hi(NMAIN + 3, 0)
            split_hi(NMAIN + 3, 1)
            for t in range(TB):
                act.wait_ge(y_aggr, t + 1)
                nc.scalar.activation(rstd[:, t, 0:1], aggr[:, t, 1:2], ACT.Ln, bias=eps[:, 1:2]).then_inc(ln_log, 1)
                act.wait_ge(ln_log, t + 1)
                nc.scalar.activation(rstd[:, t, 1:2], rstd[:, t, 0:1], ACT.Exp, scale=-0.5).then_inc(ln_rstd, 1)

        @block.vector
        def _(dve):
            steps = [0]

            def link(ins):
                steps[0] += 1
                ins.then_inc(dve_step, 1)
                dve.wait_ge(dve_step, steps[0])

            def split_x(k):
                dve.wait_ge(x_in[k], 16)
                nc.vector.tensor_copy(x_hi[:, k, :], x_raw[:, k, :]).then_inc(x_hi_done, 1)
                dve.wait_ge(x_hi_done, k + 1)
                nc.vector.tensor_tensor(x_lo[:, k, :], x_raw[:, k, :], x_hi[:, k, :].bitcast(F32),
                                        ALU.subtract).then_inc(x_lo_done, 1)

            def lower_bound():
                nc.vector.tensor_tensor(lb[:, 1, :], lb[:, 0, :], lb[:, 0, :], ALU.subtract).then_inc(lb_step, 1)
                dve.wait_ge(lb_exp, 1)
                nc.vector.reciprocal(lb[:, 3, :], lb[:, 2, :]).then_inc(lb_step, 1)
                dve.wait_ge(lb_step, 2)
                nc.vector.tensor_tensor(lb[:, 4, :], lb[:, 2, :], lb[:, 3, :], ALU.mult).then_inc(lb_step, 1)
                dve.wait_ge(lb_step, 3)
                nc.vector.tensor_tensor(lb[:, 5, :], lb[:, 4, :], lb[:, 4, :], ALU.subtract).then_inc(lb_step, 1)
                dve.wait_ge(lb_step, 4)

            def leave_bank(u, i):
                name = UNITS[u]
                kind = name[:2]
                if name == "kiwi" and i == 0:
                    dve.wait_ge(k_hi_done, 1)
                    dve.wait_ge(wi_done, 1)
                    nc.vector.scalar_tensor_tensor(out=k_lo2[0:64, :], in0=proj_bank[1][0:64, :],
                                                   scalar=bias[0:64, 2 * u:2 * u + 1], in1=k_hi2[0:64, :].bitcast(F32),
                                                   op0=ALU.add, op1=ALU.subtract).then_inc(kiwi_out, 1)
                elif kind == "qi":
                    c = 2 * u + i
                    for h in (4 * int(name[2]) + 2 * i, 4 * int(name[2]) + 2 * i + 1):
                        dve.wait_ge(q_hi_done, h + 1)
                        ins = nc.vector.scalar_tensor_tensor(
                            out=q_hl[rows(h + 1), h, :], in0=proj_bank[i][rows(h), :], scalar=bias[rows(h), c:c + 1],
                            in1=q_hl[rows(h), h, :].bitcast(F32), op0=ALU.add, op1=ALU.subtract)
                    ins.then_inc(proj_out[i], 1)
                elif kind in ("vb", "ia"):
                    n = int(name[2])
                    c = slice(n * UW, n * UW + UW)
                    if kind == "ia":
                        dve.wait_ge(rep_out, 16)
                    dve.wait_ge(part_done, 2 * u + i + 1)
                    row = (bias_vb if kind == "vb" else bias_ia)[:, c].unsqueeze(1).broadcast_to([P, 2, UW])
                    nc.vector.tensor_tensor((v_b if kind == "vb" else v_a)[:, 2 * i:2 * i + 2, c],
                                            proj_bank[i][:].rearrange("p (t n) -> p t n", t=2), row,
                                            ALU.add).then_inc(proj_out[i], 1)
                elif kind in ("zb", "za"):
                    n = 2 * (u - UNITS.index("zb0")) + i
                    dve.wait_ge(z_sig, n + 1)
                    nc.vector.scalar_tensor_tensor(out=z_part(n), in0=proj_bank[i][:],
                                                   scalar=bias[:, 2 * u + i:2 * u + i + 1], in1=gate_a[:, n, :],
                                                   op0=ALU.add, op1=ALU.mult).then_inc(proj_out[i], 1)
                elif name == "kiwi" and i == 1:
                    dve.wait_ge(part_done, 2 * u + 2)
                    nc.vector.tensor_scalar(
                        w_idx[:], turn_bank[0][:, 0:TB * HEADS_I].rearrange("p (t h) -> p t h", t=TB),
                        WSCALE, None, ALU.mult).then_inc(w_idx_done, 1)
                    dve.wait_ge(kiwi_out, 1)
                    nc.vector.tensor_copy(k_lo2[64:P, :], k_lo2[0:64, :]).then_inc(k_twice, 1)
                    nc.vector.tensor_copy(k_hi2[64:P, :], k_hi2[0:64, :]).then_inc(k_twice, 1)

            def add_score(i):
                b, h = DOTS[i]
                wait_log_out(dve, i)
                n = (b + 1) * P
                w = w_idx[:, b, h:h + 1]
                if i == 0:
                    dve.wait_ge(w_idx_done, 1)
                    dve.wait_ge(consts_in, 16 * N_CONSTS)
                if h == 0:
                    ins = nc.vector.tensor_scalar(score[b][:], relus[:, i % 2, 0:n], w, None, ALU.mult)
                else:
                    dve.wait_ge(relu_used, i)
                    ins = nc.vector.scalar_tensor_tensor(out=score[b][:], in0=relus[:, i % 2, 0:n], scalar=w,
                                                         in1=score[b][:], op0=ALU.mult, op1=ALU.add)
                ins.then_inc(relu_used, 1)
                if h == HEADS_I - 1:
                    dve.wait_ge(relu_used, i + 1)
                    diag = score[b][:, b * P:b * P + P]
                    link(nc.vector.tensor_tensor(diag, diag, causal_sb[:], ALU.add))

            def topk_round(b, r):
                link(nc.vector.max(best8[:], score[b][:]))
                link(nc.vector.match_replace(score[b][:], best8[:], score[b][:], TAKEN))
                if r == ROUNDS - 1:
                    nc.vector.tensor_scalar(pen[b][:], score[b][:], TAKEN, NEG, ALU.not_equal,
                                            ALU.mult).then_inc(pen_done, 1)

            def move_probs(i):
                b, h = ITEMS[i]
                m = item_turn(i)
                dve.wait_ge(turn_full, m + 1)
                if i >= 2:
                    dve.wait_ge(pv_done, i - 1)
                n = (b + 1) * P
                nc.vector.tensor_copy(prob_t[:, i % 2, 0:n], turn_bank[m % 2][:, 0:n]).then_inc(turn_out[m % 2], 1)

            def logits(i):
                b, h = ITEMS[i]
                dve.wait_ge(log_full, QK0 + i + 1)
                dve.wait_ge(logit_pre, i + 1)
                if i >= 2:
                    dve.wait_ge(exp_done, i - 1)
                n = (b + 1) * P
                lg = logit[:, i % 2, 0:n]
                nc.vector.tensor_tensor_reduce(out=lg, in0=log_bank[i % 2][:, 0:n], in1=lg, scale=-1.0, scalar=3e38,
                                               op0=ALU.add, op1=ALU.min,
                                               accum_out=nmax[:, i % 2:i % 2 + 1]).then_inc(log_out[i % 2], 1)

            def divide_group(n):
                dve.wait_ge(exp_done, 4 * n + 4)
                if n >= 2:
                    dve.wait_ge(out_out[n % 2], n // 2)
                    dve.wait_ge(turn_full, group_turn(n - 2) + 1)
                nc.vector.reciprocal(prob_rcp[:, n % 2, :], prob_sum[:, n % 2, :]).then_inc(rcp_done, 1)
                dve.wait_ge(rcp_done, n + 1)
                dve.wait_ge(pv_done, 4 * n + 4)
                nc.vector.tensor_tensor(o_tok[:, n % 2, :].rearrange("p (h d) -> p h d", h=4),
                                        out_bank[n % 2][:, 0:256].rearrange("p (h d) -> p h d", h=4),
                                        prob_rcp[:, n % 2, :].unsqueeze(2).broadcast_to([P, 4, 64]),
                                        ALU.mult).then_inc(out_out[n % 2], 1)

            def gate_group(n):
                g, b = GROUPS[n]
                m = group_turn(n)
                dve.wait_ge(turn_full, m + 1)
                if n == 0:
                    for name in ("zb0", "zb1"):
                        wait_proj_out(dve, name, 0)
                        wait_proj_out(dve, name, 1)
                z = z_b[:, 2 * g:2 * g + 2, queries(b)]
                nc.vector.tensor_tensor(z, turn_bank[m % 2][:, 0:256].rearrange("p (c t) -> p c t", c=2), z,
                                        ALU.mult).then_inc(turn_out[m % 2], 1)

            def forget(p, n):
                f = flat(cum[:, 2 * p:2 * p + 2, :])
                if n == 0:
                    if p == 0:
                        dve.wait_ge(pv_done, len(ITEMS))
                    else:
                        dve.wait_ge(qk_done, 12)
                    for name in (f"fa{p}", f"qa{p}"):
                        wait_proj_out(dve, name, 0)
                        wait_proj_out(dve, name, 1)
                    nc.vector.scalar_tensor_tensor(out=dec[:, 0, :], in0=f, scalar=-1.0, in1=f, op0=ALU.mult,
                                                   op1=ALU.min).then_inc(f_dve, 1)
                    nc.vector.tensor_scalar(dec[:, 1, :], f, F_FLOOR, None, ALU.max).then_inc(f_dve, 1)
                else:
                    if p:
                        dve.wait_ge(log_full, TREE0 + NTREE)
                    log_sig = k_c[:, 0, :]
                    dve.wait_ge(f_act, 5 * p + 2)
                    nc.vector.scalar_tensor_tensor(out=log_sig, in0=f, scalar=0.0, in1=dec[:, 0, :], op0=ALU.min,
                                                   op1=ALU.subtract).then_inc(f_dve, 1)
                    dve.wait_ge(f_dve, 4 * p + 3)
                    nc.vector.tensor_tensor(k_c[:, 1, :], log_sig, f, ALU.subtract).then_inc(f_dve, 1)
                    dve.wait_ge(f_dve, 4 * p + 4)
                    dve.wait_ge(f_act, 5 * p + 5)
                    link(nc.vector.tensor_tensor(log_sig, log_sig, dec[:, 1, :], ALU.add))
                    dve.wait_ge(reset_set, 2)
                    for a in range(2):
                        nc.vector.tensor_tensor_scan(cum[:, 2 * p + a, :], reset[:], log_sig[:, a * SEQ:a * SEQ + SEQ],
                                                     0.0, ALU.mult, ALU.add).then_inc(cum_done, 1)

            def near_products(p):
                dve.wait_ge(rl_done, 2 * p + 2)
                dve.wait_ge(k_done, 2 * (p + 1))
                nc.vector.tensor_tensor(q_r[:], q_r[:], q_a[:, 2 * p:2 * p + 2, :], ALU.mult).then_inc(near_done, 1)
                nc.vector.tensor_tensor(k_l[:], k_l[:], k_a[:], ALU.mult).then_inc(near_done, 1)

            def far_products(p):
                dve.wait_ge(near_done, 2 * p + 2)
                dve.wait_ge(far_f_done, p + 1)
                if p:
                    dve.wait_ge(log_full, TREE0 + NTREE)
                for kind, (src, quad0) in enumerate(((k_l, 0), (q_r, 2))):
                    for a in range(2):
                        s4 = src[:, a, :].rearrange("p (b s t) -> p b s t", b=2, t=SEG)[:, :, quad0:quad0 + 2, :]
                        f4 = far_f[:, kind, a, :].rearrange("p (b s) -> p b s", b=2)
                        nc.vector.tensor_tensor(far[:, kind, a, :].rearrange("p (b s t) -> p b s t", b=2, t=SEG), s4,
                                                f4.unsqueeze(3).broadcast_to([P, 2, 2, SEG]),
                                                ALU.mult).then_inc(far_done, 1)
                for kind, (src, half) in enumerate(((k_l, 0), (q_r, 256)), 2):
                    s4 = src[:, :, half:half + 256].rearrange("p a (s t) -> p a s t", t=SEG)
                    nc.vector.tensor_tensor(far[:, kind, :, :].rearrange("p a (s t) -> p a s t", t=SEG), s4,
                                            far_f[:, kind, :, :].unsqueeze(3).broadcast_to([P, 2, 4, SEG]),
                                            ALU.mult).then_inc(far_done, 1)

            def distance(p, lv):
                if lv > 1:
                    dve.wait_ge(qk_done, 2 * (6 * p + lv - 2))
                level_distance(nc.vector, p, lv).then_inc(dist_dve, 1)

            def level_products(p, lv):
                h = LEVELS[lv]
                ring = (lv - 1) % 2
                dve.wait_ge(fac_done, 2 * (6 * p + lv))
                if lv > 2:
                    wait_lvl_multiplied(dve, p, lv - 2)
                v = groups(dec[:, lv % 2, :], h)
                q = groups(flat(q_a[:, 2 * p:2 * p + 2, :]), h)
                k = groups(flat(k_a[:]), h)
                nc.vector.tensor_tensor(flat(q_c[:, ring]).rearrange("p (n t) -> p n t", t=h), v[:, :, h:2 * h],
                                        q[:, :, h:2 * h], ALU.mult).then_inc(qk_done, 1)
                nc.vector.tensor_tensor(groups(k_c[:, ring, :], h)[:, :, 0:h], v[:, :, 0:h], k[:, :, 0:h],
                                        ALU.mult).then_inc(qk_done, 1)

            def tree_place(p, n):
                kind, m = TREE[n]
                if kind not in ("diag", "lv"):
                    return
                idx = TREE0 + NTREE * p + n
                bank = log_bank[idx % 2]
                dve.wait_ge(log_full, idx + 1)
                if kind == "diag":
                    if p:
                        dve.wait_ge(recur_done, m + 1)
                    nc.vector.tensor_tensor(att_blocks(m), bank[:].rearrange("p (t n) -> p t n", t=TB),
                                            id_sb[:].unsqueeze(1).broadcast_to([P, TB, P]),
                                            ALU.mult).then_inc(log_out[idx % 2], 1)
                    return
                h = LEVELS[m]
                if m == 0:
                    for d in range(2):
                        wait_log_out(dve, TREE0 + NTREE * p + d)
                else:
                    link_level(p, m)
                if m < 2:
                    for row, col in ((0, 0),) if m == 0 else ((0, 0), (64, 32)):
                        keys = slice(row, row + h)
                        src = bank[keys, :].rearrange("p (a t n) -> p a t n", a=2, t=TB)[:, :, :, col:col + h]
                        base = att[keys, 0, 0, row + h:row + 2 * h]
                        ins = nc.vector.tensor_copy(strided(base, [[TB * SEQ, 2], [SEQ + P, TB], [1, h]]), src)
                    ins.then_inc(log_out[idx % 2], 1)
                    return
                for a in range(2):
                    src = strided(bank[:, a * 256:a * 256 + 256], [[64, TB], [h, 64 // h], [1, h]])
                    mask = strided(masks_sb[:, m - 2, :], [[0, TB], [h, 64 // h], [1, h]])
                    ins = nc.vector.copy_predicated(att_blocks(a, h), mask, src)
                ins.then_inc(log_out[idx % 2], 1)

            def link_level(p, lv):
                wait_log_out(dve, TREE0 + NTREE * p + TREE.index(("lv", lv - 1)))

            def gate_branch_a(h):
                dve.wait_ge(rms_done, h + 1)
                for name in ("za0", "za1"):
                    wait_proj_out(dve, name, 0)
                    wait_proj_out(dve, name, 1)
                root = square[:, h % 2, :]
                nc.vector.tensor_tensor(root, out_bank[h % 2][:], root, ALU.mult).then_inc(out_out[h % 2], 1)
                dve.wait_ge(out_out[h % 2], len(GROUPS) // 2 + h // 2 + 1)
                nc.vector.scalar_tensor_tensor(out=z_a[:, h, :], in0=root, scalar=g_a[:, h:h + 1], in1=z_a[:, h, :],
                                               op0=ALU.mult, op1=ALU.mult).then_inc(branch_a, 1)

            def split_branches(j):
                z = z_a if j < 2 else z_b
                dve.wait_ge(branch_a, HEADS_A)
                dve.wait_ge(o_hi_done, j + 1)
                nc.vector.tensor_tensor(flat(o_lo[:, 2 * j:2 * j + 2, :]), flat(z[:, 2 * j % 4:2 * j % 4 + 2, :]),
                                        flat(o_hi[:, 2 * j:2 * j + 2, :]).bitcast(F32),
                                        ALU.subtract).then_inc(o_lo_done, 1)

            def merge(m):
                u = UNITS.index(f"up{m // 2}")
                dve.wait_ge(part_done, 2 * u + m % 2 + 1)
                dve.wait_ge(gate_a_done, m // 2 + 1)
                wait_proj_out(dve, f"gb{m // 2}", m % 2)
                if m >= 2:
                    dve.wait_ge(m_hi_done, m - 1)
                    dve.wait_ge(m_lo_done, m - 1)
                fa, fb = 2 * m % 4, (2 * m + 1) % 4
                mx, gb = mix[:, m % 2, :], g_b[:, m % 4, :]
                nc.vector.tensor_tensor(mx, up_bank[fa][:], gate_a[:, m, :], ALU.mult).then_inc(up_out[fa], 1)
                nc.vector.tensor_tensor(gb, up_bank[fb][:], gb, ALU.mult).then_inc(up_out[fb], 1)
                dve.wait_ge(up_out[fa], m // 2 + 1)
                dve.wait_ge(up_out[fb], m // 2 + 1)
                nc.vector.tensor_tensor(mx, mx, gb, ALU.add).then_inc(mix_done, 1)
                dve.wait_ge(m_hi_done, m + 1)
                nc.vector.tensor_tensor(m_lo[:, m, :], mx, m_hi[:, m, :].bitcast(F32),
                                        ALU.subtract).then_inc(m_lo_done, 1)

            def residual(t, half):
                c = slice(half * 512, half * 512 + 512)
                dve.wait_ge(y_full, TB * half + t + 1)
                dve.wait_ge(res_in[t], 16)
                link(nc.vector.scalar_tensor_tensor(out=y_sb[:, t, c], in0=x_res[:, t, c], scalar=ALPHA,
                                                    in1=y_bank[half][t][:], op0=ALU.mult, op1=ALU.add))
                link(nc.vector.bn_stats(stats[:, t, half, :], y_sb[:, t, c]))

            def side(q):
                u, j = q // 4, q % 4
                if j == 0 and u >= 1:
                    leave_bank(u - 1, 1)
                if j == 2:
                    leave_bank(u, 0)
                for i in range(2 * (q - Q_DOTS), 2 * (q - Q_DOTS) + 2):
                    if 0 <= i < len(DOTS):
                        add_score(i)
                for n in groups_at(q):
                    divide_group(n)
                for i in items_at(q - 1):
                    move_probs(i)
                for n in groups_at(q):
                    gate_group(n)
                for i in items_at(q):
                    logits(i)
                for b, r in rounds.get(q, ()):
                    topk_round(b, r)
                for p in range(2):
                    at = q - Q_TREE[p]
                    if at == 0:
                        distance(p, 1)
                    if at == 2:
                        level_products(p, 1)
                        distance(p, 3)
                        level_products(p, 2)
                    if at == 3:
                        level_products(p, 3)
                        distance(p, 5)
                        level_products(p, 4)
                    if at == 4:
                        level_products(p, 5)
                        level_products(p, 6)
                for p, n in tree_at(q):
                    tree_place(p, n)
                for p in range(2):
                    at = q - Q_PREP[p]
                    if at == 0:
                        forget(p, 0)
                    if at == 1:
                        forget(p, 1)
                    if at == 3:
                        near_products(p)
                    if at == 4:
                        far_products(p)
                for h in range(HEADS_A):
                    if q == Q_TREE[h // 2] + 8:
                        gate_branch_a(h)
                if Q_MERGE <= q < Q_MERGE + 4:
                    split_branches(j)
                m = merged_at(q)
                if m is not None:
                    merge(m)

            for k in range(KT):
                split_x(k)
            dve.wait_ge(early_in, 32)
            nc.vector.tensor_scalar(bias_q[:], bias[:], QSCALE, None, ALU.mult).then_inc(bias_q_done, 1)
            for q in range(4 * NMAIN):
                side(q)
                if q == Q_ITEM[0] - 3:
                    lower_bound()
                if q == 7:
                    dve.wait_ge(table_full, 1)
                    for c in range(2):
                        nc.vector.tensor_copy(table[:, c * T5W // 2:(c + 1) * T5W // 2],
                                              turn_bank[c][0:HEADS_B, 0:T5W // 2]).then_inc(table_done, 1)
            merge(KT - 1)
            for t in range(TB):
                residual(t, 0)
            for t in range(TB):
                residual(t, 1)
                if t == 0:
                    dve.wait_ge(ln_in, 32)
                nc.vector.bn_aggr(aggr[:, t, :], stats[:, t, :, :].rearrange("p a b -> p (a b)")).then_inc(y_aggr, 1)
                dve.wait_ge(ln_rstd, t + 1)
                for c in (slice(0, 512), slice(512, 1024)):
                    y = y_sb[:, t, c]
                    link(nc.vector.scalar_tensor_tensor(out=y, in0=y, scalar=aggr[:, t, 0:1], in1=ln_gb[:, 0, c],
                                                        op0=ALU.subtract, op1=ALU.mult))
                    nc.vector.scalar_tensor_tensor(out=y, in0=y, scalar=rstd[:, t, 1:2], in1=ln_gb[:, 1, c],
                                                   op0=ALU.mult, op1=ALU.add).then_inc(y_done, 1)

        @block.gpsimd
        def _(pool):
            nc.gpsimd.memset(ones_sb[:], 1.0 / P)
            nc.gpsimd.memset(eps[:, 0:1], RMS_EPS)
            nc.gpsimd.memset(eps[:, 1:2], LN_EPS).then_inc(pool_set, 1)

            def split_lo(u, j):
                pool.wait_ge(hi_done, 2 * u + j // 2 + 1)
                k = slice(2 * j, 2 * j + 2)
                nc.gpsimd.tensor_tensor(split_target(u, x_lo, w_lo)[:, k, :], raw(u)[:, k, :],
                                        split_target(u, x_hi, w_hi)[:, k, :].bitcast(F32),
                                        ALU.subtract).then_inc(lo_done, 1)

            def bias_and_penalty(i):
                b, h = ITEMS[i]
                if i == 0:
                    pool.wait_ge(t5_in, 16)
                    pool.wait_ge(consts_in, 16 * N_CONSTS)
                if h == 0 and b:
                    pool.wait_ge(pen_done, b)
                if i >= 2:
                    pool.wait_ge(exp_done, i - 1)
                n = (b + 1) * P
                nc.gpsimd.tensor_tensor(logit[:, i % 2, 0:n], t5[:, h, SEQ - n:SEQ], pen[b][:] if b else causal_sb[:],
                                        ALU.add).then_inc(logit_pre, 1)

            def make_reset():
                pool.wait_ge(pv_done, len(ITEMS))
                nc.gpsimd.memset(far_f[:], 1.0)
                nc.gpsimd.memset(reset[:], 1.0).then_inc(reset_set, 1)
                pool.wait_ge(reset_set, 1)
                nc.gpsimd.memset(reset[:, 0:SEQ:SEG], 0.0).then_inc(reset_set, 1)

            def end_distance(p):
                pool.wait_ge(cum_done, 2 * (p + 1))
                c = flat(cum[:, 2 * p:2 * p + 2, :]).rearrange("p (s t) -> p s t", t=SEG)
                nc.gpsimd.tensor_tensor(dec[:, 0, :].rearrange("p (s t) -> p s t", t=SEG),
                                        c[:, :, SEG - 1:SEG].broadcast_to([P, 2 * NSEG, SEG]), c,
                                        ALU.subtract).then_inc(dist_pool, 1)

            def far_factors(p):
                pool.wait_ge(seg_decay, p + 1)
                if p:
                    pool.wait_ge(far_done, 6)
                n = 7 * p
                g = far_g
                for dst, src in ((far_f[:, 0, :, 0:4:2], g[:, :, 1:8:4]), (far_f[:, 1, :, 1:4:2], g[:, :, 2:8:4]),
                                 (far_f[:, 2, :, 2:3], g[:, :, 3:4]), (far_f[:, 3, :, 1:2], g[:, :, 4:5])):
                    n += 1
                    nc.gpsimd.tensor_copy(dst, src).then_inc(far_f_step, 1)
                for dst, x, y in ((far_f[:, 2, :, 1:2], far_f[:, 2, :, 2:3], g[:, :, 2:3]),
                                  (far_f[:, 3, :, 2:3], far_f[:, 3, :, 1:2], g[:, :, 5:6]),
                                  (far_f[:, 2, :, 0:1], far_f[:, 2, :, 1:2], g[:, :, 1:2])):
                    pool.wait_ge(far_f_step, n)
                    n += 1
                    nc.gpsimd.tensor_tensor(dst, x, y, ALU.mult).then_inc(far_f_step, 1)
                pool.wait_ge(far_f_step, n)
                nc.gpsimd.tensor_tensor(far_f[:, 3, :, 3:4], far_f[:, 3, :, 2:3], g[:, :, 6:7],
                                        ALU.mult).then_inc(far_f_done, 1)

            def distance(p, lv):
                if lv == 2:
                    pool.wait_ge(rl_done, 2 * p + 2)
                else:
                    pool.wait_ge(qk_done, 2 * (6 * p + lv - 2))
                level_distance(nc.gpsimd, p, lv).then_inc(dist_pool, 1)

            def side(q):
                j = q % 4
                u = q // 4 + 1
                if u >= 2:
                    for piece in ((0,), (1, 2), (3,), ())[j]:
                        split_lo(u, piece)
                if q == Q_ITEM[0] - 1:
                    bias_and_penalty(0)
                    bias_and_penalty(1)
                for i in items_at(q):
                    if i + 2 < len(ITEMS):
                        bias_and_penalty(i + 2)
                if q == Q_PREP[0] - 1:
                    make_reset()
                for p in range(2):
                    if q == Q_PREP[p] + 2:
                        end_distance(p)
                        far_factors(p)
                    at = q - Q_TREE[p]
                    if at == 1:
                        distance(p, 2)
                    if at == 2:
                        distance(p, 4)
                    if at == 3:
                        distance(p, 6)

            for u in (0, 1):
                for j in range(4):
                    split_lo(u, j)
            for q in range(4 * NMAIN):
                side(q)
            for u in range(NMAIN + 1, NU):
                for j in range(4):
                    split_lo(u, j)


def t5_one_hot():
    d = np.arange(SEQ - 1, -1, -1)
    exact = BUCKETS // 2
    large = exact + (np.log(np.maximum(d, 1).astype(np.float32) / np.float32(exact))
                     / np.float32(np.log(MAX_DISTANCE / exact)) * (BUCKETS - exact)).astype(np.int32)
    bucket = np.where(d < exact, d, np.minimum(large, BUCKETS - 1))
    hot = np.zeros((BUCKETS, T5W), np.float32)
    hot[bucket, np.arange(SEQ)] = 1.0
    return hot


def tree_level_masks():
    key, n = np.arange(P)[:, None], np.arange(64)[None, :]
    return np.stack([(key // (2 * h) == n // h) & (key % (2 * h) < h) for h in LEVELS[2:]], 1).astype(np.int32)


def kernel(**inputs):
    import concourse.bacc as bacc
    from concourse.bass_utils import run_bass_kernel_spmd

    a = {k: np.asarray(v) for k, v in inputs.items()}
    x, w_in, b_in = a["x"][0], a["w_in"][0], a["b_in"][0]

    def unit(rows_by_tile):
        return rows_by_tile.reshape(KT, P, -1).transpose(1, 0, 2).reshape(P, -1)

    units, b_cols = [], np.zeros((P, 2 * NMAIN), np.float32)
    for u, name in enumerate(UNITS):
        kind = name[:2]
        if name == "kiwi":
            ki = COLUMNS["ki"]
            w_kiwi = unit(w_in[:, ki:ki + WKI])
            b_cols[0:WKI, 2 * u] = b_in[ki:ki + WKI]
        elif kind == "up":
            c = slice(int(name[2]) * UW, int(name[2]) * UW + UW)
            units.append(unit(np.concatenate([a["w_up_a"][0][:, c], a["w_up_b"][0][:, c]], 0)))
        else:
            c = COLUMNS[kind] + int(name[2]) * UW
            units.append(unit(w_in[:, c:c + UW]))
            b_cols[:, 2 * u], b_cols[:, 2 * u + 1] = b_in[c:c + P], b_in[c + P:c + UW]
    for n in (0, 1, 3, 2):
        units.append(unit(a["w_out"][0][:, n * UW:n * UW + UW]))
    arrays = {
        "x_t": x.reshape(SEQ, KT, P).transpose(2, 1, 0), "x_tok": x.reshape(TB, P, D_MODEL),
        "w_units": np.stack(units), "w_kiwi": w_kiwi, "b_cols": b_cols,
        "b_ia": b_in[COLUMNS["ia"]:COLUMNS["ia"] + D_A], "b_vb": b_in[COLUMNS["vb"]:COLUMNS["vb"] + D_B],
        "lb_cols": a["lb_logits"][0].reshape(HEADS_A, P).T, "g_cols": a["norm_a_g"][0].reshape(HEADS_A, P).T,
        "rel_bias": a["rel_bias"], "ln_g": a["ln_g"][0], "ln_b": a["ln_b"][0],
        "one_hot": t5_one_hot(), "ident": np.eye(P, dtype=np.float32),
        "causal": np.where(np.arange(P)[None, :] > np.arange(P)[:, None], np.float32(NEG), np.float32(0)),
        "tree_masks": tree_level_masks(),
    }
    arrays = {k: np.ascontiguousarray(v) for k, v in arrays.items()}
    nc = bacc.Bacc("TRN2", target_bir_lowering=False, num_devices=1)
    args = [nc.dram_tensor(f"in_{k}", v.shape, mybir.dt.from_np(v.dtype), kind="ExternalInput").ap()
            for k, v in arrays.items()]
    out = nc.dram_tensor("out_0", (TB, P, D_MODEL), F32, kind="ExternalOutput").ap()
    hybrid_kernel(nc, *args, out)
    r = run_bass_kernel_spmd(nc, [{f"in_{k}": v for k, v in arrays.items()}], core_ids=[0])
    return r.results[0]["out_0"].reshape(1, SEQ, D_MODEL)
```
